# Optimizing a Trainium2 kernel written in Bass

```python
import jax, jax.numpy as jnp
from jax import lax
import numpy as np

D_MODEL = 1024
BATCH = 1
SEQ = 256
DEPTH = 2

HEAD_DIM = 128
MOBA_HEADS = 4
RET_HEADS = 4
MOBA_BLOCK = 256
MOBA_TOPK = 3
MOBA_QCHUNK = 32
RET_CHUNK = 128
CONV_WIDTH = 3
PEER_HEADS = 8
PEER_NKEYS = 128
PEER_NEXPERTS = PEER_NKEYS * PEER_NKEYS
PEER_TOPK = 16
PEER_DKEY = 256
PEER_TOKCHUNK = 128
ROPE_THETA = 10000.0
EPS = 1e-6
N_EVEN = (DEPTH + 1) // 2
N_ODD = DEPTH // 2
MOBA_W = MOBA_HEADS * HEAD_DIM
RET_W = RET_HEADS * HEAD_DIM
EVEN_SPLITS = (MOBA_W, MOBA_W, MOBA_W, RET_W, RET_W, RET_W, RET_W)
EVEN_IN = sum(EVEN_SPLITS)
EVEN_OUT_IN = MOBA_W + RET_W


def rmsnorm(x, g):
    xf = x.astype(jnp.float32)
    y = xf * lax.rsqrt(jnp.mean(xf * xf, axis=-1, keepdims=True) + EPS)
    return (y * g.astype(jnp.float32)).astype(x.dtype)

def rope(t):
    s, dh = t.shape[2], t.shape[3]
    half = dh // 2
    inv = ROPE_THETA ** (-jnp.arange(half, dtype=jnp.float32) / half)
    ang = jnp.arange(s, dtype=jnp.float32)[:, None] * inv[None, :]
    cos = jnp.cos(ang).astype(t.dtype)
    sin = jnp.sin(ang).astype(t.dtype)
    t1, t2 = t[..., :half], t[..., half:]
    return jnp.concatenate([t1 * cos - t2 * sin, t2 * cos + t1 * sin], axis=-1)

def split_heads(t, n):
    b, s, _ = t.shape
    return t.reshape(b, s, n, HEAD_DIM).transpose(0, 2, 1, 3)

def merge_heads(t):
    b, h, s, dh = t.shape
    return t.transpose(0, 2, 1, 3).reshape(b, s, h * dh)

def moba_attention(q, k, v):
    b, h, s, dh = q.shape
    nb = -(-s // MOBA_BLOCK)
    pad = nb * MOBA_BLOCK - s
    kb = jnp.pad(k, ((0, 0), (0, 0), (0, pad), (0, 0))).reshape(b, h, nb, MOBA_BLOCK, dh)
    vb = jnp.pad(v, ((0, 0), (0, 0), (0, pad), (0, 0))).reshape(b, h, nb, MOBA_BLOCK, dh)
    counts = jnp.minimum(MOBA_BLOCK, s - jnp.arange(nb) * MOBA_BLOCK).astype(jnp.float32)
    kmean = kb.astype(jnp.float32).sum(axis=3) / counts[None, None, :, None]
    gate = jnp.einsum('bhsd,bhnd->bhsn', q.astype(jnp.float32), kmean)
    qblk = jnp.arange(s) // MOBA_BLOCK
    past = jnp.arange(nb)[None, :] < qblk[:, None]
    gate = jnp.where(past, gate, -jnp.inf)
    kk = min(MOBA_TOPK, nb)
    _, sel = lax.top_k(gate, kk)
    valid = sel < qblk[:, None]
    nq = s // MOBA_QCHUNK
    def chunked(t):
        return t.reshape(b, h, nq, MOBA_QCHUNK, *t.shape[3:]).transpose(2, 0, 1, 3, *range(4, t.ndim + 1))
    qs, sels, valids = chunked(q), chunked(sel), chunked(valid)
    scale = dh ** -0.5
    bi = jnp.arange(b)[:, None, None, None]
    hi = jnp.arange(h)[None, :, None, None]

    def step(args):
        ci, qc, selc, validc = args
        tpos = ci * MOBA_QCHUNK + jnp.arange(MOBA_QCHUNK)
        ob = (ci * MOBA_QCHUNK) // MOBA_BLOCK
        k_own = lax.dynamic_index_in_dim(kb, ob, axis=2, keepdims=False)
        v_own = lax.dynamic_index_in_dim(vb, ob, axis=2, keepdims=False)
        kpos = ob * MOBA_BLOCK + jnp.arange(MOBA_BLOCK)
        s_own = jnp.einsum('bhqd,bhkd->bhqk', qc, k_own).astype(jnp.float32) * scale
        s_own = jnp.where(kpos[None, :] <= tpos[:, None], s_own, -jnp.inf)
        kg = kb[bi, hi, selc]
        vg = vb[bi, hi, selc]
        s_sel = jnp.einsum('bhqd,bhqjkd->bhqjk', qc, kg).astype(jnp.float32) * scale
        s_sel = jnp.where(validc[..., None], s_sel, -jnp.inf)
        scores = jnp.concatenate([s_sel.reshape(b, h, MOBA_QCHUNK, kk * MOBA_BLOCK), s_own], axis=-1)
        p = jax.nn.softmax(scores, axis=-1).astype(v.dtype)
        p_sel = p[..., :kk * MOBA_BLOCK].reshape(b, h, MOBA_QCHUNK, kk, MOBA_BLOCK)
        p_own = p[..., kk * MOBA_BLOCK:]
        return (jnp.einsum('bhqjk,bhqjkd->bhqd', p_sel, vg)
                + jnp.einsum('bhqk,bhkd->bhqd', p_own, v_own))

    out = lax.map(step, (jnp.arange(nq), qs, sels, valids))
    return out.transpose(1, 2, 0, 3, 4).reshape(b, h, s, dh)

def retention(q, k, v):
    b, h, s, dh = q.shape
    c = RET_CHUNK
    nc = s // c
    log_g = jnp.log(1.0 - 2.0 ** (-5.0 - jnp.arange(h, dtype=jnp.float32)))
    idx = jnp.arange(c, dtype=jnp.float32)
    diff = idx[:, None] - idx[None, :]
    dmask = jnp.where(diff >= 0, jnp.exp(log_g[:, None, None] * jnp.maximum(diff, 0.0)), 0.0)
    xi = jnp.exp(log_g[:, None] * (idx + 1.0))[..., None]
    zeta = jnp.exp(log_g[:, None] * (c - 1.0 - idx))[..., None]
    gc = jnp.exp(log_g * c)[:, None, None]
    def chunked(t):
        return t.astype(jnp.float32).reshape(b, h, nc, c, dh).transpose(2, 0, 1, 3, 4)
    qs, ks, vs = chunked(q), chunked(k * (dh ** -0.5)), chunked(v)

    def step(state, inp):
        qc, kc, vc = inp
        inner = jnp.einsum('bhnd,bhmd->bhnm', qc, kc) * dmask
        o = jnp.einsum('bhnm,bhmd->bhnd', inner, vc) + jnp.einsum('bhnd,bhde->bhne', qc, state) * xi
        state = state * gc + jnp.einsum('bhmd,bhme->bhde', kc * zeta, vc)
        return state, o

    state0 = jnp.zeros((b, h, dh, dh), jnp.float32)
    _, outs = lax.scan(step, state0, (qs, ks, vs))
    return outs.transpose(1, 2, 0, 3, 4).reshape(b, h, s, dh)

def attn_retention_mixer(xn, w_in, w_out):
    proj = xn @ w_in
    cuts = list(np.cumsum(EVEN_SPLITS)[:-1])
    mq, mk, mv, rq, rk, rv, rg = jnp.split(proj, cuts, axis=-1)
    mq, mk, mv = split_heads(mq, MOBA_HEADS), split_heads(mk, MOBA_HEADS), split_heads(mv, MOBA_HEADS)
    rq, rk, rv = split_heads(rq, RET_HEADS), split_heads(rk, RET_HEADS), split_heads(rv, RET_HEADS)
    mo = merge_heads(moba_attention(rope(mq), rope(mk), mv))
    ro = retention(rope(rq), rope(rk), rv)
    ro = ro * lax.rsqrt(jnp.mean(ro * ro, axis=-1, keepdims=True) + EPS)
    ro = merge_heads(ro).astype(xn.dtype) * jax.nn.silu(rg)
    return jnp.concatenate([mo, ro], axis=-1) @ w_out

def short_conv_mixer(xn, w_in, conv_w, w_out):
    d = xn.shape[-1]
    bg, cg, hx = jnp.split(xn @ w_in, 3, axis=-1)
    u = cg * hx
    y = lax.conv_general_dilated(u, conv_w[:, None, :], window_strides=(1,),
                                 padding=[(CONV_WIDTH - 1, 0)],
                                 dimension_numbers=('NWC', 'WIO', 'NWC'),
                                 feature_group_count=d)
    return (bg * y) @ w_out

def peer(xn, w_q, sub_keys, u, v):
    b, s, d = xn.shape
    t = xn.reshape(b * s, d)
    n_tok = b * s
    q = (t @ w_q).reshape(n_tok, PEER_HEADS, 2, PEER_DKEY // 2)
    sc = jnp.einsum('thpd,hpnd->thpn', q, sub_keys).astype(jnp.float32)
    s1, i1 = lax.top_k(sc[:, :, 0], PEER_TOPK)
    s2, i2 = lax.top_k(sc[:, :, 1], PEER_TOPK)
    cand = (s1[..., :, None] + s2[..., None, :]).reshape(n_tok, PEER_HEADS, PEER_TOPK * PEER_TOPK)
    cidx = (i1[..., :, None] * PEER_NKEYS + i2[..., None, :]).reshape(n_tok, PEER_HEADS, PEER_TOPK * PEER_TOPK)
    top_s, pos = lax.top_k(cand, PEER_TOPK)
    eidx = jnp.take_along_axis(cidx, pos, axis=-1)
    gate = jax.nn.softmax(top_s, axis=-1).astype(xn.dtype)
    nt = n_tok // PEER_TOKCHUNK

    def step(args):
        tc, ec, gc = args
        hid = jax.nn.gelu(jnp.einsum('td,thkd->thk', tc, u[ec]), approximate=False)
        return jnp.einsum('thk,thkd->td', gc * hid, v[ec])

    out = lax.map(step, (t.reshape(nt, PEER_TOKCHUNK, d),
                         eidx.reshape(nt, PEER_TOKCHUNK, PEER_HEADS, PEER_TOPK),
                         gate.reshape(nt, PEER_TOKCHUNK, PEER_HEADS, PEER_TOPK)))
    return out.reshape(b, s, d)

def first_inputs(seed: int = 0) -> dict:
    key = jax.random.key(seed)
    ks = jax.random.split(key, 16)
    f32 = jnp.float32
    nrm = lambda k, shape, sc: jax.random.normal(k, shape, f32) * sc
    return {
        "x": nrm(ks[0], (BATCH, SEQ, D_MODEL), 1.0),
        "norm_mix": 1.0 + nrm(ks[1], (DEPTH, D_MODEL), 0.02),
        "norm_ffn": 1.0 + nrm(ks[2], (DEPTH, D_MODEL), 0.02),
        "even_w_in": nrm(ks[3], (N_EVEN, D_MODEL, EVEN_IN), D_MODEL ** -0.5),
        "even_w_out": nrm(ks[4], (N_EVEN, EVEN_OUT_IN, D_MODEL), EVEN_OUT_IN ** -0.5),
        "odd_w_in": nrm(ks[5], (N_ODD, D_MODEL, 3 * D_MODEL), D_MODEL ** -0.5),
        "odd_conv": nrm(ks[6], (N_ODD, CONV_WIDTH, D_MODEL), CONV_WIDTH ** -0.5),
        "odd_w_out": nrm(ks[7], (N_ODD, D_MODEL, D_MODEL), D_MODEL ** -0.5),
        "peer_w_q": nrm(ks[8], (DEPTH, D_MODEL, PEER_HEADS * PEER_DKEY), D_MODEL ** -0.5),
        "peer_sub_keys": nrm(ks[9], (DEPTH, PEER_HEADS, 2, PEER_NKEYS, PEER_DKEY // 2), (PEER_DKEY // 2) ** -0.5),
        "peer_u": nrm(ks[10], (DEPTH, PEER_NEXPERTS, D_MODEL), D_MODEL ** -0.5),
        "peer_v": nrm(ks[11], (DEPTH, PEER_NEXPERTS, D_MODEL), 0.1),
        "final_norm": 1.0 + nrm(ks[12], (D_MODEL,), 0.02),
    }

def first_block(x, norm_mix, norm_ffn, even_w_in, even_w_out, odd_w_in, odd_conv, odd_w_out,
              peer_w_q, peer_sub_keys, peer_u, peer_v, final_norm):
    h = x
    for layer in range(DEPTH):
        xn = rmsnorm(h, norm_mix[layer])
        i = layer // 2
        if layer % 2 == 0:
            h = h + attn_retention_mixer(xn, even_w_in[i], even_w_out[i])
        else:
            h = h + short_conv_mixer(xn, odd_w_in[i], odd_conv[i], odd_w_out[i])
        h = h + peer(rmsnorm(h, norm_ffn[layer]), peer_w_q[layer], peer_sub_keys[layer],
                     peer_u[layer], peer_v[layer])
    return rmsnorm(h, final_norm)


DEPTH_2 = 1

CHUNK = 64
N_PREV_CHUNKS = 8
BAND = (N_PREV_CHUNKS + 1) * CHUNK
HEAD_DIM_2 = 64
N_HEADS_ATTN = 8
N_HEADS_RWKV = 8
D_ATTN = N_HEADS_ATTN * HEAD_DIM_2
D_RWKV = N_HEADS_RWKV * HEAD_DIM_2
REL_CLIP = 128
DECAY_LORA = 64
AAA_LORA = 64
MV_LORA = 32
GATE_LORA = 160
N_GROUPS = 4
EXPERTS_PER_GROUP = 8
N_EXPERTS = N_GROUPS * EXPERTS_PER_GROUP
TOP_K_IN_GROUP = 2
D_EXPERT = 256
D_PLE = 256
DEEPNORM_ALPHA = (2 * DEPTH_2) ** 0.25
DEEPNORM_BETA = (8 * DEPTH_2) ** -0.25
LN_EPS = 1e-5
GN_EPS = 64e-5
NEG_INF = -1e30

Q0 = 0
K0 = D_ATTN
V0 = 2 * D_ATTN
RW0 = 3 * D_ATTN
RW_COLS = 3 * D_RWKV + DECAY_LORA + AAA_LORA + GATE_LORA
GATE0 = RW0 + RW_COLS
N_IN = GATE0 + 2 * D_MODEL


def layer_norm(x, g, b):
    x32 = x.astype(jnp.float32)
    mu = jnp.mean(x32, axis=-1, keepdims=True)
    var = jnp.mean(jnp.square(x32 - mu), axis=-1, keepdims=True)
    y = (x32 - mu) * lax.rsqrt(var + LN_EPS)
    return (y * g.astype(jnp.float32) + b.astype(jnp.float32)).astype(x.dtype)

def chunked_band_attention(q, k, v, rel_bias):
    B, S, _ = q.shape
    nc = S // CHUNK
    q = q.reshape(B, nc, CHUNK, N_HEADS_ATTN, HEAD_DIM_2)
    pad = ((0, 0), (N_PREV_CHUNKS * CHUNK, 0), (0, 0))
    kp = jnp.pad(k, pad).reshape(B, nc + N_PREV_CHUNKS, CHUNK, N_HEADS_ATTN, HEAD_DIM_2)
    vp = jnp.pad(v, pad).reshape(B, nc + N_PREV_CHUNKS, CHUNK, N_HEADS_ATTN, HEAD_DIM_2)
    kb = jnp.concatenate([kp[:, j:j + nc] for j in range(N_PREV_CHUNKS + 1)], axis=2)
    vb = jnp.concatenate([vp[:, j:j + nc] for j in range(N_PREV_CHUNKS + 1)], axis=2)
    scores = jnp.einsum("bcqhd,bckhd->bhcqk", q, kb).astype(jnp.float32) * (HEAD_DIM_2 ** -0.5)
    qi = jnp.arange(CHUNK)[:, None]
    kj = jnp.arange(BAND)[None, :]
    dist = qi - (kj - N_PREV_CHUNKS * CHUNK)
    idx = jnp.clip(dist, -REL_CLIP, REL_CLIP) + REL_CLIP
    bias = rel_bias[:, idx].astype(jnp.float32)
    key_chunk = jnp.arange(nc)[:, None] - N_PREV_CHUNKS + (jnp.arange(BAND) // CHUNK)[None, :]
    valid = key_chunk >= 0
    scores = jnp.where(valid[None, None, :, None, :], scores + bias[None, :, None], NEG_INF)
    prob = jax.nn.softmax(scores, axis=-1).astype(v.dtype)
    out = jnp.einsum("bhcqk,bckhd->bcqhd", prob, vb)
    return out.reshape(B, S, D_ATTN)

def rwkv7_scan(r, w, k, v, a, b):
    B, S, H, N = r.shape
    xs = tuple(jnp.swapaxes(t.astype(jnp.float32), 0, 1) for t in (r, w, k, v, a, b))

    def step(state, inp):
        rt, wt, kt, vt, at, bt = inp
        sa = jnp.einsum("bhij,bhj->bhi", state, at)
        state = state * wt[:, :, None, :] + sa[..., None] * bt[:, :, None, :] + vt[..., None] * kt[:, :, None, :]
        return state, jnp.einsum("bhij,bhj->bhi", state, rt)

    state0 = jnp.zeros((B, H, N, N), jnp.float32)
    _, ys = lax.scan(step, state0, xs)
    return jnp.swapaxes(ys, 0, 1)

def rwkv7_time_mix(cols, mu, v_first, decay_base, decay_up, aaa_base, aaa_up, gate_up,
                   k_k, k_a, r_k, gn_g, gn_b, vres):
    B, S, _ = cols.shape
    prev = jnp.pad(cols, ((0, 0), (1, 0), (0, 0)))[:, :-1]
    cols = cols + (prev - cols) * mu
    splits = [D_RWKV, 2 * D_RWKV, 3 * D_RWKV, 3 * D_RWKV + DECAY_LORA, 3 * D_RWKV + DECAY_LORA + AAA_LORA]
    r, k, v, wd, ad, gd = jnp.split(cols, splits, axis=-1)
    w_log = -jax.nn.softplus(-(decay_base + jnp.tanh(wd) @ decay_up)) - 0.5
    decay = jnp.exp(-jnp.exp(w_log.astype(jnp.float32)))
    a = jax.nn.sigmoid(aaa_base + ad @ aaa_up)
    g = jax.nn.sigmoid(gd) @ gate_up
    heads = lambda t: t.reshape(B, S, N_HEADS_RWKV, HEAD_DIM_2)
    kk = heads(k * k_k).astype(jnp.float32)
    kk = kk * lax.rsqrt(jnp.maximum(jnp.sum(kk * kk, axis=-1, keepdims=True), 1e-24))
    k = k * (1.0 + (a - 1.0) * k_a)
    if vres is None:
        v_first = v
    else:
        vres_base, vres_down, vres_up = vres
        v = v + (v_first - v) * jax.nn.sigmoid(vres_base + (v @ vres_down) @ vres_up)
    r_h, k_h, v_h, a_h = heads(r), heads(k), heads(v), heads(a)
    y = rwkv7_scan(r_h, heads(decay), k_h, v_h, -kk, kk * a_h.astype(jnp.float32))
    m = jnp.mean(y, axis=-1, keepdims=True)
    var = jnp.mean(jnp.square(y - m), axis=-1, keepdims=True)
    yn = ((y - m) * lax.rsqrt(var + GN_EPS)).reshape(B, S, D_RWKV)
    yn = yn * gn_g.astype(jnp.float32) + gn_b.astype(jnp.float32)
    bonus = (jnp.sum(r_h * k_h * r_k, axis=-1, keepdims=True) * v_h).reshape(B, S, D_RWKV)
    out = (yn.astype(cols.dtype) + bonus) * g
    return out, v_first

def hier_moe(x, w_grp, b_grp, w_exp, b_exp, e_gate, e_up, e_down):
    B, S, D = x.shape
    T = B * S
    xt = x.reshape(T, D)
    glog = (xt @ w_grp + b_grp).astype(jnp.float32)
    gprob = jax.nn.softmax(glog, axis=-1)
    grp = jnp.argmax(glog, axis=-1)
    g_gate = jnp.take_along_axis(gprob, grp[:, None], axis=1)
    elog = (xt @ w_exp + b_exp).astype(jnp.float32).reshape(T, N_GROUPS, EXPERTS_PER_GROUP)
    sel = jnp.take_along_axis(elog, grp[:, None, None], axis=1)[:, 0]
    top_v, top_i = lax.top_k(sel, TOP_K_IN_GROUP)
    wk = jax.nn.softmax(top_v, axis=-1) * g_gate
    eid = grp[:, None] * EXPERTS_PER_GROUP + top_i
    comb = jnp.sum(jax.nn.one_hot(eid, N_EXPERTS, dtype=jnp.float32) * wk[..., None], axis=1).astype(x.dtype)
    out = jnp.zeros_like(xt)
    for e in range(N_EXPERTS):
        h = jax.nn.silu(xt @ e_gate[e]) * (xt @ e_up[e])
        out = out + (h * comb[:, e:e + 1]) @ e_down[e]
    return out.reshape(B, S, D)

def second_inputs(seed: int = 0) -> dict:
    key = jax.random.key(seed)
    keys = iter(jax.random.split(key, 48))
    nrm = lambda shape, s: jax.random.normal(next(keys), shape, jnp.float32) * s
    uni = lambda shape, lo, hi: jax.random.uniform(next(keys), shape, jnp.float32, lo, hi)
    col_scale = jnp.ones((N_IN,), jnp.float32)
    col_scale = col_scale.at[V0:RW0].set(DEEPNORM_BETA)
    col_scale = col_scale.at[RW0 + 2 * D_RWKV:RW0 + 3 * D_RWKV].set(DEEPNORM_BETA)
    return {
        "x": nrm((BATCH, SEQ, D_MODEL), 1.0),
        "p": nrm((DEPTH_2, BATCH, SEQ, D_PLE), 1.0),
        "ln_in_g": 1.0 + nrm((D_MODEL,), 0.02),
        "ln_in_b": nrm((D_MODEL,), 0.02),
        "rel_bias": nrm((N_HEADS_ATTN, 2 * REL_CLIP + 1), 0.1),
        "w_in": nrm((DEPTH_2, D_MODEL, N_IN), D_MODEL ** -0.5) * col_scale,
        "tok_mix": uni((DEPTH_2, RW_COLS), 0.0, 1.0),
        "decay_base": uni((DEPTH_2, D_RWKV), -6.0, -1.0),
        "decay_up": nrm((DEPTH_2, DECAY_LORA, D_RWKV), DECAY_LORA ** -0.5),
        "aaa_base": nrm((DEPTH_2, D_RWKV), 0.1),
        "aaa_up": nrm((DEPTH_2, AAA_LORA, D_RWKV), AAA_LORA ** -0.5),
        "gate_up": nrm((DEPTH_2, GATE_LORA, D_RWKV), GATE_LORA ** -0.5),
        "k_k": 0.85 + nrm((DEPTH_2, D_RWKV), 0.02),
        "k_a": 1.0 + nrm((DEPTH_2, D_RWKV), 0.02),
        "r_k": nrm((DEPTH_2, N_HEADS_RWKV, HEAD_DIM_2), 0.1),
        "vres_base": nrm((DEPTH_2 - 1, D_RWKV), 0.1),
        "vres_down": nrm((DEPTH_2 - 1, D_RWKV, MV_LORA), D_RWKV ** -0.5),
        "vres_up": nrm((DEPTH_2 - 1, MV_LORA, D_RWKV), MV_LORA ** -0.5),
        "gn_g": 1.0 + nrm((DEPTH_2, D_RWKV), 0.02),
        "gn_b": nrm((DEPTH_2, D_RWKV), 0.02),
        "w_branch_attn": nrm((DEPTH_2, D_ATTN, D_MODEL), D_ATTN ** -0.5 * DEEPNORM_BETA),
        "w_branch_rwkv": nrm((DEPTH_2, D_RWKV, D_MODEL), D_RWKV ** -0.5 * DEEPNORM_BETA),
        "w_out": nrm((DEPTH_2, D_MODEL, D_MODEL), D_MODEL ** -0.5 * DEEPNORM_BETA),
        "router_grp": nrm((DEPTH_2, D_MODEL, N_GROUPS), D_MODEL ** -0.5),
        "router_grp_bias": nrm((DEPTH_2, N_GROUPS), 0.01),
        "router_exp": nrm((DEPTH_2, D_MODEL, N_EXPERTS), D_MODEL ** -0.5),
        "router_exp_bias": nrm((DEPTH_2, N_EXPERTS), 0.01),
        "exp_gate": nrm((DEPTH_2, N_EXPERTS, D_MODEL, D_EXPERT), D_MODEL ** -0.5),
        "exp_up": nrm((DEPTH_2, N_EXPERTS, D_MODEL, D_EXPERT), D_MODEL ** -0.5),
        "exp_down": nrm((DEPTH_2, N_EXPERTS, D_EXPERT, D_MODEL), D_EXPERT ** -0.5 * DEEPNORM_BETA),
        "ple_proj": nrm((DEPTH_2, D_PLE, D_MODEL), D_PLE ** -0.5 * DEEPNORM_BETA),
        "ple_gate": nrm((DEPTH_2, D_MODEL, D_MODEL), D_MODEL ** -0.5),
        "ln_g": 1.0 + nrm((DEPTH_2, 3, D_MODEL), 0.02),
        "ln_b": nrm((DEPTH_2, 3, D_MODEL), 0.02),
    }

def second_block(x, p, ln_in_g, ln_in_b, rel_bias, w_in, tok_mix, decay_base, decay_up,
              aaa_base, aaa_up, gate_up, k_k, k_a, r_k, vres_base, vres_down, vres_up,
              gn_g, gn_b, w_branch_attn, w_branch_rwkv, w_out, router_grp, router_grp_bias,
              router_exp, router_exp_bias, exp_gate, exp_up, exp_down, ple_proj, ple_gate,
              ln_g, ln_b):
    x = layer_norm(x, ln_in_g, ln_in_b)
    v_first = None
    for i in range(DEPTH_2):
        proj = x @ w_in[i]
        y_attn = chunked_band_attention(proj[..., Q0:K0], proj[..., K0:V0], proj[..., V0:RW0], rel_bias)
        vres = None if i == 0 else (vres_base[i - 1], vres_down[i - 1], vres_up[i - 1])
        y_rwkv, v_first = rwkv7_time_mix(proj[..., RW0:GATE0], tok_mix[i], v_first, decay_base[i],
                                         decay_up[i], aaa_base[i], aaa_up[i], gate_up[i], k_k[i],
                                         k_a[i], r_k[i], gn_g[i], gn_b[i], vres)
        gate_a = jax.nn.sigmoid(proj[..., GATE0:GATE0 + D_MODEL])
        gate_b = jax.nn.sigmoid(proj[..., GATE0 + D_MODEL:])
        mixed = (gate_a * (y_attn @ w_branch_attn[i]) + gate_b * (y_rwkv @ w_branch_rwkv[i])) @ w_out[i]
        x = layer_norm(DEEPNORM_ALPHA * x + mixed, ln_g[i, 0], ln_b[i, 0])
        moe = hier_moe(x, router_grp[i], router_grp_bias[i], router_exp[i], router_exp_bias[i],
                       exp_gate[i], exp_up[i], exp_down[i])
        x = layer_norm(DEEPNORM_ALPHA * x + moe, ln_g[i, 1], ln_b[i, 1])
        ple = (p[i] @ ple_proj[i]) * jax.nn.sigmoid(x @ ple_gate[i])
        x = layer_norm(DEEPNORM_ALPHA * x + ple, ln_g[i, 2], ln_b[i, 2])
    return x


def setup_inputs(seed=0):
    out = dict(first_inputs(seed))
    for name, value in second_inputs(seed + 1).items():
        if name != "x":
            out[name + "_2"] = value
    return out


def reference(
    x, norm_mix, norm_ffn, even_w_in, even_w_out, odd_w_in, odd_conv, odd_w_out, peer_w_q,
    peer_sub_keys, peer_u, peer_v, final_norm, p_2, ln_in_g_2, ln_in_b_2, rel_bias_2, w_in_2,
    tok_mix_2, decay_base_2, decay_up_2, aaa_base_2, aaa_up_2, gate_up_2, k_k_2, k_a_2, r_k_2,
    vres_base_2, vres_down_2, vres_up_2, gn_g_2, gn_b_2, w_branch_attn_2, w_branch_rwkv_2,
    w_out_2, router_grp_2, router_grp_bias_2, router_exp_2, router_exp_bias_2, exp_gate_2,
    exp_up_2, exp_down_2, ple_proj_2, ple_gate_2, ln_g_2, ln_b_2,
):
    x = first_block(
        x, norm_mix, norm_ffn, even_w_in, even_w_out, odd_w_in, odd_conv, odd_w_out, peer_w_q,
        peer_sub_keys, peer_u, peer_v, final_norm,
    )
    return second_block(
        x, p_2, ln_in_g_2, ln_in_b_2, rel_bias_2, w_in_2, tok_mix_2, decay_base_2, decay_up_2,
        aaa_base_2, aaa_up_2, gate_up_2, k_k_2, k_a_2, r_k_2, vres_base_2, vres_down_2,
        vres_up_2, gn_g_2, gn_b_2, w_branch_attn_2, w_branch_rwkv_2, w_out_2, router_grp_2,
        router_grp_bias_2, router_exp_2, router_exp_bias_2, exp_gate_2, exp_up_2, exp_down_2,
        ple_proj_2, ple_gate_2, ln_g_2, ln_b_2,
    )


_drawn_inputs = setup_inputs


def setup_inputs(seed=0):
    import zlib

    import numpy as np

    out = dict(_drawn_inputs(seed))
    spreads = {}
    factors = {'norm_ffn': 3.673,
     'rel_bias_2': 28.765,
     'decay_up_2': 8.0,
     'aaa_base_2': 8.0,
     'k_k_2': 193.057,
     'k_a_2': 8.0,
     'r_k_2': 3.427,
     'gn_g_2': 32.141,
     'gn_b_2': 92.158,
     'w_branch_attn_2': 2.705,
     'router_grp_bias_2': 21.163,
     'router_exp_bias_2': 22.397}
    for name, (base, spread) in spreads.items():
        noise = np.random.default_rng([zlib.crc32(name.encode()), seed]).standard_normal(out[name].shape)
        drawn = base * np.exp(spread * noise) if base else spread * noise
        out[name] = __import__('jax').numpy.asarray(drawn.astype(out[name].dtype))
    for name, factor in factors.items():
        out[name] = (out[name] * factor).astype(out[name].dtype)
    return out
```

```python
from contextlib import ExitStack

import numpy as np

import concourse.bass as bass
from concourse import mybir

ALU = mybir.AluOpType
ACT = mybir.ActivationFunctionType
F32 = mybir.dt.float32
U32 = mybir.dt.uint32
AX = mybir.AxisListType.X

P = 128
T = 256
NX = T // P
D = 1024
KD = D // P
RING = 4
BLK = 1024
EPS = 1e-6
LN_EPS = 1e-5
GN_EPS = 64e-5
ALPHA = 2.0 ** 0.25
NEG = -1e30

LAYERS = 2
HEADS1 = 4
HD1 = 128
PEER_H = 8
NK = 128
TOPK = 16
HALF = NK // 2
GTOK = 4

HEADS2 = 8
HD2 = 64
RW_TILES = 15
CH = 32
NCH = T // CH
NEXP = 32
DEXP = 256
ATT_COLS = 3 * P

STREAM = [("even_qk", 16), ("even_vg", 12), ("even_out", 8)]
for _l in range(LAYERS):
    if _l == 1:
        STREAM += [("odd_in", 24), ("odd_out", 8)]
    STREAM += [(f"peer_q{_l}", 16), (f"peer_keys{_l}", 2), (f"peer_u{_l}", NK), (f"peer_v{_l}", NK)]
STREAM += [("qk2", 8), ("v2", 4), ("rw2", RW_TILES), ("gate2", 16), ("branch", 8), ("out2", 8),
           ("moe", 6 * NEXP), ("ple_proj", 2), ("ple_gate", 8)]
BASE, _n = {}, 0
for _name, _k in STREAM:
    BASE[_name] = _n
    _n += _k
FMBASE, _n = {}, 0
for _name, _k in STREAM:
    if _name in ("even_qk", "odd_in", "qk2", "rw2", "gate2") or _name[:6] in ("peer_q", "peer_u"):
        FMBASE[_name] = _n
        _n += _k

def _order(*names):
    return {name: n + 1 for n, name in enumerate(names)}


NORMED = _order("mix0", "cat", "ffn0", "route0", "mix1", "ffn1", "route1", "blk2", "band", "ln0", "comb", "ln1", "ln2")
FM = _order("mix0", "cat", "ffn0", "mix1", "conv", "ffn1", "blk2", "band", "til", "rwkv", "mixed", "ln0", "comb", "ln1")
ROOT = _order("mix0", "ret", "ffn0", "mix1", "ffn1", "final", "ln_in", "kk", "gn", "ln0", "ln1", "ln2")

VEC, _n = {}, 0
for _name, _k in (("mix0", 8), ("mix1", 8), ("ffn0", 8), ("ffn1", 8), ("conv", 24), ("mu", RW_TILES), ("decay", 4),
                  ("aaa", 4), ("k_k", 4), ("k_a", 4), ("r_k", 4), ("gn_g", 4), ("gn_b", 4)):
    VEC[_name] = _n
    _n += _k
NVEC = _n

CA, CB, CC = {}, {}, {}
for _tab, _items in ((CA, (("ident", 128), ("iota", 128))),
                     (CB, (("rot", 128), ("cos", T), ("sin", T), ("causal", ATT_COLS), ("decay", HEADS1 * ATT_COLS))),
                     (CC, (("up16", 128), ("low16", 128), ("off32", 128), ("up32", 128), ("upi32", 128),
                           ("ones64", 128), ("eye64", 64), ("ones", 128), ("iota8", 8), ("start", T)))):
    _n = 0
    for _name, _k in _items:
        _tab[_name] = (_n, _k)
        _n += _k
    _tab["all"] = (0, _n)


def constant_tables():
    f = np.float32
    i = np.arange(P)
    a = np.zeros((P, CA["all"][1]), f)
    a[:, 0:128] = np.eye(P, dtype=f)
    a[:, 128:256] = np.arange(128, dtype=f)
    b = np.zeros((P, CB["all"][1]), f)

    def put(tab, arr, name, val):
        s, n = tab[name]
        arr[:, s:s + n] = val

    rot = np.zeros((P, P), f)
    rot[i[:64] + 64, i[:64]] = -1.0
    rot[i[:64], i[:64] + 64] = 1.0
    put(CB, b, "rot", rot)
    half = HD1 // 2
    inv = (f(10000.0) ** (-np.arange(half, dtype=f) / f(half))).astype(f)
    ang = (np.arange(T, dtype=f)[:, None] * inv[None, :]).astype(f)
    put(CB, b, "cos", np.cos(ang).astype(f).T[i % half])
    put(CB, b, "sin", np.sin(ang).astype(f).T[i % half])
    causal = np.zeros((P, 3, P), f)
    causal[:, 0] = causal[:, 2] = np.where(i[None, :] <= i[:, None], 0.0, NEG)
    put(CB, b, "causal", causal.reshape(P, -1))
    dec = np.zeros((P, HEADS1, 3, P))
    for h in range(HEADS1):
        lg = np.log(1.0 - 2.0 ** (-5.0 - h))
        diff = (i[None, :] - i[:, None]).astype(np.float64)
        dec[:, h, 0] = dec[:, h, 2] = np.where(diff >= 0, np.exp(lg * np.maximum(diff, 0)), 0.0)
        dec[:, h, 1] = np.exp(lg * (diff + P))
    put(CB, b, "decay", (dec * HD1 ** -0.5).astype(f).reshape(P, -1))
    c = np.zeros((P, CC["all"][1]), f)
    s, t = i[:, None], i[None, :]
    put(CC, c, "up16", (s // 16 == t // 16) & (s < t))
    put(CC, c, "low16", (s // 16 == t // 16) & (s > t))
    put(CC, c, "off32", (s // 32 == t // 32) & (s // 16 < t // 16))
    put(CC, c, "up32", (s // 32 == t // 32) & (s < t))
    put(CC, c, "upi32", (s // 32 == t // 32) & (s <= t))
    put(CC, c, "ones64", s // 64 == t // 64)
    put(CC, c, "eye64", i[:, None] % 64 == np.arange(64)[None, :])
    put(CC, c, "ones", 1.0)
    put(CC, c, "iota8", np.arange(8))
    put(CC, c, "start", (np.arange(T) % CH != 0)[None, :])
    return a, b, c


def build(nc, dram, out):
    with ExitStack() as ctx:
        def sb(name, cols, dt=F32):
            return ctx.enter_context(nc.sbuf_tensor(name, [P, cols], dt))

        def ps(name, banks):
            return ctx.enter_context(nc.psum_tensor(name, [P, banks, 512], F32))

        def sem(name):
            return ctx.enter_context(nc.semaphore(name))

        ring = ctx.enter_context(nc.sbuf_tensor("ring", [P, RING, BLK], F32))
        resid = ctx.enter_context(nc.sbuf_tensor("resid", [P, NX, D], F32))
        xT = ctx.enter_context(nc.sbuf_tensor("xT", [P, KD, T], F32))
        const_a = sb("const_a", CA["all"][1])
        const_c = sb("const_c", CC["all"][1])
        vec = sb("vec", NVEC)
        gains = ctx.enter_context(nc.sbuf_tensor("gains", [P, 2, 2, D], F32))
        hk = ctx.enter_context(nc.sbuf_tensor("hk", [P, 3, T], F32))
        hot1 = ctx.enter_context(nc.sbuf_tensor("hot1", [P, GTOK, NK], F32))
        hot2 = ctx.enter_context(nc.sbuf_tensor("hot2", [P, GTOK, HALF], F32))
        gates2 = ctx.enter_context(nc.sbuf_tensor("gates2", [P, 16, T], F32))
        router = ctx.enter_context(nc.sbuf_tensor("router", [P, KD, 36], F32))
        router_b = sb("router_b", 36)
        st = sb("st", 128)
        arena = sb("arena", NK * T)

        def at(off, *dims):
            n = int(np.prod(dims))
            assert off + n <= NK * T
            v = arena[:, off:off + n]
            if len(dims) == 2:
                v = v.rearrange("p (a b) -> p a b", b=dims[1])
            elif len(dims) == 3:
                v = v.rearrange("p (a b c) -> p a b c", b=dims[1], c=dims[2])
            return v

        def ca(name):
            return const_a[:, CA[name][0]:CA[name][0] + CA[name][1]]

        def cc(name):
            return const_c[:, CC[name][0]:CC[name][0] + CC[name][1]]

        def vcol(name, i, n=1):
            return vec[:, VEC[name] + i:VEC[name] + i + n]

        ident, iota = ca("ident"), ca("iota")
        const_b = at(0, CB["all"][1])

        def cb(name):
            return const_b[:, CB[name][0]:CB[name][0] + CB[name][1]]

        o = CB["all"][1]
        qk1 = at(o, 16, T); o += 16 * T
        v_moba = at(o, NX, 512); o += NX * 512
        v_ret = at(o, NX, 512); o += NX * 512
        g_ret = at(o, NX, 512); o += NX * 512
        sc1 = at(o, HEADS1, ATT_COLS); o += HEADS1 * ATT_COLS
        pT1 = at(o, HEADS1, ATT_COLS); o += HEADS1 * ATT_COLS
        rT1 = at(o, HEADS1, ATT_COLS); o += HEADS1 * ATT_COLS
        cat1 = at(o, NX, D); o += NX * D
        rope_tmp = at(o, 2, T); o += 2 * T
        xn = at(24576, NX, D)
        ret_sq = at(26624, NX, 512)
        hid = at(0, NK, T)
        peer_qT = at(16384, 16, T)
        score = at(20480, NX, 16, NK)
        o = 26624
        top_s = at(o, 16, TOPK); o += 256
        top_u = at(o, 16, TOPK); o += 256
        top_f = at(o, 16, TOPK); o += 256
        sel_s = at(o, NX, PEER_H, TOPK); o += 256
        pos_u = at(o, PEER_H, TOPK); o += 128
        pos_a = at(o, PEER_H, TOPK); o += 128
        pos_f = at(o, PEER_H, TOPK); o += 128
        sel_i = at(o, 3, NX, P); o += 3 * 256
        cand = at(o, PEER_H, TOPK * TOPK); o += 2048
        pick = at(24576, PEER_H * TOPK, TOPK)
        assert o <= NK * T
        peer_yT = at(0, KD, T)
        cv_b = at(0, KD, T)
        cv_c = at(2048, KD, T)
        cv_h = at(4096, KD, T)
        cv_u = at(6144, KD, T + 2)
        cv_y = at(8448, KD, T)
        cv_z = at(10496, KD, T)
        rkv = at(1024, 12, T)
        r_fm, k_fm, v_fm = (at(1024 * (1 + n), 4, T) for n in range(3))
        g_fm = at(4096, 4, T)
        a_til, b_til, k_til, r_til = (at(5120 + 1024 * n, 4, T) for n in range(4))
        a_tm, bh_tm, kh_tm, v_tm = (at(9216 + 1024 * n, NX, 512) for n in range(4))
        qk2 = at(5120, 8, T)
        v2 = at(7168, NX, 512)
        sc2 = at(8192, 4, ATT_COLS)
        pT2 = at(9728, 4, ATT_COLS)
        ob2 = at(11264, NX, 512)
        ya_fm = at(13312, 4, T)
        step_m = at(14336, 4, NCH, HD2)
        step_n = at(16384, 4, NCH, HD2)
        state = at(18432, NCH, 4, HD2)
        q_eff = at(20736, 4, T)
        y_fm = at(21760, 4, T)
        sol = at(22784, 8, P)
        mats = [at(23808 + 1024 * n, 8, P) for n in range(8)]
        cols = at(14336, RW_TILES, T + 1)
        kk_fm = at(18432, 4, T)
        aa_fm = at(19456, 4, T)
        cum = at(20480, 4, T)
        e1 = at(21504, 4, T)
        e2 = at(22528, 4, T)
        bh_fm = at(23552, 4, T)
        kh_fm = at(24576, 4, T)
        lora = at(25600, 3, 512)
        band_bias = at(27136, HEADS2, ATT_COLS)
        low = at(30208, 3, T)
        shift = at(4096, 2, T)
        y_out = at(22784, 4, T)
        y_sq = at(23808, 4, T)
        y_mu = at(24832, 4, T)
        y_rs = at(25856, 4, T)
        bonus = at(26880, 4, T)
        y_tmp = at(27904, 4, T)
        mixT = at(5120, KD, T)
        mix_tmp = at(7168, 2, T)
        comb_d = at(0, NEXP, T)
        h_sig = at(8192, 2, 2 * T)
        h_mid = at(9216, 2, 2 * T)
        o = 10240
        logit = at(o, NX, 36); o += 72
        g8 = at(o, NX, 8); o += 16
        g8m = at(o, NX, 8); o += 16
        g8i = at(o, NX, 8); o += 16
        hot_g = at(o, NX, 8); o += 16
        sel8 = at(o, NX, 8); o += 16
        sel8m = at(o, NX, 8); o += 16
        sel8i = at(o, NX, 8); o += 16
        sel8f = at(o, NX, 8); o += 16
        sel_t = at(o, NX, 8, 4); o += 64
        comb8 = at(o, NX, 8); o += 16
        comb8b = at(o, NX, 8); o += 16
        comb = at(o, NX, NEXP); o += 64
        combT = at(o, T); o += T
        pT_ple = at(12288, 2, T)
        ple = at(12800, NX, D)
        sig_ple = at(14848, NX, D)
        ln_sq = at(31744, D)

        acc = ps("acc", 4)
        prod = ps("prod", 2)
        gen = ps("gen", 2)

        landed = [sem(f"landed{i}") for i in range(RING)]
        w_used = sem("w_used")
        fm_out = sem("fm_out")
        acc_out = sem("acc_out")
        gen_mm = sem("gen_mm")
        gen_out = sem("gen_out")
        x_in = sem("x_in")
        small_in = sem("small_in")
        table_b_in = sem("table_b_in")
        gain_in = [sem("gain_in0"), sem("gain_in1")]
        gain_used = sem("gain_used")
        block2_in = sem("block2_in")
        ple_in = sem("ple_in")
        arena_free = sem("arena_free")
        ms_ready = sem("ms_ready")
        root_ready = sem("root_ready")
        normed = sem("normed")
        fm_ready = sem("fm_ready")
        roped = sem("roped")
        att_s = sem("att_s")
        att_m = sem("att_m")
        att_p = sem("att_p")
        att_pt = sem("att_pt")
        att_o = sem("att_o")
        att_done = sem("att_done")
        topk_ready = sem("topk_ready")
        gate_exp = sem("gate_exp")
        hot_ready = sem("hot_ready")
        tok_mm = sem("tok_mm")
        gated = sem("gated")
        yT_ready = sem("yT_ready")
        conv_in = sem("conv_in")
        shifted = sem("shifted")
        low_act = sem("low_act")
        lora_mm = sem("lora_mm")
        lora_out = sem("lora_out")
        logw_ready = sem("logw_ready")
        exp_ready = sem("exp_ready")
        til_ready = sem("til_ready")
        sq_ready = sem("sq_ready")
        scan_mm = sem("scan_mm")
        state_ready = sem("state_ready")
        branch_out = sem("branch_out")
        silu_ready = sem("silu_ready")
        mid_ready = sem("mid_ready")
        comb_mm = sem("comb_mm")
        max_ready = sem("max_ready")
        moe_exp = sem("moe_exp")
        ple_sig = sem("ple_sig")
        v_chain = sem("v_chain")
        a_chain = sem("a_chain")
        out_done = sem("out_done")

        block = ctx.enter_context(nc.Block())

        @block.sync
        def _(sp):
            def load(g, src, later=0):
                if g >= RING:
                    sp.wait_ge(w_used, g - RING + 1 + later)
                sp.dma_start(ring[:, g % RING, :], src).then_inc(landed[g % RING], 16)

            def stream(name, src, n, first=0):
                base = BASE[name]
                start = 0
                if base + first == 0:
                    for j in range(RING):
                        load(j, src[j])
                    start = 1
                whole = n // RING
                if whole - start > 1:
                    with sp.Fori(start, whole) as i:
                        for j in range(RING):
                            load(base + RING + j, src[RING * i + j], RING * i - RING) if base + j < RING else \
                                load(base + j, src[RING * i + j], RING * i)
                else:
                    for b in range(RING * start, RING * whole):
                        load(base + b, src[b])
                for b in range(RING * whole, n):
                    load(base + b, src[b])

            for name in ("even_qk", "even_vg", "even_out"):
                stream(name, dram[name], dict(STREAM)[name])
            for layer in range(LAYERS):
                if layer == 1:
                    stream("odd_in", dram["odd_in"], 24)
                    stream("odd_out", dram["odd_out"], 8)
                stream(f"peer_q{layer}", dram[f"peer_q{layer}"], 16)
                stream(f"peer_keys{layer}", dram[f"peer_keys{layer}"], 2)
                stream(f"peer_u{layer}", dram[f"peer_u{layer}"], NK)
                stream(f"peer_v{layer}", dram["peer_v"][layer].rearrange("(a c) d -> c a d", c=NK), NK)
            stream("qk2", dram["qk2"], 8)
            stream("v2", dram["v2"], 4)
            stream("rw2", dram["rw2"], RW_TILES)
            stream("gate2", dram["gate2"], 16)
            for j in range(4):
                load(BASE["branch"] + 2 * j, dram["branch_a"][j])
                load(BASE["branch"] + 2 * j + 1, dram["branch_r"][j])
            stream("out2", dram["out2"], 8)
            g = BASE["moe"]
            for j in range(4):
                load(g + j, (dram["exp_gate"], dram["exp_up"])[j // 2][j % 2])

            def expert(g, e, later):
                for j in range(4):
                    load(g + j, (dram["exp_gate"], dram["exp_up"])[j // 2][2 * e + j % 2], later)
                for j in range(2):
                    load(g + 4 + j, dram["exp_down"][2 * e - 2 + j], later)

            with sp.Fori(0, (NEXP - 2) // 2) as i:
                for j in range(2):
                    expert(g + 4 + 6 * j, 2 * i + 1 + j, 12 * i)
            expert(g + 4 + 6 * (NEXP - 2), NEXP - 1, 0)
            for j in range(2):
                load(g + 6 * NEXP - 2 + j, dram["exp_down"][2 * NEXP - 2 + j])
            stream("ple_proj", dram["ple_proj"], 2)
            stream("ple_gate", dram["ple_gate"], 8)
            sp.wait_ge(normed, NORMED["ln2"])
            sp.dma_start(out.rearrange("a (x p) d -> p (a x) d", p=P), resid[:, :, :]).then_inc(out_done, 16)
            sp.wait_ge(out_done, 16)

        @block.gpsimd
        def _(pool):
            pool.dma_start(const_a[:, :], dram["const_a"]).then_inc(small_in, 16)
            pool.dma_start(vec[:, :], dram["vec"]).then_inc(small_in, 16)
            pool.dma_start(const_b, dram["const_b"]).then_inc(table_b_in, 16)
            pool.dma_start(gains[:, 0, 0, :], dram["final_norm"].partition_broadcast(P)).then_inc(gain_in[0], 16)
            pool.dma_start(gains[:, 1, 0, :], dram["ln_in_g"].partition_broadcast(P)).then_inc(gain_in[1], 16)
            pool.dma_start(gains[:, 1, 1, :], dram["ln_in_b"].partition_broadcast(P)).then_inc(gain_in[1], 16)
            pool.dma_start(const_c[:, :], dram["const_c"]).then_inc(small_in, 16)
            pool.dma_start(router[:, :, :], dram["router"]).then_inc(small_in, 16)
            pool.dma_start(router_b[:, :], dram["router_b"].partition_broadcast(P)).then_inc(small_in, 16)
            pool.wait_ge(arena_free, 1)
            pool.dma_start(lora[:, :, :], dram["lora"]).then_inc(block2_in, 16)
            pool.dma_start(band_bias[:, :, :], dram["band_bias"]).then_inc(block2_in, 16)
            for n in range(3):
                pool.wait_ge(gain_used, n + 1)
                for j, name in enumerate(("ln_g", "ln_b")):
                    pool.dma_start(gains[:, n % 2, j, :], dram[name][n].partition_broadcast(P)).then_inc(gain_in[n % 2], 16)
            pool.dma_start(pT_ple[:, :, :], dram["p"]).then_inc(ple_in, 16)
            pool.wait_ge(ple_in, 16)

        @block.tensor
        def _(pe):
            gi = [0]
            au = [0]

            def arrive(g, later=0):
                pe.wait_ge(landed[g % RING], 16 * (g // RING + 1) + later)
                return ring[:, g % RING, :]

            def gen_bank():
                if gi[0] >= 2:
                    pe.wait_ge(gen_out, gi[0] - 1)
                gi[0] += 1
                return gen[:, (gi[0] - 1) % 2, :]

            def acc_free():
                if au[0]:
                    pe.wait_ge(acc_out, au[0])
                au[0] += 1

            def fm_block(g, f, later=0, flater=0):
                w = arrive(g, later)
                if f >= 2:
                    pe.wait_ge(fm_out, f - 1 + flater)
                for k in range(KD):
                    mm = pe.matmul(prod[:, f % 2, 0:T], w[:, k * P:(k + 1) * P], xT[:, k, :],
                                   start=(k == 0), stop=(k == KD - 1))
                mm.then_inc(w_used, 1)

            def tm_block(g, lhs, kpair, banks, last):
                w = arrive(g)
                for x in range(NX):
                    for k in range(2):
                        kk = 2 * kpair + k
                        mm = pe.matmul(acc[:, banks[x], :], lhs[:, kk, x * P:(x + 1) * P], w[:, k * 512:(k + 1) * 512],
                                       start=(kk == 0), stop=(kk == last))
                mm.then_inc(w_used, 1)

            def tm_square(name, lhs):
                acc_free()
                for b in range(8):
                    tm_block(BASE[name] + b, lhs, b % 4, (b // 4, 2 + b // 4), KD - 1)

            def turn(src, tiles):
                for x in range(NX):
                    for q in range(tiles // 4):
                        bank = gen_bank()
                        for k in range(4):
                            mm = pe.transpose(bank[:, k * P:(k + 1) * P], src[:, x, (4 * q + k) * P:(4 * q + k + 1) * P], ident)
                        mm.then_inc(gen_mm, 1)

            def attend_scores(q_of, k_of):
                acc_free()
                for h in range(4):
                    pe.matmul(acc[:, h, 0:P], q_of(h)[:, 0:P], k_of(h)[:, 0:P], start=True, stop=True)
                    pe.matmul(acc[:, h, P:ATT_COLS], q_of(h)[:, P:T], k_of(h), start=True, stop=True).then_inc(att_s, 1)

            def attend_values(soft, turned, p_sb, pT, v_of, width):
                for h in range(4):
                    pe.wait_ge(att_p, soft + h + 1)
                    bank = gen_bank()
                    for b in range(3):
                        mm = pe.transpose(bank[:, b * P:(b + 1) * P], p_sb[:, h, b * P:(b + 1) * P], ident)
                    mm.then_inc(gen_mm, 1)
                for h in range(4):
                    pe.wait_ge(att_pt, turned + h + 1)
                    values(pT, v_of, h, width, h == 3)

            def values(pT, v_of, h, width, last):
                cols_ = slice(h * width, (h + 1) * width)
                pe.matmul(prod[:, 0, cols_], pT[:, h, 0:P], v_of(0, h), start=True, stop=True)
                pe.matmul(prod[:, 1, cols_], pT[:, h, P:2 * P], v_of(0, h), start=True, stop=False)
                mm = pe.matmul(prod[:, 1, cols_], pT[:, h, 2 * P:3 * P], v_of(1, h), start=False, stop=True)
                if last:
                    mm.then_inc(att_o, 1)

            pe.wait_ge(small_in, 80)
            pe.wait_ge(normed, NORMED["mix0"])
            turn(xn, KD)
            pe.wait_ge(fm_ready, FM["mix0"])
            for b in range(16):
                fm_block(BASE["even_qk"] + b, FMBASE["even_qk"] + b)
            pe.wait_ge(table_b_in, 16)
            for b in range(12):
                if b in (0, 8):
                    acc_free()
                tm_block(BASE["even_vg"] + b, xT, b % 4, ((0, 1), (2, 3), (0, 1))[b // 4], KD - 1)
                if b < 8:
                    pe.wait_ge(fm_out, 2 * b + 2)
                    pe.matmul(gen_bank(), cb("rot"), qk1[:, 2 * b:2 * b + 2, :].rearrange("p a b -> p (a b)"),
                              start=True, stop=True).then_inc(gen_mm, 1)
            pe.wait_ge(roped, 8)
            attend_scores(lambda h: qk1[:, h, :], lambda h: qk1[:, 4 + h, :])
            attend_values(0, 0, sc1, pT1, lambda x, h: v_moba[:, x, h * HD1:(h + 1) * HD1], HD1)
            acc_free()
            for h in range(4):
                q, k = qk1[:, 8 + h, :], qk1[:, 12 + h, :]
                pe.matmul(acc[:, h, 0:T], k[:, 0:P], q, start=True, stop=True)
                pe.matmul(acc[:, h, T:ATT_COLS], k[:, P:T], q[:, P:T], start=True, stop=True).then_inc(att_s, 1)
            pe.wait_ge(att_done, 1)
            for h in range(4):
                pe.wait_ge(att_pt, 4 + h + 1)
                values(rT1, lambda x, h: v_ret[:, x, h * HD1:(h + 1) * HD1], h, HD1, h == 3)
            pe.wait_ge(normed, NORMED["cat"])
            turn(cat1, KD)
            pe.wait_ge(fm_ready, FM["cat"])
            tm_square("even_out", xT)

            def peer(layer):
                pe.wait_ge(normed, NORMED[f"ffn{layer}"])
                turn(xn, KD)
                pe.wait_ge(fm_ready, FM[f"ffn{layer}"])
                pe.wait_ge(att_done, 2)
                for b in range(16):
                    fm_block(BASE[f"peer_q{layer}"] + b, FMBASE[f"peer_q{layer}"] + b)
                pe.wait_ge(fm_out, FMBASE[f"peer_q{layer}"] + 16)
                for b in range(2):
                    w = arrive(BASE[f"peer_keys{layer}"] + b)
                    for x in range(NX):
                        for q in range(2):
                            bank = gen_bank()
                            for j in range(4):
                                n = 4 * q + j
                                mm = pe.matmul(bank[:, j * P:(j + 1) * P], peer_qT[:, 8 * b + n, x * P:(x + 1) * P],
                                               w[:, n * P:(n + 1) * P], start=True, stop=True)
                            mm.then_inc(gen_mm, 1)
                    pe.wait_ge(gen_mm, gi[0])
                    pe.nop().then_inc(w_used, 1)
                ub, fb, vb = BASE[f"peer_u{layer}"], FMBASE[f"peer_u{layer}"], BASE[f"peer_v{layer}"]
                tb = 2 * layer * HALF

                def hidden(i, j):
                    fm_block(ub + j, fb + j, 16 * i, RING * i)

                def token_gates(i, j, half):
                    pe.wait_ge(hot_ready, tb + half * HALF + j + 1 + RING * i)
                    for t in range(GTOK):
                        mm = pe.matmul(gen[:, 0, t * HALF:(t + 1) * HALF], hot1[:, t, :], hot2[:, t, :],
                                       start=True, stop=True)
                    mm.then_inc(tok_mm, 1)

                def down(i, j, first=False, last=False):
                    w = arrive(vb + j, 16 * i)
                    for d in range(KD):
                        mm = pe.matmul(acc[:, d // 2, (d % 2) * T:(d % 2 + 1) * T], w[:, d * P:(d + 1) * P],
                                       hid[:, RING * i + j, :], start=(first and d % 2 == 0), stop=last,
                                       skip_group_check=True)
                    mm.then_inc(w_used, 1)

                with pe.Fori(0, HALF // RING) as i:
                    for j in range(RING):
                        hidden(i, j)
                pe.wait_ge(normed, NORMED[f"route{layer}"])
                for x in range(NX):
                    bank = gen_bank()
                    for n in range(3):
                        mm = pe.transpose(bank[:, n * P:(n + 1) * P], sel_i[:, n, x, :], ident)
                    mm.then_inc(gen_mm, 1)
                with pe.Fori(0, HALF // RING) as i:
                    for j in range(RING):
                        token_gates(i, j, 0)
                        hidden(i + HALF // RING, j)
                acc_free()
                pe.wait_ge(gated, tb + HALF)
                for j in range(RING):
                    token_gates(0, j, 1)
                    down(0, j, first=(j == 0))
                with pe.Fori(1, HALF // RING) as i:
                    for j in range(RING):
                        token_gates(i, j, 1)
                        down(i, j)
                pe.wait_ge(gated, tb + 2 * HALF)
                with pe.Fori(HALF // RING, NK // RING - 1) as i:
                    for j in range(RING):
                        down(i, j)
                for j in range(RING):
                    down(NK // RING - 1, j, last=(j == RING - 1))
                pe.wait_ge(acc_out, au[0])
                for x in range(NX):
                    for q in range(2):
                        bank = gen_bank()
                        for k in range(4):
                            mm = pe.transpose(bank[:, k * P:(k + 1) * P], peer_yT[:, 4 * q + k, x * P:(x + 1) * P], ident)
                        mm.then_inc(gen_mm, 1)

            peer(0)
            pe.wait_ge(normed, NORMED["mix1"])
            turn(xn, KD)
            pe.wait_ge(fm_ready, FM["mix1"])
            for b in range(24):
                fm_block(BASE["odd_in"] + b, FMBASE["odd_in"] + b)
            pe.wait_ge(fm_ready, FM["conv"])
            tm_square("odd_out", cv_z)
            peer(1)
            pe.wait_ge(normed, NORMED["blk2"])
            turn(resid, KD)
            pe.wait_ge(fm_ready, FM["blk2"])
            for b in range(8):
                fm_block(BASE["qk2"] + b, FMBASE["qk2"] + b)
            acc_free()
            for b in range(4):
                tm_block(BASE["v2"] + b, xT, b, (0, 1), KD - 1)
            pe.wait_ge(fm_out, FMBASE["rw2"])

            def band(r):
                def rows(h, tile):
                    hh = 4 * r + h
                    return qk2[HD2 * (hh % 2):HD2 * (hh % 2 + 1), tile + hh // 2, :]
                return lambda h: rows(h, 0), lambda h: rows(h, 4), \
                    lambda x, h: v2[:, x, (4 * r + h) * HD2:(4 * r + h + 1) * HD2]

            q_of, k_of, v_of = band(0)
            attend_scores(q_of, k_of)
            for b in range(RW_TILES):
                fm_block(BASE["rw2"] + b, FMBASE["rw2"] + b)
            pe.wait_ge(fm_out, FMBASE["gate2"])
            attend_values(4, 8, sc2, pT2, v_of, HD2)
            q_of, k_of, v_of = band(1)
            pe.wait_ge(att_done, 3)
            attend_scores(q_of, k_of)
            for b in range(16):
                fm_block(BASE["gate2"] + b, FMBASE["gate2"] + b)
            pe.wait_ge(fm_out, FMBASE["gate2"] + 16)
            attend_values(8, 12, sc2, pT2, v_of, HD2)
            pe.wait_ge(normed, NORMED["band"])
            turn(ob2, 4)
            pe.wait_ge(block2_in, 32)
            pe.wait_ge(low_act, 2)
            for n in range(6):
                if n >= 2:
                    pe.wait_ge(lora_out, n - 1)
                for j in range(2):
                    f = 2 * (n % 2) + j
                    dst = prod[:, n % 2, j * T:(j + 1) * T]
                    if n < 4:
                        rows = slice(64 * (n // 2), 64 * (n // 2) + 64)
                        mm = pe.matmul(dst, lora[rows, 0, f * P:(f + 1) * P], low[rows, 0, :], start=True, stop=True)
                    else:
                        pe.matmul(dst, lora[:, 1, f * P:(f + 1) * P], low[:, 1, :], start=True, stop=False)
                        mm = pe.matmul(dst, lora[0:32, 2, f * P:(f + 1) * P], low[0:32, 2, :], start=False, stop=True)
                mm.then_inc(lora_mm, 1)

            def head_sums(src, count):
                pe.wait_ge(sq_ready, count)
                for q in range(2):
                    pe.matmul(gen_bank(), cc("ones64"), src[:, 2 * q:2 * q + 2, :].rearrange("p a b -> p (a b)"),
                              start=True, stop=True).then_inc(gen_mm, 1)

            head_sums(e1, 1)
            pe.wait_ge(fm_ready, FM["til"])
            for x in range(NX):
                for src in (a_til, bh_fm, kh_fm, v_fm):
                    bank = gen_bank()
                    for pr in range(4):
                        mm = pe.transpose(bank[:, pr * P:(pr + 1) * P], src[:, pr, x * P:(x + 1) * P], ident)
                    mm.then_inc(gen_mm, 1)

            def by_head(lhs, rhs, x):
                for q in range(2):
                    bank = gen_bank()
                    rows = slice(64 * q, 64 * q + 64)
                    for pr in range(4):
                        mm = pe.matmul(bank[:, pr * P:(pr + 1) * P], lhs[rows, pr, x * P:(x + 1) * P],
                                       rhs[rows, pr, x * P:(x + 1) * P], start=True, stop=True)
                    mm.then_inc(gen_mm, 1)

            def square(lhs, rhs):
                for q in range(2):
                    bank = gen_bank()
                    for u in range(4):
                        mm = pe.matmul(bank[:, u * P:(u + 1) * P], lhs[:, 4 * q + u, :], rhs[:, 4 * q + u, :],
                                       start=True, stop=True)
                    mm.then_inc(gen_mm, 1)

            def all_out():
                pe.wait_ge(gen_out, gi[0])

            m_lT, m_l, m_ak, m_rb, m_rk, m_off, m_a, m_b = mats
            for x in range(NX):
                by_head(b_til, a_til, x)
                by_head(a_til, b_til, x)
                by_head(k_til, a_til, x)
                by_head(b_til, r_til, x)
                by_head(k_til, r_til, x)
                all_out()
                bank = gen_bank()
                for hd in range(HEADS2):
                    mm = pe.matmul(bank[:, hd * HD2:(hd + 1) * HD2], m_ak[:, hd, :], v_tm[:, x, hd * HD2:(hd + 1) * HD2],
                                   start=True, stop=True)
                mm.then_inc(gen_mm, 1)
                square(m_lT, m_l)
                square(m_l, m_lT)
                all_out()
                square(m_a, m_ak)
                square(m_b, m_a)
                square(m_a, m_b)
                all_out()
                square(m_l, m_ak)
                square(m_lT, m_l)
                all_out()
                square(m_a, m_ak)
                all_out()
                square(m_ak, sol)
                all_out()
                square(m_off, m_b)
                all_out()
                square(m_ak, m_lT)
                all_out()
                bank = gen_bank()
                for hd in range(HEADS2):
                    rows = slice(64 * (hd % 2), 64 * (hd % 2) + 64)
                    mm = pe.matmul(bank[rows, (hd // 2) * P:(hd // 2 + 1) * P], sol[:, hd, 0:HD2], m_rb[:, hd, :],
                                   start=True, stop=True)
                mm.then_inc(gen_mm, 1)
                bank = gen_bank()
                for hd in range(HEADS2):
                    rows = slice(64 * (hd % 2), 64 * (hd % 2) + 64)
                    dst = bank[rows, (hd // 2) * P:(hd // 2 + 1) * P]
                    pe.matmul(dst, sol[:, hd, HD2:P], m_rb[:, hd, :], start=True, stop=False)
                    mm = pe.matmul(dst, v_tm[:, x, hd * HD2:(hd + 1) * HD2], m_rk[:, hd, :], start=False, stop=True)
                mm.then_inc(gen_mm, 1)
                for c in range(4):
                    bank = gen_bank()
                    tok = slice(CH * c, CH * c + CH)
                    for hd in range(HEADS2):
                        rows, hc = slice(64 * (hd % 2), 64 * (hd % 2) + 64), slice(hd * HD2, (hd + 1) * HD2)
                        o_ = (hd // 2) * HD2
                        pe.matmul(bank[rows, o_:o_ + HD2], sol[tok, hd, 0:HD2], bh_tm[tok, x, hc], start=True, stop=True)
                        o_ += 4 * HD2
                        pe.matmul(bank[rows, o_:o_ + HD2], bh_tm[tok, x, hc], sol[tok, hd, HD2:P], start=True, stop=False)
                        mm = pe.matmul(bank[rows, o_:o_ + HD2], kh_tm[tok, x, hc], v_tm[tok, x, hc], start=False, stop=True)
                    mm.then_inc(gen_mm, 1)
            for c in range(1, NCH - 1):
                pe.wait_ge(state_ready, c)
                bank = gen_bank()
                for hd in range(HEADS2):
                    rows = slice(64 * (hd % 2), 64 * (hd % 2) + 64)
                    mm = pe.matmul(bank[rows, (hd // 2) * HD2:(hd // 2 + 1) * HD2], step_m[rows, hd // 2, c, :],
                                   state[rows, c, hd // 2, :], start=True, stop=True)
                mm.then_inc(gen_mm, 1)
            pe.wait_ge(state_ready, NCH - 1)
            for q in range(2):
                bank = gen_bank()
                for hd in range(4 * q, 4 * q + 4):
                    rows = slice(64 * (hd % 2), 64 * (hd % 2) + 64)
                    for c in range(1, NCH):
                        o_ = (hd // 2 - 2 * q) * T + c * CH
                        mm = pe.matmul(bank[rows, o_:o_ + CH], state[rows, c, hd // 2, :],
                                       q_eff[rows, hd // 2, c * CH:(c + 1) * CH], start=True, stop=True)
                mm.then_inc(gen_mm, 1)
            head_sums(y_fm, 2)
            head_sums(y_sq, 3)
            head_sums(bonus, 4)
            pe.wait_ge(fm_ready, FM["rwkv"])
            pe.wait_ge(lora_out, 6)
            for j in range(4):
                if j:
                    pe.wait_ge(branch_out, j)
                for n, src in enumerate((ya_fm, y_out)):
                    w = arrive(BASE["branch"] + 2 * j + n)
                    for f in range(2):
                        for k in range(4):
                            mm = pe.matmul(prod[:, n, f * T:(f + 1) * T], w[:, (2 * k + f) * P:(2 * k + f + 1) * P],
                                           src[:, k, :], start=(k == 0), stop=(k == 3))
                    mm.then_inc(w_used, 1)
            pe.wait_ge(fm_ready, FM["mixed"])
            tm_square("out2", mixT)
            pe.wait_ge(normed, NORMED["ln0"])
            turn(resid, KD)
            pe.wait_ge(fm_ready, FM["ln0"])
            bank = gen_bank()
            for x in range(NX):
                for k in range(KD):
                    mm = pe.matmul(bank[:, x * 36:(x + 1) * 36], xT[:, k, x * P:(x + 1) * P], router[:, k, :],
                                   start=(k == 0), stop=(k == KD - 1))
            mm.then_inc(gen_mm, 1)
            pe.wait_ge(normed, NORMED["comb"])
            bank = gen_bank()
            for x in range(NX):
                mm = pe.transpose(bank[0:NEXP, x * P:(x + 1) * P], comb[:, x, :], ident)
            mm.then_inc(gen_mm, 1)
            pe.wait_ge(fm_ready, FM["comb"])
            acc_free()
            eb = BASE["moe"]

            def expert_up(g, e, later, elater, first=False):
                for n in range(2):
                    if not first:
                        pe.wait_ge((silu_ready, mid_ready)[n], e + elater)
                    for f in range(2):
                        w = arrive(g + 2 * n + f, later)
                        for k in range(KD):
                            mm = pe.matmul(prod[:, n, f * T:(f + 1) * T], w[:, k * P:(k + 1) * P], xT[:, k, :],
                                           start=(k == 0), stop=(k == KD - 1))
                        mm.then_inc(w_used, 1)
                pe.matmul(gen[:, 0, 0:T], cc("ones")[0:NEXP, :], comb_d[0:NEXP, e + elater, :], start=True, stop=True)\
                    .then_inc(comb_mm, 1)

            def expert_down(g, s, later, first=False, last=False):
                for f in range(2):
                    w = arrive(g + f, later)
                    for x in range(NX):
                        for n in range(2):
                            mm = pe.matmul(acc[:, 2 * x + n, :], h_mid[:, s, f * T + x * P:f * T + (x + 1) * P],
                                           w[:, n * 512:(n + 1) * 512], start=(first and f == 0), stop=(last and f == 1),
                                           skip_group_check=True)
                    mm.then_inc(w_used, 1)

            expert_up(eb, 0, 0, 0, first=True)
            expert_up(eb + 4, 1, 0, 0)
            expert_down(eb + 8, 0, 0, first=True)
            with pe.Fori(0, (NEXP - 2) // 2) as i:
                for j in range(2):
                    expert_up(eb + 10 + 6 * j, 2 + j, 48 * i, 2 * i)
                    expert_down(eb + 14 + 6 * j, (1 + j) % 2, 48 * i)
            pe.wait_ge(mid_ready, NEXP)
            expert_down(eb + 6 * NEXP - 2, (NEXP - 1) % 2, 0, last=True)
            acc_free()
            pe.wait_ge(ple_in, 16)
            for b in range(2):
                w = arrive(BASE["ple_proj"] + b)
                for x in range(NX):
                    for k in range(2):
                        mm = pe.matmul(acc[:, 2 * x + b, :], pT_ple[:, k, x * P:(x + 1) * P], w[:, k * 512:(k + 1) * 512],
                                       start=(k == 0), stop=(k == 1))
                mm.then_inc(w_used, 1)
            pe.wait_ge(normed, NORMED["ln1"])
            turn(resid, KD)
            pe.wait_ge(fm_ready, FM["ln1"])
            tm_square("ple_gate", xT)

        @block.scalar
        def _(act):
            def take(name, b, dst, func, **kw):
                act.wait_ge(w_used, BASE[name] + b + 1)
                act.activation(dst, prod[:, (FMBASE[name] + b) % 2, 0:T], func, **kw).then_inc(fm_out, 1)

            def root(name, dst, src):
                act.wait_ge(ms_ready, ROOT[name])
                act.activation(dst, src, ACT.Sqrt).then_inc(root_ready, 1)

            def norm_root(name):
                root(name, st[:, 4:6], st[:, 2:4])

            def soft(base, s):
                for h in range(4):
                    act.wait_ge(att_m, base + h + 1)
                    act.activation(s[:, h, 0:P], s[:, h, 0:P], ACT.Exp, bias=st[:, 16 + h:17 + h],
                                   accum_out=st[:, 24 + h:25 + h])
                    act.activation(s[:, h, P:ATT_COLS], s[:, h, P:ATT_COLS], ACT.Exp, bias=st[:, 20 + h:21 + h],
                                   accum_out=st[:, 28 + h:29 + h]).then_inc(att_p, 1)

            act.dma_start(resid[:, :, :], dram["x"].rearrange("a (x p) d -> p (a x) d", p=P)).then_inc(x_in, 16)
            norm_root("mix0")
            for b in range(16):
                take("even_qk", b, qk1[:, b, :], ACT.Copy)
            act.wait_ge(w_used, BASE["even_vg"] + 8)
            for n, dst in enumerate((v_moba, v_ret)):
                for x in range(NX):
                    mv = act.activation(dst[:, x, :], acc[:, 2 * n + x, :], ACT.Copy)
            mv.then_inc(acc_out, 1)
            act.wait_ge(w_used, BASE["even_vg"] + 12)
            for x in range(NX):
                mv = act.activation(g_ret[:, x, :], acc[:, x, :], ACT.Silu)
            mv.then_inc(acc_out, 1)
            soft(0, sc1)
            root("ret", st[:, 56:64], st[:, 48:56])

            def peer(layer):
                norm_root(f"ffn{layer}")
                for b in range(16):
                    take(f"peer_q{layer}", b, peer_qT[:, b, :], ACT.Copy)
                ub, fb = BASE[f"peer_u{layer}"], FMBASE[f"peer_u{layer}"]

                def hidden(i):
                    for j in range(RING):
                        act.wait_ge(w_used, ub + j + 1 + RING * i)
                        act.activation(hid[:, RING * i + j, :], prod[:, (fb + j) % 2, 0:T], ACT.Gelu).then_inc(fm_out, 1)

                early = 12
                with act.Fori(0, early) as i:
                    hidden(i)
                act.wait_ge(topk_ready, layer + 1)
                act.activation(sel_i[:, 2, :, :], sel_i[:, 2, :, :], ACT.Exp).then_inc(gate_exp, 1)
                with act.Fori(early, NK // RING) as i:
                    hidden(i)
                act.wait_ge(w_used, BASE[f"peer_v{layer}"] + NK)
                for n in range(4):
                    mv = act.activation(peer_yT[:, 2 * n:2 * n + 2, :].rearrange("p a b -> p (a b)"), acc[:, n, :], ACT.Copy)
                mv.then_inc(acc_out, 1)

            peer(0)
            norm_root("mix1")
            for b in range(24):
                take("odd_in", b, (cv_b, cv_c, cv_h)[b % 3][:, b // 3, :], ACT.Copy)
            peer(1)
            norm_root("final")
            norm_root("ln_in")
            for b in range(8):
                take("qk2", b, qk2[:, b, :], ACT.Copy)
            act.wait_ge(w_used, BASE["v2"] + 4)
            for x in range(NX):
                mv = act.activation(v2[:, x, :], acc[:, x, :], ACT.Copy)
            mv.then_inc(acc_out, 1)
            soft(4, sc2)
            for b in range(RW_TILES):
                take("rw2", b, cols[:, b, 1:T + 1], ACT.Copy)
            soft(8, sc2)
            for b in range(16):
                take("gate2", b, gates2[:, b, :], ACT.Sigmoid)
            act.wait_ge(shifted, 1)
            act.activation(low[0:64, 0, :], low[0:64, 0, :], ACT.Tanh).then_inc(low_act, 1)
            act.activation(low[:, 1:3, :], low[:, 1:3, :], ACT.Sigmoid).then_inc(low_act, 1)
            for n in range(6):
                act.wait_ge(lora_mm, n + 1)
                for j in range(2):
                    f = 2 * (n % 2) + j
                    src = prod[:, n % 2, j * T:(j + 1) * T]
                    if n < 4:
                        dst, base = ((e2, vcol("decay", f)), (aa_fm, vcol("aaa", f)))[n // 2]
                        mv = act.activation(dst[:, f, :], src, ACT.Sigmoid, bias=base)
                    else:
                        mv = act.activation(g_fm[:, f, :], src, ACT.Copy)
                mv.then_inc(lora_out, 1)
            root("kk", e1, e1)
            act.wait_ge(logw_ready, 1)
            act.activation(a_til, a_til, ACT.Exp)
            act.activation(r_til, cum, ACT.Exp)
            act.activation(b_til, cum, ACT.Exp, scale=-1.0)
            act.activation(bh_fm, bh_fm, ACT.Exp).then_inc(exp_ready, 1)
            root("gn", y_rs, y_rs)
            norm_root("ln0")
            act.wait_ge(max_ready, 1)
            for x in range(NX):
                act.activation(g8m[:, x, 0:4], logit[:, x, 0:4], ACT.Exp, bias=st[:, 104 + x:105 + x],
                               accum_out=st[:, 106 + x:107 + x])
            act.activation(st[:, 112:114], st[:, 110:112], ACT.Exp).then_inc(moe_exp, 1)
            eb = BASE["moe"]

            def silu(e, later):
                first = eb if e == 0 else eb + 4 + 6 * (e - 1)
                act.wait_ge(w_used, first + 2 + later)
                act.activation(h_sig[:, e % 2, :], prod[:, 0, :], ACT.Silu).then_inc(silu_ready, 1)

            silu(0, 0)
            silu(1, 0)
            with act.Fori(0, (NEXP - 2) // 2) as i:
                for j in range(2):
                    silu(2 + j, 12 * i)
            act.wait_ge(w_used, BASE["ple_proj"] + 2)
            for n in range(4):
                mv = act.activation(ple[:, n // 2, (n % 2) * 512:(n % 2 + 1) * 512], acc[:, n, :], ACT.Copy)
            mv.then_inc(acc_out, 1)
            norm_root("ln1")
            act.wait_ge(w_used, BASE["ple_gate"] + 8)
            for n in range(4):
                mv = act.activation(sig_ple[:, n // 2, (n % 2) * 512:(n % 2 + 1) * 512], acc[:, n, :], ACT.Sigmoid)
            mv.then_inc(ple_sig, 1)
            norm_root("ln2")

        @block.vector
        def _(dve):
            chain = [0]
            taken = [0]

            def link(ins):
                chain[0] += 1
                ins.then_inc(v_chain, 1)
                dve.wait_ge(v_chain, chain[0])

            def group():
                dve.wait_ge(gen_mm, taken[0] + 1)
                taken[0] += 1
                return gen[:, (taken[0] - 1) % 2, :]

            def wide(ap, axis, n):
                shape = list(ap.shape)
                shape.insert(axis, n)
                return ap.unsqueeze(axis).broadcast_to(shape)

            def rstd(name):
                dve.wait_ge(root_ready, ROOT[name])
                link(dve.reciprocal(st[:, 6:8], st[:, 4:6]))

            def mean_square(eps):
                for x in range(NX):
                    link(dve.tensor_tensor_reduce(ln_sq, resid[:, x, :], resid[:, x, :], 1.0, 0.0, ALU.mult, ALU.add,
                                                  st[:, x:x + 1]))
                dve.tensor_scalar(st[:, 2:4], st[:, 0:2], 1.0 / D, eps, ALU.mult, ALU.add).then_inc(ms_ready, 1)

            def rms_norm(name):
                mean_square(EPS)
                rstd(name)
                for x in range(NX):
                    last = dve.tensor_scalar(xn[:, x, :], resid[:, x, :], st[:, 6 + x:7 + x], None, ALU.mult)
                last.then_inc(normed, 1)

            def layer_norm(name, pair, arrived, out_sem):
                link(dve.tensor_reduce(st[:, 8:10], resid[:, :, :], AX, ALU.add))
                link(dve.tensor_scalar(st[:, 10:12], st[:, 8:10], -1.0 / D, None, ALU.mult))
                for x in range(NX):
                    c = dve.tensor_scalar(resid[:, x, :], resid[:, x, :], st[:, 10 + x:11 + x], None, ALU.add)
                link(c)
                mean_square(LN_EPS)
                rstd(name)
                dve.wait_ge(gain_in[pair], arrived)
                for x in range(NX):
                    c = dve.scalar_tensor_tensor(resid[:, x, :], resid[:, x, :], st[:, 6 + x:7 + x], gains[:, pair, 0, :],
                                                 ALU.mult, ALU.mult)
                link(c)
                link(dve.tensor_tensor(resid[:, :, :], resid[:, :, :], wide(gains[:, pair, 1, :], 1, NX), ALU.add))
                dve.sem_inc(gain_used, 1)
                dve.sem_inc(out_sem, 1)

            def take_fm(dst, tiles, gain=None):
                for x in range(NX):
                    for q in range(tiles // 4):
                        bank = group().rearrange("p (a b) -> p a b", b=P)
                        out_ = dst[:, 4 * q:4 * q + 4, x * P:(x + 1) * P]
                        if gain is None:
                            c = dve.tensor_copy(out_, bank)
                        else:
                            c = dve.tensor_tensor(out_, bank, wide(vcol(gain, 4 * q, 4), 2, P), ALU.mult)
                        link2(c)
                dve.sem_inc(fm_ready, 1)

            def link2(ins):
                ins.then_inc(gen_out, 1)
                dve.wait_ge(gen_out, taken[0])

            def add_acc(scale):
                for x in range(NX):
                    c = dve.scalar_tensor_tensor(resid[:, x, :], resid[:, x, :], scale,
                                                 acc[:, 2 * x:2 * x + 2, :].rearrange("p a b -> p (a b)"), ALU.mult, ALU.add)
                c.then_inc(acc_out, 1)
                dve.wait_ge(acc_out, acc_uses[0])

            acc_uses = [0]

            dve.wait_ge(small_in, 80)
            dve.wait_ge(x_in, 16)
            rms_norm("mix0")
            take_fm(xT, KD, "mix0")
            dve.wait_ge(table_b_in, 16)
            for n in range(8):
                dve.wait_ge(fm_out, 2 * n + 2)
                pair = qk1[:, 2 * n:2 * n + 2, :]
                bank = group().rearrange("p (a b) -> p a b", b=T)
                dve.tensor_tensor(rope_tmp, bank, wide(cb("sin"), 1, 2), ALU.mult).then_inc(gen_out, 1)
                link(dve.tensor_tensor(pair, pair, wide(cb("cos"), 1, 2), ALU.mult))
                dve.tensor_tensor(pair, pair, rope_tmp, ALU.add).then_inc(roped, 1)
                dve.wait_ge(roped, n + 1)

            def soft(scores, s, scale, bias_of, mask_band):
                for h in range(4):
                    dve.wait_ge(att_s, scores + h + 1)
                    link(dve.scalar_tensor_tensor(s[:, h, :], acc[:, h, 0:ATT_COLS], scale, bias_of(h), ALU.mult, ALU.add))
                    if h == 3:
                        dve.sem_inc(acc_out, 1)
                    if mask_band:
                        dve.memset(s[0:64, h, 64:P], NEG)
                        link(dve.memset(s[0:64, h, 2 * P + 64:3 * P], NEG))
                    dve.tensor_reduce(st[:, 32 + h:33 + h], s[:, h, 0:P], AX, ALU.max)
                    link(dve.tensor_reduce(st[:, 36 + h:37 + h], s[:, h, P:ATT_COLS], AX, ALU.max))
                    dve.tensor_scalar(st[:, 16 + h:24:4], st[:, 32 + h:40:4], -1.0, None, ALU.mult).then_inc(att_m, 1)

            def probs_T(pT):
                for h in range(4):
                    bank = group()
                    link2(dve.tensor_copy(pT[:, h, :], bank[:, 0:ATT_COLS]))
                    dve.sem_inc(att_pt, 1)

            def take_heads(n, soft_count, dst, width):
                dve.wait_ge(att_p, soft_count)
                link(dve.reciprocal(st[:, 32:40], st[:, 24:32]))
                dve.wait_ge(att_o, n)
                for x in range(NX):
                    c = dve.tensor_tensor(dst(x).rearrange("p (a b) -> p a b", b=width),
                                          prod[:, x, 0:4 * width].rearrange("p (a b) -> p a b", b=width),
                                          wide(st[:, 32 + 4 * x:36 + 4 * x], 2, width), ALU.mult)
                c.then_inc(att_done, 1)

            soft(0, sc1, HD1 ** -0.5, lambda h: cb("causal"), False)
            probs_T(pT1)
            take_heads(1, 4, lambda x: cat1[:, x, 0:512], HD1)
            for h in range(4):
                dve.wait_ge(att_s, 5 + h)
                c = dve.tensor_tensor(rT1[:, h, :], acc[:, h, 0:ATT_COLS],
                                      cb("decay")[:, h * ATT_COLS:(h + 1) * ATT_COLS], ALU.mult)
                c.then_inc(att_pt, 1)
            dve.wait_ge(att_pt, 8)
            dve.sem_inc(acc_out, 1)
            dve.wait_ge(att_o, 2)
            for x in range(NX):
                c = dve.tensor_copy(cat1[:, x, 512:D], prod[:, x, :])
            c.then_inc(att_done, 1)
            dve.wait_ge(att_done, 2)
            ret = cat1[:, :, 512:D]
            link(dve.tensor_tensor(ret_sq, ret, ret, ALU.mult))
            for x in range(NX):
                c = dve.tensor_reduce(st[:, 40 + 4 * x:44 + 4 * x], ret_sq[:, x, :].rearrange("p (a b) -> p a b", b=HD1),
                                      AX, ALU.add)
            link(c)
            dve.tensor_scalar(st[:, 48:56], st[:, 40:48], 1.0 / HD1, EPS, ALU.mult, ALU.add).then_inc(ms_ready, 1)
            dve.wait_ge(root_ready, ROOT["ret"])
            link(dve.reciprocal(st[:, 64:72], st[:, 56:64]))
            for x in range(NX):
                v = cat1[:, x, 512:D].rearrange("p (a b) -> p a b", b=HD1)
                c = dve.tensor_tensor(v, v, wide(st[:, 64 + 4 * x:68 + 4 * x], 2, HD1), ALU.mult)
            link(c)
            dve.wait_ge(acc_out, 2)
            dve.tensor_tensor(ret, ret, g_ret, ALU.mult).then_inc(normed, 1)
            take_fm(xT, KD)
            dve.wait_ge(w_used, BASE["even_out"] + 8)
            acc_uses[0] = 5
            add_acc(1.0)

            def top16(vals, idx, src, n):
                for r in range(2):
                    lo = slice(8 * r, 8 * r + 8)
                    for m in range(n):
                        c = dve.max(vals(m)[:, lo], src(m))
                    link(c)
                    for m in range(n):
                        c = dve.max_index(idx(m)[:, lo], vals(m)[:, lo], src(m))
                    if r == 0:
                        for m in range(n):
                            c = dve.match_replace(src(m), vals(m)[:, lo], src(m), -3.0e38)
                    link(c)

            def route(x):
                top16(lambda m: top_s[:, m, :], lambda m: top_u[:, m, :].bitcast(U32), lambda m: score[:, x, m, :], 16)
                dve.tensor_copy(top_f, top_u.bitcast(U32))
                c4 = cand.rearrange("p h (a b) -> p h a b", b=TOPK)
                link(dve.tensor_tensor(c4, wide(top_s[:, 0::2, :], 3, TOPK), wide(top_s[:, 1::2, :], 2, TOPK), ALU.add))
                top16(lambda m: sel_s[:, x, m, :], lambda m: pos_u[:, m, :].bitcast(U32), lambda m: cand[:, m, :], PEER_H)
                for n, (op, by) in enumerate(((ALU.logical_shift_right, 4), (ALU.bitwise_and, TOPK - 1))):
                    link(dve.tensor_scalar(pos_a.bitcast(U32), pos_u.bitcast(U32), by, None, op))
                    link(dve.tensor_copy(pos_f, pos_a.bitcast(U32)))
                    flat = pos_f.rearrange("p h k -> p (h k)")
                    link(dve.tensor_tensor(pick, wide(iota[:, 0:TOPK], 1, P), wide(flat, 2, TOPK), ALU.is_equal))
                    p4 = pick.rearrange("p (h k) a -> p h k a", k=TOPK)
                    link(dve.tensor_tensor(p4, p4, wide(top_f[:, n::2, :], 2, TOPK), ALU.mult))
                    link(dve.tensor_reduce(sel_i[:, n, x, :], pick, AX, ALU.add))
                g = sel_i[:, 2, x, :].rearrange("p (h k) -> p h k", k=TOPK)
                return dve.tensor_tensor(g, sel_s[:, x, :, :], wide(sel_s[:, x, :, 0], 2, TOPK), ALU.subtract)

            def peer(layer):
                rms_norm(f"ffn{layer}")
                take_fm(xT, KD, f"ffn{layer}")
                for b in range(2):
                    for x in range(NX):
                        for q in range(2):
                            bank = group().rearrange("p (a b) -> p a b", b=NK)
                            link2(dve.tensor_copy(score[:, x, 8 * b + 4 * q:8 * b + 4 * q + 4, :], bank))
                for x in range(NX):
                    last = route(x)
                last.then_inc(topk_ready, 1)
                dve.wait_ge(gate_exp, layer + 1)
                gate = sel_i[:, 2, :, :].rearrange("p x (h k) -> p (x h) k", k=TOPK)
                link(dve.tensor_reduce(st[:, 16:32], gate, AX, ALU.add))
                link(dve.reciprocal(st[:, 32:48], st[:, 16:32]))
                dve.tensor_tensor(gate, gate, wide(st[:, 32:48], 2, TOPK), ALU.mult).then_inc(normed, 1)
                for x in range(NX):
                    bank = group()
                    link2(dve.tensor_copy(hk[:, :, x * P:(x + 1) * P],
                                          bank[:, 0:3 * P].rearrange("p (a b) -> p a b", b=P)))
                tb = 2 * layer * HALF
                for half in range(2):
                    dve.wait_ge(fm_out, FMBASE[f"peer_u{layer}"] + (half + 1) * HALF)
                    before, chained = tb + half * HALF, chain[0]
                    with dve.Fori(0, HALF) as n:
                        tok = bass.ds(GTOK * n, GTOK)
                        dve.tensor_tensor(hot1[:, :, :], wide(iota, 1, GTOK), wide(hk[:, 0, tok], 2, NK), ALU.is_equal)
                        dve.tensor_tensor(hot2[:, :, :], wide(iota[:, half * HALF:(half + 1) * HALF], 1, GTOK),
                                          wide(hk[:, 1, tok], 2, HALF), ALU.is_equal).then_inc(v_chain, 1)
                        dve.wait_ge(v_chain, chained + 1 + n)
                        dve.tensor_tensor(hot2[:, :, :], hot2[:, :, :], wide(hk[:, 2, tok], 2, HALF), ALU.mult)\
                            .then_inc(hot_ready, 1)
                        dve.wait_ge(tok_mm, before + 1 + n)
                        h = hid[:, half * HALF:(half + 1) * HALF, tok]
                        dve.tensor_tensor(h, h, gen[:, 0, 0:GTOK * HALF].rearrange("p (t c) -> p c t", c=HALF), ALU.mult)\
                            .then_inc(gated, 1)
                    chain[0] += HALF
                for x in range(NX):
                    for q in range(2):
                        bank = group()
                        r = resid[:, x, 512 * q:512 * q + 512]
                        link2(dve.tensor_tensor(r, r, bank, ALU.add))

            peer(0)
            rms_norm("mix1")
            take_fm(xT, KD, "mix1")
            dve.memset(cv_u[:, :, 0:2], 0.0)
            for k in range(KD):
                dve.wait_ge(fm_out, FMBASE["odd_in"] + 3 * k + 3)
                link(dve.tensor_tensor(cv_u[:, k, 2:T + 2], cv_c[:, k, :], cv_h[:, k, :], ALU.mult))
                link(dve.tensor_scalar(cv_y[:, k, :], cv_u[:, k, 0:T], vcol("conv", k), None, ALU.mult))
                for w in (1, 2):
                    link(dve.scalar_tensor_tensor(cv_y[:, k, :], cv_u[:, k, w:w + T], vcol("conv", 8 * w + k),
                                                  cv_y[:, k, :], ALU.mult, ALU.add))
                c = dve.tensor_tensor(cv_z[:, k, :], cv_b[:, k, :], cv_y[:, k, :], ALU.mult)
            c.then_inc(fm_ready, 1)
            dve.wait_ge(w_used, BASE["odd_out"] + 8)
            acc_uses[0] = 7
            add_acc(1.0)
            peer(1)
            dve.sem_inc(arena_free, 1)
            mean_square(EPS)
            rstd("final")
            dve.wait_ge(gain_in[0], 16)
            for x in range(NX):
                c = dve.scalar_tensor_tensor(resid[:, x, :], resid[:, x, :], st[:, 6 + x:7 + x], gains[:, 0, 0, :],
                                             ALU.mult, ALU.mult)
            c.then_inc(gain_used, 1)
            dve.wait_ge(gain_used, 1)
            layer_norm("ln_in", 1, 32, normed)
            take_fm(xT, KD)
            dve.wait_ge(block2_in, 32)
            soft(8, sc2, HD2 ** -0.5, lambda h: band_bias[:, h, :], True)
            link(dve.memset(cols[:, :, 0:1], 0.0))
            dve.wait_ge(fm_out, FMBASE["gate2"])
            dve.tensor_tensor(rkv, cols[:, 0:12, 0:T], cols[:, 0:12, 1:T + 1], ALU.subtract)
            link(dve.tensor_tensor(low, cols[:, 12:15, 0:T], cols[:, 12:15, 1:T + 1], ALU.subtract))
            for n in range(RW_TILES):
                v = rkv[:, n, :] if n < 12 else low[:, n - 12, :]
                c = dve.scalar_tensor_tensor(v, v, vcol("mu", n), cols[:, n, 1:T + 1], ALU.mult, ALU.add)
            link(c)
            dve.sem_inc(shifted, 1)
            probs_T(pT2)
            take_heads(3, 8, lambda x: ob2[:, x, 0:256], HD2)
            soft(12, sc2, HD2 ** -0.5, lambda h: band_bias[:, 4 + h, :], True)
            probs_T(pT2)
            take_heads(4, 12, lambda x: ob2[:, x, 256:512], HD2)
            dve.wait_ge(att_done, 4)
            dve.sem_inc(normed, 1)
            take_fm(ya_fm, 4)
            for pr in range(4):
                c = dve.tensor_scalar(kk_fm[:, pr, :], k_fm[:, pr, :], vcol("k_k", pr), None, ALU.mult)
            link(c)
            dve.tensor_tensor(e1, kk_fm, kk_fm, ALU.mult).then_inc(sq_ready, 1)
            for q in range(2):
                bank = group().rearrange("p (a b) -> p a b", b=T)
                link2(dve.tensor_scalar(e1[:, 2 * q:2 * q + 2, :], bank, 1e-24, None, ALU.max))
            dve.sem_inc(ms_ready, 1)
            dve.wait_ge(root_ready, ROOT["kk"])
            link(dve.reciprocal(e1, e1))
            link(dve.tensor_tensor(kk_fm, kk_fm, e1, ALU.mult))
            dve.wait_ge(lora_out, 6)
            for pr in range(4):
                c = dve.tensor_scalar(e1[:, pr, :], aa_fm[:, pr, :], -1.0, vcol("k_a", pr), ALU.add, ALU.mult)
            link(c)
            link(dve.scalar_tensor_tensor(k_fm, e1, 1.0, k_fm, ALU.add, ALU.mult))
            link(dve.tensor_scalar(e1, e2, -float(np.exp(-0.5)), None, ALU.mult))
            for pr in range(4):
                c = dve.tensor_tensor_scan(cum[:, pr, :], cc("start"), e1[:, pr, :], 0.0, ALU.mult, ALU.add)
            link(c)
            dve.tensor_tensor(a_til, cum, e1, ALU.subtract)
            for pr in range(4):
                cpr = cum[:, pr, :].rearrange("p (c t) -> p c t", t=CH)
                c = dve.tensor_tensor(bh_fm[:, pr, :].rearrange("p (c t) -> p c t", t=CH),
                                      wide(cpr[:, :, CH - 1], 2, CH), cpr, ALU.subtract)
            c.then_inc(logw_ready, 1)
            dve.wait_ge(exp_ready, 1)
            for pr in range(4):
                c = dve.tensor_copy(st[:, 72 + NCH * pr:72 + NCH * (pr + 1)], r_til[:, pr, CH - 1::CH])
            link(c)
            dve.scalar_tensor_tensor(a_til, a_til, -1.0, kk_fm, ALU.mult, ALU.mult)
            link(dve.tensor_tensor(kk_fm, kk_fm, aa_fm, ALU.mult))
            dve.tensor_tensor(k_til, b_til, k_fm, ALU.mult)
            dve.tensor_tensor(kh_fm, bh_fm, k_fm, ALU.mult)
            dve.tensor_tensor(b_til, b_til, kk_fm, ALU.mult)
            dve.tensor_tensor(bh_fm, bh_fm, kk_fm, ALU.mult)
            link(dve.tensor_tensor(r_til, r_til, r_fm, ALU.mult))
            dve.sem_inc(fm_ready, 1)
            for x in range(NX):
                for dst in (a_tm, bh_tm, kh_tm, v_tm):
                    bank = group()
                    link2(dve.tensor_copy(dst[:, x, :], bank))
            m_lT, m_l, m_ak, m_rb, m_rk, m_off, m_a, m_b = mats

            def masked(dst, mask, also=None):
                for q in range(2):
                    bank = group().rearrange("p (a b) -> p a b", b=P)
                    if also is not None:
                        dve.tensor_tensor(also[0][:, q::2, :], bank, wide(cc(also[1]), 1, 4), ALU.mult)
                    link2(dve.tensor_tensor(dst[:, q::2, :], bank, wide(cc(mask), 1, 4), ALU.mult))

            def stored(dst, plus=None):
                for q in range(2):
                    bank = group().rearrange("p (a b) -> p a b", b=P)
                    d = dst[:, 4 * q:4 * q + 4, :]
                    if plus is None:
                        link2(dve.tensor_copy(d, bank))
                    else:
                        link2(dve.tensor_tensor(d, plus[:, 4 * q:4 * q + 4, :], bank, ALU.add))

            for x in range(NX):
                masked(m_lT, "up16", (m_off, "off32"))
                masked(m_l, "low16")
                masked(m_ak, "up32")
                masked(m_rb, "upi32")
                masked(m_rk, "upi32")
                bank = group()
                dve.tensor_copy(sol[:, :, 0:HD2], a_tm[:, x, :].rearrange("p (a b) -> p a b", b=HD2))
                dve.tensor_tensor(m_ak, m_lT, wide(ident, 1, 8), ALU.add)
                link2(dve.tensor_copy(sol[:, :, HD2:P], bank.rearrange("p (a b) -> p a b", b=HD2)))
                stored(m_a)
                stored(m_b)
                stored(m_ak, m_ak)
                stored(m_l)
                stored(m_lT)
                stored(m_ak, m_ak)
                stored(m_a)
                stored(m_ak, m_ak)
                stored(m_b)
                stored(m_lT)
                stored(sol, m_b)
                tx = slice(x * P, (x + 1) * P)
                bank = group().rearrange("p (a b) -> p a b", b=P)
                link2(dve.tensor_tensor(q_eff[:, :, tx], bank, r_til[:, :, tx], ALU.add))
                bank = group().rearrange("p (a b) -> p a b", b=P)
                link2(dve.tensor_copy(y_fm[:, :, tx], bank))
                cs = slice(4 * x, 4 * x + 4)
                for pr in range(4):
                    c = dve.tensor_tensor(step_m[:, pr, cs, :], wide(cc("eye64"), 1, 4),
                                          wide(st[:, 72 + NCH * pr + 4 * x:76 + NCH * pr + 4 * x], 2, HD2), ALU.mult)
                link(c)
                for c in range(4 * x, 4 * x + 4):
                    bank = group().rearrange("p (n a b) -> p n a b", n=2, b=HD2)
                    dve.tensor_tensor(step_m[:, :, c, :], step_m[:, :, c, :], bank[:, 0], ALU.add)
                    link2(dve.tensor_copy(step_n[:, :, c, :], bank[:, 1]))
            dve.tensor_copy(state[:, 1, :, :], step_n[:, :, 0, :]).then_inc(state_ready, 1)
            for c in range(1, NCH - 1):
                bank = group()[:, 0:4 * HD2].rearrange("p (a b) -> p a b", b=HD2)
                link2(dve.tensor_tensor(state[:, c + 1, :, :], step_n[:, :, c, :], bank, ALU.add))
                dve.sem_inc(state_ready, 1)
            for q in range(2):
                bank = group().rearrange("p (a b) -> p a b", b=T)
                d = y_fm[:, 2 * q:2 * q + 2, CH:T]
                link2(dve.tensor_tensor(d, d, bank[:, :, CH:T], ALU.add))
            dve.sem_inc(sq_ready, 1)
            for q in range(2):
                bank = group().rearrange("p (a b) -> p a b", b=T)
                link2(dve.scalar_tensor_tensor(y_tmp[:, 2 * q:2 * q + 2, :], bank, -1.0 / HD2, y_fm[:, 2 * q:2 * q + 2, :],
                                               ALU.mult, ALU.add))
            dve.tensor_tensor(y_sq, y_tmp, y_tmp, ALU.mult).then_inc(sq_ready, 1)
            for pr in range(4):
                c = dve.scalar_tensor_tensor(bonus[:, pr, :], r_fm[:, pr, :], vcol("r_k", pr), k_fm[:, pr, :],
                                             ALU.mult, ALU.mult)
            for q in range(2):
                bank = group().rearrange("p (a b) -> p a b", b=T)
                link2(dve.tensor_scalar(y_rs[:, 2 * q:2 * q + 2, :], bank, 1.0 / HD2, GN_EPS, ALU.mult, ALU.add))
            dve.sem_inc(sq_ready, 1)
            dve.sem_inc(ms_ready, 1)
            for q in range(2):
                bank = group().rearrange("p (a b) -> p a b", b=T)
                h = slice(2 * q, 2 * q + 2)
                link2(dve.tensor_tensor(y_mu[:, h, :], bank, v_fm[:, h, :], ALU.mult))
            dve.wait_ge(root_ready, ROOT["gn"])
            link(dve.reciprocal(y_rs, y_rs))
            link(dve.tensor_tensor(y_tmp, y_tmp, y_rs, ALU.mult))
            for pr in range(4):
                c = dve.tensor_scalar(y_tmp[:, pr, :], y_tmp[:, pr, :], vcol("gn_g", pr), vcol("gn_b", pr), ALU.mult, ALU.add)
            link(c)
            link(dve.tensor_tensor(y_tmp, y_tmp, y_mu, ALU.add))
            dve.tensor_tensor(y_out, y_tmp, g_fm, ALU.mult).then_inc(fm_ready, 1)
            for j in range(4):
                h = slice(2 * j, 2 * j + 2)
                for n, dst in enumerate((mixT[:, h, :], mix_tmp)):
                    dve.wait_ge(w_used, BASE["branch"] + 2 * j + n + 1)
                    c = dve.tensor_tensor(dst, gates2[:, 8 * n + 2 * j:8 * n + 2 * j + 2, :],
                                          prod[:, n, :].rearrange("p (a b) -> p a b", b=T), ALU.mult)
                c.then_inc(branch_out, 1)
                dve.wait_ge(branch_out, j + 1)
                link(dve.tensor_tensor(mixT[:, h, :], mixT[:, h, :], mix_tmp, ALU.add))
            dve.sem_inc(fm_ready, 1)
            dve.wait_ge(w_used, BASE["out2"] + 8)
            acc_uses[0] = 12
            add_acc(ALPHA)
            layer_norm("ln0", 0, 48, normed)
            take_fm(xT, KD)
            bank = group()[:, 0:NX * 36].rearrange("p (a b) -> p a b", b=36)
            link2(dve.tensor_tensor(logit, bank, wide(router_b[:, :], 1, NX), ALU.add))
            link(dve.memset(g8, -3.0e38))
            link(dve.tensor_copy(g8[:, :, 0:4], logit[:, :, 0:4]))
            for x in range(NX):
                c = dve.max(sel8m[:, x, :], g8[:, x, :])
            link(c)
            for x in range(NX):
                c = dve.max_index(g8i[:, x, :].bitcast(U32), sel8m[:, x, :], g8[:, x, :])
            link(c)
            dve.tensor_scalar(st[:, 104:106], sel8m[:, :, 0], -1.0, None, ALU.mult)
            link(dve.tensor_copy(sel8f, g8i.bitcast(U32)))
            for x in range(NX):
                c = dve.tensor_scalar(hot_g[:, x, :], cc("iota8"), sel8f[:, x, 0:1], None, ALU.is_equal)
            link(c)
            elog = logit[:, :, 4:36].rearrange("p x (g e) -> p x e g", e=8)
            for x in range(NX):
                c = dve.tensor_tensor(sel_t[:, x, :, :], elog[:, x, :, :], wide(hot_g[:, x, 0:4], 1, 8), ALU.mult)
            link(c)
            link(dve.tensor_reduce(sel8, sel_t, AX, ALU.add))
            for x in range(NX):
                c = dve.max(sel8m[:, x, :], sel8[:, x, :])
            link(c)
            for x in range(NX):
                c = dve.max_index(sel8i[:, x, :].bitcast(U32), sel8m[:, x, :], sel8[:, x, :])
            link(c)
            dve.tensor_copy(sel8f, sel8i.bitcast(U32))
            link(dve.tensor_tensor(st[:, 110:112], sel8m[:, :, 1], sel8m[:, :, 0], ALU.subtract))
            dve.sem_inc(max_ready, 1)
            dve.wait_ge(moe_exp, 1)
            link(dve.tensor_scalar(st[:, 118:120], st[:, 112:114], 1.0, None, ALU.add))
            link(dve.tensor_tensor(st[:, 118:120], st[:, 118:120], st[:, 106:108], ALU.mult))
            link(dve.reciprocal(st[:, 114:116], st[:, 118:120]))
            link(dve.tensor_tensor(st[:, 116:118], st[:, 114:116], st[:, 112:114], ALU.mult))
            for x in range(NX):
                dve.tensor_scalar(comb8[:, x, :], cc("iota8"), sel8f[:, x, 0:1], st[:, 114 + x:115 + x],
                                  ALU.is_equal, ALU.mult)
                c = dve.tensor_scalar(comb8b[:, x, :], cc("iota8"), sel8f[:, x, 1:2], st[:, 116 + x:117 + x],
                                      ALU.is_equal, ALU.mult)
            link(c)
            link(dve.tensor_tensor(comb8, comb8, comb8b, ALU.add))
            for x in range(NX):
                c = dve.tensor_tensor(comb[:, x, :].rearrange("p (g e) -> p g e", e=8), wide(comb8[:, x, :], 1, 4),
                                      wide(hot_g[:, x, 0:4], 2, 8), ALU.mult)
            c.then_inc(normed, 1)
            bank = group()
            link2(dve.tensor_copy(combT[0:NEXP, :], bank[0:NEXP, 0:T]))
            dve.tensor_tensor(comb_d[0:NEXP, :, :], wide(combT[0:NEXP, :], 1, NEXP), wide(ident[0:NEXP, 0:NEXP], 2, T),
                              ALU.mult).then_inc(fm_ready, 1)
            eb = BASE["moe"]

            def weigh(e, later, elater, chained):
                first = eb if e == 0 else eb + 4 + 6 * (e - 1)
                mid = h_mid[:, e % 2, :]
                dve.wait_ge(silu_ready, e + 1 + elater)
                dve.wait_ge(w_used, first + 4 + later)
                dve.tensor_tensor(mid, h_sig[:, e % 2, :], prod[:, 1, :], ALU.mult).then_inc(v_chain, 1)
                dve.wait_ge(v_chain, chained + 1 + e + elater)
                dve.wait_ge(comb_mm, e + 1 + elater)
                m2 = mid.rearrange("p (a b) -> p a b", b=T)
                dve.tensor_tensor(m2, m2, wide(gen[:, 0, 0:T], 1, 2), ALU.mult).then_inc(mid_ready, 1)

            chained = chain[0]
            weigh(0, 0, 0, chained)
            weigh(1, 0, 0, chained)
            with dve.Fori(0, (NEXP - 2) // 2) as i:
                for j in range(2):
                    weigh(2 + j, 12 * i, 2 * i, chained)
            chain[0] += NEXP
            dve.wait_ge(w_used, eb + 6 * NEXP)
            acc_uses[0] = 13
            add_acc(ALPHA)
            layer_norm("ln1", 1, 64, normed)
            take_fm(xT, KD)
            dve.wait_ge(acc_out, 14)
            dve.wait_ge(ple_sig, 1)
            link(dve.tensor_tensor(ple, ple, sig_ple, ALU.mult))
            link(dve.scalar_tensor_tensor(resid[:, :, :], resid[:, :, :], ALPHA, ple, ALU.mult, ALU.add))
            layer_norm("ln2", 0, 80, normed)


def _fm(w):
    n = w.shape[1] // P
    return w.reshape(KD, P, n, P).transpose(2, 1, 0, 3).reshape(n, P, BLK)


def _tm(w):
    k, n = w.shape[0] // (2 * P), w.shape[1] // 512
    return w.reshape(k, 2, P, n, 512).transpose(3, 0, 2, 1, 4).reshape(n * k, P, BLK)


def _col(v, tiles):
    return v.reshape(tiles, P).T


def _layout(i):
    a = {}
    w = i["even_w_in"][0]
    a["even_qk"] = _fm(np.concatenate([w[:, 0:1024], w[:, 1536:2560]], axis=1))
    a["even_vg"] = _tm(np.concatenate([w[:, 1024:1536], w[:, 2560:3584]], axis=1))
    a["even_out"] = _tm(i["even_w_out"][0])
    a["odd_in"] = _fm(i["odd_w_in"][0].reshape(D, 3, KD, P).transpose(0, 2, 1, 3).reshape(D, 3 * D))
    a["odd_out"] = _tm(i["odd_w_out"][0])
    for n in range(LAYERS):
        a[f"peer_q{n}"] = _fm(i["peer_w_q"][n])
        a[f"peer_keys{n}"] = i["peer_sub_keys"][n].reshape(2, 8, NK, P).transpose(0, 3, 1, 2).reshape(2, P, BLK)
        a[f"peer_u{n}"] = i["peer_u"][n].reshape(NK, NK, KD, P).transpose(1, 3, 2, 0).reshape(NK, P, BLK)
    a["peer_v"] = i["peer_v"]
    w = i["w_in_2"][0]
    a["qk2"] = _fm(w[:, 0:1024])
    a["v2"] = _tm(w[:, 1024:1536])
    a["rw2"] = _fm(np.pad(w[:, 1536:3360], ((0, 0), (0, RW_TILES * P - 1824))))
    a["gate2"] = _fm(w[:, 3360:])
    for name, key in (("branch_a", "w_branch_attn_2"), ("branch_r", "w_branch_rwkv_2")):
        a[name] = i[key][0].reshape(4, P, 4, 2, P).transpose(2, 1, 0, 3, 4).reshape(4, P, BLK)
    a["out2"] = _tm(i["w_out_2"][0])
    for name, key in (("exp_gate", "exp_gate_2"), ("exp_up", "exp_up_2")):
        a[name] = i[key][0].reshape(NEXP, KD, P, 2, P).transpose(0, 3, 2, 1, 4).reshape(2 * NEXP, P, BLK)
    a["exp_down"] = i["exp_down_2"][0].reshape(2 * NEXP, P, BLK)
    a["ple_proj"] = _tm(i["ple_proj_2"][0])
    a["ple_gate"] = _tm(i["ple_gate_2"][0])
    a["x"] = i["x"]
    a["const_a"], a["const_b"], a["const_c"] = constant_tables()
    vec = [_col(i["norm_mix"][0], 8), _col(i["norm_mix"][1], 8), _col(i["norm_ffn"][0], 8), _col(i["norm_ffn"][1], 8)]
    vec += [_col(i["odd_conv"][0][w], 8) for w in range(3)]
    vec += [_col(np.pad(i["tok_mix_2"][0], (0, RW_TILES * P - 1824)), RW_TILES)]
    vec += [_col(i[k][0].reshape(-1), 4) for k in ("decay_base_2", "aaa_base_2", "k_k_2", "k_a_2", "r_k_2", "gn_g_2", "gn_b_2")]
    a["vec"] = np.concatenate(vec, axis=1)
    a["final_norm"] = i["final_norm"]
    a["ln_in_g"], a["ln_in_b"] = i["ln_in_g_2"], i["ln_in_b_2"]
    a["ln_g"], a["ln_b"] = i["ln_g_2"][0], i["ln_b_2"][0]
    both = np.concatenate([i["router_grp_2"][0], i["router_exp_2"][0]], axis=1)
    a["router"] = both.reshape(KD, P, 36).transpose(1, 0, 2)
    a["router_b"] = np.concatenate([i["router_grp_bias_2"][0], i["router_exp_bias_2"][0]])
    lora = np.zeros((P, 3, 512), np.float32)
    lora[0:64, 0], lora[64:128, 0] = i["decay_up_2"][0], i["aaa_up_2"][0]
    lora[:, 1], lora[0:32, 2] = i["gate_up_2"][0][0:128], i["gate_up_2"][0][128:160]
    a["lora"] = lora
    pos = np.arange(T)
    place = np.clip(pos[:, None] - pos[None, :], -128, 128) + 128
    place = np.concatenate([place[0:P, 0:P], place[P:T, :]], axis=1)
    a["band_bias"] = i["rel_bias_2"][:, place].transpose(1, 0, 2)
    a["p"] = i["p_2"][0, 0].reshape(T, 2, P).transpose(2, 1, 0)
    return {k: np.ascontiguousarray(v) for k, v in a.items()}


def kernel(**inputs):
    from concourse.bacc import Bacc
    from concourse.bass_utils import run_bass_kernel_spmd

    arrays = _layout({k: np.asarray(v) for k, v in inputs.items()})
    nc = Bacc("TRN2", target_bir_lowering=False, num_devices=1)
    dram = {k: nc.dram_tensor(f"in_{k}", v.shape, mybir.dt.from_np(v.dtype), kind="ExternalInput").ap()
            for k, v in arrays.items()}
    out = nc.dram_tensor("out_x", (1, T, D), F32, kind="ExternalOutput").ap()
    build(nc, dram, out)
    r = run_bass_kernel_spmd(nc, [{f"in_{k}": v for k, v in arrays.items()}], core_ids=[0])
    return r.results[0]["out_x"]
```

```python
from contextlib import ExitStack

import numpy as np

import concourse.bass as bass
from concourse import mybir

ALU = mybir.AluOpType
ACT = mybir.ActivationFunctionType
F32 = mybir.dt.float32
F32R = mybir.dt.float32r
U32 = mybir.dt.uint32
AX = mybir.AxisListType.X

P = 128
T = 256
NX = T // P
D = 1024
KD = D // P
RING = 4
PAIR = 2
BLK = 1024
EPS = 1e-6
LN_EPS = 1e-5
GN_EPS = 64e-5
ALPHA = 2.0 ** 0.25
NEG = -1e30

LAYERS = 2
HEADS1 = 4
HD1 = 128
PEER_H = 8
NK = 128
TOPK = 16
HALF = NK // 2
GTOK = 4

HEADS2 = 8
HD2 = 64
RW_TILES = 15
CH = 32
NCH = T // CH
NEXP = 32
DEXP = 256
ATT_COLS = 3 * P

STREAM = [("even_qk", 16), ("even_vg", 12), ("even_out", 8)]
for _l in range(LAYERS):
    if _l == 1:
        STREAM += [("odd_in", 24), ("odd_out", 8)]
    STREAM += [(f"peer_q{_l}", 16), (f"peer_keys{_l}", 2), (f"peer_u{_l}", NK), (f"peer_v{_l}", NK)]
STREAM += [("qk2", 8), ("v2", 4), ("rw2", RW_TILES), ("gate2", 16), ("branch", 8), ("out2", 8),
           ("moe", 6 * NEXP), ("ple_proj", 2), ("ple_gate", 8)]
BASE, _n = {}, 0
for _name, _k in STREAM:
    BASE[_name] = _n
    _n += _k
FMBASE, _n = {}, 0
for _name, _k in STREAM:
    if _name in ("even_qk", "odd_in", "qk2", "rw2", "gate2") or _name[:6] in ("peer_q", "peer_u"):
        FMBASE[_name] = _n
        _n += _k
WHOLE = ("even_qk", "even_vg", "even_out", "odd_out", "peer_keys0", "peer_keys1", "qk2", "v2", "rw2", "branch", "out2",
         "ple_proj", "ple_gate")
SPLIT, SPLIT_BLOCKS = {}, []
for _name, _k in STREAM:
    if _name not in WHOLE:
        SPLIT[_name] = len(SPLIT_BLOCKS)
        SPLIT_BLOCKS += range(BASE[_name], BASE[_name] + _k)
SPLIT_PLACE = {g: s for s, g in enumerate(SPLIT_BLOCKS)}


def _order(*names):
    return {name: n + 1 for n, name in enumerate(names)}


NORMED = _order("mix0", "cat", "ffn0", "route0", "mix1", "ffn1", "route1", "blk2", "band", "ln0", "comb", "ln1", "ln2")
FM = _order("mix0", "cat", "ffn0", "mix1", "conv", "ffn1", "blk2", "band", "til", "rwkv", "mixed", "ln0", "comb", "ln1")
ROOT = _order("mix0", "ret", "ffn0", "mix1", "ffn1", "final", "ln_in", "kk", "gn", "ln0", "ln1", "ln2")

VEC, _n = {}, 0
for _name, _k in (("mix0", 8), ("mix1", 8), ("ffn0", 8), ("ffn1", 8), ("conv", 24), ("mu", RW_TILES), ("decay", 4),
                  ("aaa", 4), ("k_k", 4), ("k_a", 4), ("r_k", 4), ("gn_g", 4), ("gn_b", 4)):
    VEC[_name] = _n
    _n += _k
NVEC = _n

CA, CB, CC = {}, {}, {}
for _tab, _items in ((CA, (("ident", 128), ("iota", 128))),
                     (CB, (("rot", 128), ("cos", T), ("sin", T), ("causal", ATT_COLS), ("decay", HEADS1 * ATT_COLS))),
                     (CC, (("up16", 128), ("low16", 128), ("off32", 128), ("up32", 128), ("upi32", 128),
                           ("ones64", 128), ("eye64", 64), ("ones", 128), ("iota8", 8)))):
    _n = 0
    for _name, _k in _items:
        _tab[_name] = (_n, _k)
        _n += _k
    _tab["all"] = (0, _n)


def constant_tables():
    f = np.float32
    i = np.arange(P)
    a = np.zeros((P, CA["all"][1]), f)
    a[:, 0:128] = np.eye(P, dtype=f)
    a[:, 128:256] = np.arange(128, dtype=f)
    b = np.zeros((P, CB["all"][1]), f)

    def put(tab, arr, name, val):
        s, n = tab[name]
        arr[:, s:s + n] = val

    rot = np.zeros((P, P), f)
    rot[i[:64] + 64, i[:64]] = -1.0
    rot[i[:64], i[:64] + 64] = 1.0
    put(CB, b, "rot", rot)
    half = HD1 // 2
    inv = (f(10000.0) ** (-np.arange(half, dtype=f) / f(half))).astype(f)
    ang = (np.arange(T, dtype=f)[:, None] * inv[None, :]).astype(f)
    put(CB, b, "cos", np.cos(ang).astype(f).T[i % half])
    put(CB, b, "sin", np.sin(ang).astype(f).T[i % half])
    causal = np.zeros((P, 3, P), f)
    causal[:, 0] = causal[:, 2] = np.where(i[None, :] <= i[:, None], 0.0, NEG)
    put(CB, b, "causal", causal.reshape(P, -1))
    dec = np.zeros((P, HEADS1, 3, P))
    for h in range(HEADS1):
        lg = np.log(1.0 - 2.0 ** (-5.0 - h))
        diff = (i[None, :] - i[:, None]).astype(np.float64)
        dec[:, h, 0] = dec[:, h, 2] = np.where(diff >= 0, np.exp(lg * np.maximum(diff, 0)), 0.0)
        dec[:, h, 1] = np.exp(lg * (diff + P))
    put(CB, b, "decay", (dec * HD1 ** -0.5).astype(f).reshape(P, -1))
    c = np.zeros((P, CC["all"][1]), f)
    s, t = i[:, None], i[None, :]
    put(CC, c, "up16", (s // 16 == t // 16) & (s < t))
    put(CC, c, "low16", (s // 16 == t // 16) & (s > t))
    put(CC, c, "off32", (s // 32 == t // 32) & (s // 16 < t // 16))
    put(CC, c, "up32", (s // 32 == t // 32) & (s < t))
    put(CC, c, "upi32", (s // 32 == t // 32) & (s <= t))
    put(CC, c, "ones64", s // 64 == t // 64)
    put(CC, c, "eye64", i[:, None] % 64 == np.arange(64)[None, :])
    put(CC, c, "ones", 1.0)
    put(CC, c, "iota8", np.arange(8))
    return a, b, c


def build(nc, dram, out):
    with ExitStack() as ctx:
        def sb(name, cols, dt=F32):
            return ctx.enter_context(nc.sbuf_tensor(name, [P, cols], dt))

        def ps(name, banks):
            return ctx.enter_context(nc.psum_tensor(name, [P, banks, 512], F32))

        def sem(name):
            return ctx.enter_context(nc.semaphore(name))

        ring = ctx.enter_context(nc.sbuf_tensor("ring", [P, RING, BLK], F32))
        resid = ctx.enter_context(nc.sbuf_tensor("resid", [P, NX, D], F32))
        const_a = sb("const_a", CA["all"][1])
        vec = sb("vec", NVEC)
        gains = ctx.enter_context(nc.sbuf_tensor("gains", [P, 3, D], F32))
        whi = ctx.enter_context(nc.sbuf_tensor("whi", [P, PAIR, BLK], F32R))
        wlo = ctx.enter_context(nc.sbuf_tensor("wlo", [P, PAIR, BLK], F32R))
        xh = ctx.enter_context(nc.sbuf_tensor("xh", [P, KD, T], F32R))
        xl = ctx.enter_context(nc.sbuf_tensor("xl", [P, KD, T], F32R))
        hot1 = ctx.enter_context(nc.sbuf_tensor("hot1", [P, GTOK, NK], F32R))
        hot2 = ctx.enter_context(nc.sbuf_tensor("hot2", [P, 2, GTOK, HALF], F32R))
        hid_hi, hid_lo = xh[:, 0:RING, :], xl[:, 0:RING, :]
        mid_hi = hot1[:, :, :].rearrange("p a b -> p (a b)")
        mid_lo = hot2[:, :, :, :].rearrange("p n a b -> p (n a b)")
        aux = sb("aux", CC["all"][1] + KD * 36 + 36)
        hk = aux[:, 0:4 * T].rearrange("p (a b) -> p a b", b=T)
        const_c = aux[:, 0:CC["all"][1]]
        router = aux[:, CC["all"][1]:CC["all"][1] + KD * 36].rearrange("p (a b) -> p a b", b=36)
        router_b = aux[:, CC["all"][1] + KD * 36:]
        st = sb("st", 128)
        arena = sb("arena", NK * T)

        def at(off, *dims):
            n = int(np.prod(dims))
            assert off + n <= NK * T
            v = arena[:, off:off + n]
            if len(dims) == 2:
                v = v.rearrange("p (a b) -> p a b", b=dims[1])
            elif len(dims) == 3:
                v = v.rearrange("p (a b c) -> p a b c", b=dims[1], c=dims[2])
            return v

        def ca(name):
            return const_a[:, CA[name][0]:CA[name][0] + CA[name][1]]

        def cc(name):
            return const_c[:, CC[name][0]:CC[name][0] + CC[name][1]]

        def vcol(name, i, n=1):
            return vec[:, VEC[name] + i:VEC[name] + i + n]

        ident, iota = ca("ident"), ca("iota")
        xT = at(28800, KD, T)
        xT2 = at(18432, KD, T)
        const_b = at(0, CB["all"][1])

        def cb(name):
            return const_b[:, CB[name][0]:CB[name][0] + CB[name][1]]

        o = CB["all"][1]
        qk1 = at(o, 16, T); o += 16 * T
        v_moba = at(o, NX, 512); o += NX * 512
        v_ret = at(o, NX, 512); o += NX * 512
        g_ret = at(o, NX, 512); o += NX * 512
        sc1 = at(o, HEADS1, ATT_COLS); o += HEADS1 * ATT_COLS
        pT1 = at(o, HEADS1, ATT_COLS); o += HEADS1 * ATT_COLS
        rT1 = at(o, HEADS1, ATT_COLS); o += HEADS1 * ATT_COLS
        cat1 = at(o, NX, D); o += NX * D
        rope_tmp = at(o, 2, T); o += 2 * T
        xn = at(24576, NX, D)
        ret_sq = at(26624, NX, 512)
        hid = at(0, NK, T)
        peer_qT = at(16384, 16, T)
        score = at(20480, NX, 16, NK)
        o = 26624
        top_s = at(o, 16, TOPK); o += 256
        top_u = at(o, 16, TOPK); o += 256
        top_f = at(o, 16, TOPK); o += 256
        sel_s = at(o, NX, PEER_H, TOPK); o += 256
        pos_u = at(o, PEER_H, TOPK); o += 128
        pos_a = at(o, PEER_H, TOPK); o += 128
        pos_f = at(o, PEER_H, TOPK); o += 128
        sel_i = at(o, 3, NX, P); o += 3 * 256
        cand = at(o, PEER_H, TOPK * TOPK); o += 2048
        pick = at(24576, PEER_H * TOPK, TOPK)
        assert o <= NK * T
        peer_yT = at(0, KD, T)
        cv_b = at(0, KD, T)
        cv_c = at(2048, KD, T)
        cv_h = at(4096, KD, T)
        cv_u = at(6144, KD, T + 2)
        cv_y = at(8448, KD, T)
        cv_z = at(10496, KD, T)
        rkv = at(1024, 12, T)
        r_fm, k_fm, v_fm = (at(1024 * (1 + n), 4, T) for n in range(3))
        g_fm = at(4096, 4, T)
        a_til, b_til, k_til, r_til = (at(5120 + 1024 * n, 4, T) for n in range(4))
        a_tm, bh_tm, kh_tm, v_tm = (at(9216 + 1024 * n, NX, 512) for n in range(4))
        qk2 = at(5120, 8, T)
        v2 = at(7168, NX, 512)
        sc2 = at(8192, 4, ATT_COLS)
        pT2 = at(9728, 4, ATT_COLS)
        ob2 = at(11264, NX, 512)
        ya_fm = at(13312, 4, T)
        step_m = at(14336, 4, NCH, HD2)
        step_n = at(16384, 4, NCH, HD2)
        state = at(18432, NCH, 4, HD2)
        q_eff = at(20736, 4, T)
        y_fm = at(21760, 4, T)
        sol = at(22784, 8, P)
        mats = [at(23808 + 1024 * n, 8, P) for n in range(8)]
        cols = at(14336, RW_TILES, T + 1)
        kk_fm = at(18432, 4, T)
        aa_fm = at(19456, 4, T)
        cum = at(20480, 4, T)
        e1 = at(21504, 4, T)
        e2 = at(22528, 4, T)
        bh_fm = at(23552, 4, T)
        kh_fm = at(24576, 4, T)
        lora = at(25600, 3, 512)
        band_bias = at(27136, HEADS2, ATT_COLS)
        low = at(30208, 3, T)
        gates2 = at(9216, 16, T)
        start = at(32000, T)
        y_out = at(22784, 4, T)
        y_sq = at(23808, 4, T)
        y_mu = at(24832, 4, T)
        y_rs = at(25856, 4, T)
        bonus = at(26880, 4, T)
        y_tmp = at(27904, 4, T)
        mixT = at(5120, KD, T)
        mix_tmp = at(7168, 2, T)
        comb_d = at(512, NEXP, T)
        h_sig = at(8704, 2, 2 * T)
        h_mid = at(9728, 2, 2 * T)
        o = 10752
        logit = at(o, NX, 36); o += 72
        g8 = at(o, NX, 8); o += 16
        g8m = at(o, NX, 8); o += 16
        g8i = at(o, NX, 8); o += 16
        hot_g = at(o, NX, 8); o += 16
        sel8 = at(o, NX, 8); o += 16
        sel8m = at(o, NX, 8); o += 16
        sel8i = at(o, NX, 8); o += 16
        sel8f = at(o, NX, 8); o += 16
        sel_t = at(o, NX, 8, 4); o += 64
        comb8 = at(o, NX, 8); o += 16
        comb8b = at(o, NX, 8); o += 16
        comb = at(o, NX, NEXP); o += 64
        combT = at(o, T); o += T
        pT_ple = at(0, 2, T)
        assert o <= 12800
        ple = at(12800, NX, D)
        sig_ple = at(14848, NX, D)
        ln_sq = at(31744, D)

        acc = ps("acc", 4)
        prod = ps("prod", 2)
        gen = ps("gen", 2)

        landed = [sem(f"landed{i}") for i in range(RING)]
        hi_ready = sem("hi_ready")
        hi_used = sem("hi_used")
        lo_ready = [sem(f"lo_ready{i}") for i in range(PAIR)]
        w_used = sem("w_used")
        fm_out = sem("fm_out")
        acc_out = sem("acc_out")
        gen_mm = sem("gen_mm")
        gen_out = sem("gen_out")
        x_in = sem("x_in")
        small_in = sem("small_in")
        table_b_in = sem("table_b_in")
        gain_in = [sem("gain_in0"), sem("gain_in1")]
        gain_used = sem("gain_used")
        block2_in = sem("block2_in")
        ple_in = sem("ple_in")
        arena_free = sem("arena_free")
        ms_ready = sem("ms_ready")
        root_ready = sem("root_ready")
        normed = sem("normed")
        fm_ready = sem("fm_ready")
        roped = sem("roped")
        att_s = sem("att_s")
        att_m = sem("att_m")
        att_p = sem("att_p")
        att_pt = sem("att_pt")
        att_o = sem("att_o")
        att_done = sem("att_done")
        topk_ready = sem("topk_ready")
        gate_exp = sem("gate_exp")
        hot_ready = sem("hot_ready")
        tok_mm = sem("tok_mm")
        hh_ready = sem("hh_ready")
        hl_ready = sem("hl_ready")
        gated = sem("gated")
        yT_ready = sem("yT_ready")
        conv_in = sem("conv_in")
        shifted = sem("shifted")
        low_act = sem("low_act")
        lora_mm = sem("lora_mm")
        lora_out = sem("lora_out")
        logw_ready = sem("logw_ready")
        exp_ready = sem("exp_ready")
        til_ready = sem("til_ready")
        sq_ready = sem("sq_ready")
        scan_mm = sem("scan_mm")
        state_ready = sem("state_ready")
        branch_out = sem("branch_out")
        silu_ready = sem("silu_ready")
        mid_ready = sem("mid_ready")
        comb_mm = sem("comb_mm")
        max_ready = sem("max_ready")
        moe_exp = sem("moe_exp")
        ple_sig = sem("ple_sig")
        v_chain = sem("v_chain")
        a_chain = sem("a_chain")
        out_done = sem("out_done")

        block = ctx.enter_context(nc.Block())

        @block.sync
        def _(sp):
            def load(g, src, i=0, n=RING):
                if g >= RING:
                    if g - RING in SPLIT_PLACE:
                        s = SPLIT_PLACE[g - RING]
                        sp.wait_ge(lo_ready[s % PAIR], s // PAIR + 1 + n // PAIR * i)
                    else:
                        sp.wait_ge(w_used, g - RING + 1 + n * i)
                sp.dma_start(ring[:, g % RING, :], src).then_inc(landed[g % RING], 16)

            def stream(name, src, n):
                base = BASE[name]
                for b in range(min(n, RING)):
                    load(base + b, src[b])
                whole = n // RING
                if whole > 2:
                    with sp.Fori(0, whole - 1) as i:
                        for j in range(RING):
                            load(base + RING + j, src[RING * i + RING + j], i)
                else:
                    for b in range(RING, RING * whole):
                        load(base + b, src[b])
                for b in range(max(RING, RING * whole), n):
                    load(base + b, src[b])

            for name in ("even_qk", "even_vg", "even_out"):
                stream(name, dram[name], dict(STREAM)[name])
            for layer in range(LAYERS):
                if layer == 1:
                    stream("odd_in", dram["odd_in"], 24)
                    stream("odd_out", dram["odd_out"], 8)
                stream(f"peer_q{layer}", dram[f"peer_q{layer}"], 16)
                stream(f"peer_keys{layer}", dram[f"peer_keys{layer}"], 2)
                stream(f"peer_u{layer}", dram[f"peer_u{layer}"], NK)
                stream(f"peer_v{layer}", dram["peer_v"][layer].rearrange("(a c) d -> c a d", c=NK), NK)
            stream("qk2", dram["qk2"], 8)
            stream("v2", dram["v2"], 4)
            stream("rw2", dram["rw2"], RW_TILES)
            stream("gate2", dram["gate2"], 16)
            for j in range(4):
                load(BASE["branch"] + 2 * j, dram["branch_a"][j])
                load(BASE["branch"] + 2 * j + 1, dram["branch_r"][j])
            stream("out2", dram["out2"], 8)
            g = BASE["moe"]
            for j in range(4):
                load(g + j, (dram["exp_gate"], dram["exp_up"])[j // 2][j % 2])

            def expert(g, e, i):
                for j in range(4):
                    load(g + j, (dram["exp_gate"], dram["exp_up"])[j // 2][2 * e + j % 2], i, 12)
                for j in range(2):
                    load(g + 4 + j, dram["exp_down"][2 * e - 2 + j], i, 12)

            with sp.Fori(0, (NEXP - 2) // 2) as i:
                for j in range(2):
                    expert(g + 4 + 6 * j, 2 * i + 1 + j, i)
            expert(g + 4 + 6 * (NEXP - 2), NEXP - 1, 0)
            for j in range(2):
                load(g + 6 * NEXP - 2 + j, dram["exp_down"][2 * NEXP - 2 + j])
            stream("ple_proj", dram["ple_proj"], 2)
            stream("ple_gate", dram["ple_gate"], 8)
            sp.wait_ge(normed, NORMED["ln2"])
            sp.dma_start(out.rearrange("a (x p) d -> p (a x) d", p=P), resid[:, :, :]).then_inc(out_done, 16)
            sp.wait_ge(out_done, 16)

        @block.gpsimd
        def _(pool):
            def rest(g, s, i=0):
                pool.wait_ge(hi_ready, s + 1 + RING * i)
                if s >= PAIR:
                    pool.wait_ge(w_used, SPLIT_BLOCKS[s - PAIR] + 1 + RING * i)
                pool.tensor_tensor(wlo[:, s % PAIR, :], ring[:, g % RING, :], whi[:, s % PAIR, :].bitcast(F32), ALU.subtract)\
                    .then_inc(lo_ready[s % PAIR], 1)

            def rests(name, n):
                g, s = BASE[name], SPLIT[name]
                for b in range(RING):
                    rest(g + b, s + b)
                with pool.Fori(0, n // RING - 1) as i:
                    for j in range(RING):
                        rest(g + RING + j, s + RING + j, i)

            pool.dma_start(const_a[:, :], dram["const_a"]).then_inc(small_in, 16)
            pool.dma_start(vec[:, :], dram["vec"]).then_inc(small_in, 16)
            pool.dma_start(const_b, dram["const_b"]).then_inc(table_b_in, 16)
            pool.dma_start(gains[:, 0, :], dram["final_norm"].partition_broadcast(P)).then_inc(gain_in[0], 16)
            pool.dma_start(gains[:, 1, :], dram["ln_in_g"].partition_broadcast(P)).then_inc(gain_in[1], 16)
            pool.dma_start(gains[:, 2, :], dram["ln_in_b"].partition_broadcast(P)).then_inc(gain_in[1], 16)
            for layer in range(LAYERS):
                if layer == 1:
                    rests("odd_in", 24)
                rests(f"peer_q{layer}", 16)
                rests(f"peer_u{layer}", 2 * NK)
            pool.wait_ge(arena_free, 1)
            pool.dma_start(lora[:, :, :], dram["lora"]).then_inc(block2_in, 16)
            pool.dma_start(band_bias[:, :, :], dram["band_bias"]).then_inc(block2_in, 16)
            pool.dma_start(const_c, dram["const_c"]).then_inc(block2_in, 16)
            pool.dma_start(router, dram["router"]).then_inc(block2_in, 16)
            pool.dma_start(router_b, dram["router_b"].partition_broadcast(P)).then_inc(block2_in, 16)
            pool.dma_start(pT_ple, dram["p"]).then_inc(ple_in, 16)

            def norm_gains(n):
                pool.wait_ge(gain_used, n + 2)
                for j, name in enumerate(("ln_g", "ln_b")):
                    pool.dma_start(gains[:, 1 + j, :], dram[name][n].partition_broadcast(P)).then_inc(gain_in[1], 16)

            norm_gains(0)
            rests("gate2", 16)
            rests("moe", 6 * NEXP)
            norm_gains(1)
            norm_gains(2)
            pool.wait_ge(gain_in[1], 128)

        @block.tensor
        def _(pe):
            gi = [0]
            au = [0]

            def arrive(g):
                pe.wait_ge(landed[g % RING], 16 * (g // RING + 1))
                return ring[:, g % RING, :]

            def gen_bank():
                if gi[0] >= 2:
                    pe.wait_ge(gen_out, gi[0] - 1)
                gi[0] += 1
                return gen[:, (gi[0] - 1) % 2, :]

            def acc_free():
                if au[0]:
                    pe.wait_ge(acc_out, au[0])
                au[0] += 1

            def fm_block(g, f, src):
                w = arrive(g)
                if f >= 2:
                    pe.wait_ge(fm_out, f - 1)
                for k in range(KD):
                    mm = pe.matmul(prod[:, f % 2, 0:T], w[:, k * P:(k + 1) * P], src[:, k, :],
                                   start=(k == 0), stop=(k == KD - 1))
                mm.then_inc(w_used, 1)

            def rounded(s, i, n):
                pe.wait_ge(hi_ready, s + 1 + n * i)
                return whi[:, s % PAIR, :]

            def rest(s, i, n):
                pe.wait_ge(lo_ready[s % PAIR], s // PAIR + 1 + n // PAIR * i)
                return wlo[:, s % PAIR, :]

            def fm_passes(dst, s, i, n):
                w = rounded(s, i, n)
                for k in range(KD):
                    pe.matmul(dst, w[:, k * P:(k + 1) * P], xh[:, k, :], start=(k == 0), stop=False)
                    mm = pe.matmul(dst, w[:, k * P:(k + 1) * P], xl[:, k, :], start=False, stop=False)
                mm.then_inc(hi_used, 1)
                w = rest(s, i, n)
                for k in range(KD):
                    mm = pe.matmul(dst, w[:, k * P:(k + 1) * P], xh[:, k, :], start=False, stop=(k == KD - 1))
                mm.then_inc(w_used, 1)

            def fm_split(name, b, i=0):
                s, f = SPLIT[name] + b, FMBASE[name] + b
                pe.wait_ge(fm_out, f - 1 + RING * i)
                fm_passes(prod[:, f % 2, 0:T], s, i, RING)

            def tm_block(g, lhs, kpair, banks, last):
                w = arrive(g)
                for x in range(NX):
                    for k in range(2):
                        kk = 2 * kpair + k
                        mm = pe.matmul(acc[:, banks[x], :], lhs[:, kk, x * P:(x + 1) * P], w[:, k * 512:(k + 1) * 512],
                                       start=(kk == 0), stop=(kk == last))
                mm.then_inc(w_used, 1)

            def tm_square(name, lhs):
                acc_free()
                for b in range(8):
                    tm_block(BASE[name] + b, lhs, b % 4, (b // 4, 2 + b // 4), KD - 1)

            def turn(src, tiles):
                for x in range(NX):
                    for q in range(tiles // 4):
                        bank = gen_bank()
                        for k in range(4):
                            mm = pe.transpose(bank[:, k * P:(k + 1) * P], src[:, x, (4 * q + k) * P:(4 * q + k + 1) * P], ident)
                        mm.then_inc(gen_mm, 1)

            def attend_scores(q_of, k_of):
                acc_free()
                for h in range(4):
                    pe.matmul(acc[:, h, 0:P], q_of(h)[:, 0:P], k_of(h)[:, 0:P], start=True, stop=True)
                    pe.matmul(acc[:, h, P:ATT_COLS], q_of(h)[:, P:T], k_of(h), start=True, stop=True).then_inc(att_s, 1)

            def attend_values(soft, turned, p_sb, pT, v_of, width):
                for h in range(4):
                    pe.wait_ge(att_p, soft + h + 1)
                    bank = gen_bank()
                    for b in range(3):
                        mm = pe.transpose(bank[:, b * P:(b + 1) * P], p_sb[:, h, b * P:(b + 1) * P], ident)
                    mm.then_inc(gen_mm, 1)
                for h in range(4):
                    pe.wait_ge(att_pt, turned + h + 1)
                    values(pT, v_of, h, width, h == 3)

            def values(pT, v_of, h, width, last):
                cols_ = slice(h * width, (h + 1) * width)
                pe.matmul(prod[:, 0, cols_], pT[:, h, 0:P], v_of(0, h), start=True, stop=True)
                pe.matmul(prod[:, 1, cols_], pT[:, h, P:2 * P], v_of(0, h), start=True, stop=False)
                mm = pe.matmul(prod[:, 1, cols_], pT[:, h, 2 * P:3 * P], v_of(1, h), start=False, stop=True)
                if last:
                    mm.then_inc(att_o, 1)

            pe.wait_ge(small_in, 32)
            pe.wait_ge(normed, NORMED["mix0"])
            turn(xn, KD)
            pe.wait_ge(fm_ready, FM["mix0"])
            for b in range(16):
                fm_block(BASE["even_qk"] + b, FMBASE["even_qk"] + b, xT)
            pe.wait_ge(table_b_in, 16)
            for b in range(12):
                if b in (0, 8):
                    acc_free()
                tm_block(BASE["even_vg"] + b, xT, b % 4, ((0, 1), (2, 3), (0, 1))[b // 4], KD - 1)
                if b < 8:
                    pe.wait_ge(fm_out, 2 * b + 2)
                    pe.matmul(gen_bank(), cb("rot"), qk1[:, 2 * b:2 * b + 2, :].rearrange("p a b -> p (a b)"),
                              start=True, stop=True).then_inc(gen_mm, 1)
            pe.wait_ge(roped, 8)
            attend_scores(lambda h: qk1[:, h, :], lambda h: qk1[:, 4 + h, :])
            attend_values(0, 0, sc1, pT1, lambda x, h: v_moba[:, x, h * HD1:(h + 1) * HD1], HD1)
            acc_free()
            for h in range(4):
                q, k = qk1[:, 8 + h, :], qk1[:, 12 + h, :]
                pe.matmul(acc[:, h, 0:T], k[:, 0:P], q, start=True, stop=True)
                pe.matmul(acc[:, h, T:ATT_COLS], k[:, P:T], q[:, P:T], start=True, stop=True).then_inc(att_s, 1)
            pe.wait_ge(att_done, 1)
            for h in range(4):
                pe.wait_ge(att_pt, 4 + h + 1)
                values(rT1, lambda x, h: v_ret[:, x, h * HD1:(h + 1) * HD1], h, HD1, h == 3)
            pe.wait_ge(normed, NORMED["cat"])
            turn(cat1, KD)
            pe.wait_ge(fm_ready, FM["cat"])
            tm_square("even_out", xT)

            def peer(layer):
                pe.wait_ge(normed, NORMED[f"ffn{layer}"])
                turn(xn, KD)
                pe.wait_ge(fm_ready, FM[f"ffn{layer}"])
                pe.wait_ge(att_done, 2)
                for b in range(16):
                    fm_split(f"peer_q{layer}", b)
                pe.wait_ge(fm_out, FMBASE[f"peer_q{layer}"] + 16)
                for b in range(2):
                    w = arrive(BASE[f"peer_keys{layer}"] + b)
                    for x in range(NX):
                        for q in range(2):
                            bank = gen_bank()
                            for j in range(4):
                                n = 4 * q + j
                                mm = pe.matmul(bank[:, j * P:(j + 1) * P], peer_qT[:, 8 * b + n, x * P:(x + 1) * P],
                                               w[:, n * P:(n + 1) * P], start=True, stop=True)
                            mm.then_inc(gen_mm, 1)
                    pe.wait_ge(gen_mm, gi[0])
                    pe.nop().then_inc(w_used, 1)
                vs, hb = SPLIT[f"peer_v{layer}"], layer * NK
                tb = 2 * layer * HALF

                def hidden(i, j):
                    fm_split(f"peer_u{layer}", j, i)

                def token_gates(i, j, half):
                    pe.wait_ge(hot_ready, tb + half * HALF + j + 1 + RING * i)
                    for t in range(GTOK):
                        for n in range(2):
                            mm = pe.matmul(gen[:, 0, t * HALF:(t + 1) * HALF], hot1[:, t, :], hot2[:, n, t, :],
                                           start=(n == 0), stop=(n == 1))
                    mm.then_inc(tok_mm, 1)

                def down(i, j, first=False, last=False):
                    def value(d, w, h, start, stop):
                        return pe.matmul(acc[:, d // 2, (d % 2) * T:(d % 2 + 1) * T], w[:, d * P:(d + 1) * P], h[:, j % RING, :],
                                         start=start, stop=stop, skip_group_check=True)

                    pe.wait_ge(hl_ready, hb + j + 1 + RING * i)
                    w = rounded(vs + j, i, RING)
                    for d in range(KD):
                        value(d, w, hid_hi, first and d % 2 == 0, False)
                        mm = value(d, w, hid_lo, False, False)
                    mm.then_inc(hi_used, 1)
                    w = rest(vs + j, i, RING)
                    for d in range(KD):
                        mm = value(d, w, hid_hi, False, last)
                    mm.then_inc(w_used, 1)

                with pe.Fori(0, HALF // RING) as i:
                    for j in range(RING):
                        hidden(i, j)
                pe.wait_ge(normed, NORMED[f"route{layer}"])
                for x in range(NX):
                    bank = gen_bank()
                    for n in range(3):
                        mm = pe.transpose(bank[:, n * P:(n + 1) * P], sel_i[:, n, x, :], ident)
                    mm.then_inc(gen_mm, 1)
                with pe.Fori(0, HALF // RING) as i:
                    for j in range(RING):
                        token_gates(i, j, 0)
                        hidden(i + HALF // RING, j)
                acc_free()
                for j in range(RING):
                    token_gates(0, j, 1)
                    down(0, j, first=(j == 0))
                with pe.Fori(1, HALF // RING) as i:
                    for j in range(RING):
                        token_gates(i, j, 1)
                        down(i, j)
                with pe.Fori(HALF // RING, NK // RING - 1) as i:
                    for j in range(RING):
                        down(i, j)
                for j in range(RING):
                    down(NK // RING - 1, j, last=(j == RING - 1))
                pe.wait_ge(acc_out, au[0])
                for x in range(NX):
                    for q in range(2):
                        bank = gen_bank()
                        for k in range(4):
                            mm = pe.transpose(bank[:, k * P:(k + 1) * P], peer_yT[:, 4 * q + k, x * P:(x + 1) * P], ident)
                        mm.then_inc(gen_mm, 1)

            peer(0)
            pe.wait_ge(normed, NORMED["mix1"])
            turn(xn, KD)
            pe.wait_ge(fm_ready, FM["mix1"])
            for b in range(24):
                fm_split("odd_in", b)
            pe.wait_ge(fm_ready, FM["conv"])
            tm_square("odd_out", cv_z)
            peer(1)
            pe.wait_ge(normed, NORMED["blk2"])
            turn(resid, KD)
            pe.wait_ge(fm_ready, FM["blk2"])
            for b in range(8):
                fm_block(BASE["qk2"] + b, FMBASE["qk2"] + b, xT2)
            acc_free()
            for b in range(4):
                tm_block(BASE["v2"] + b, xT2, b, (0, 1), KD - 1)
            pe.wait_ge(fm_out, FMBASE["rw2"])

            def band(r):
                def rows(h, tile):
                    hh = 4 * r + h
                    return qk2[HD2 * (hh % 2):HD2 * (hh % 2 + 1), tile + hh // 2, :]
                return lambda h: rows(h, 0), lambda h: rows(h, 4), \
                    lambda x, h: v2[:, x, (4 * r + h) * HD2:(4 * r + h + 1) * HD2]

            q_of, k_of, v_of = band(0)
            attend_scores(q_of, k_of)
            for b in range(RW_TILES):
                fm_block(BASE["rw2"] + b, FMBASE["rw2"] + b, xT2)
            pe.wait_ge(fm_out, FMBASE["gate2"])
            attend_values(4, 8, sc2, pT2, v_of, HD2)
            q_of, k_of, v_of = band(1)
            pe.wait_ge(att_done, 3)
            attend_scores(q_of, k_of)
            attend_values(8, 12, sc2, pT2, v_of, HD2)
            pe.wait_ge(normed, NORMED["band"])
            turn(ob2, 4)
            pe.wait_ge(block2_in, 80)
            pe.wait_ge(low_act, 2)
            for n in range(6):
                if n >= 2:
                    pe.wait_ge(lora_out, n - 1)
                for j in range(2):
                    f = 2 * (n % 2) + j
                    dst = prod[:, n % 2, j * T:(j + 1) * T]
                    if n < 4:
                        rows = slice(64 * (n // 2), 64 * (n // 2) + 64)
                        mm = pe.matmul(dst, lora[rows, 0, f * P:(f + 1) * P], low[rows, 0, :], start=True, stop=True)
                    else:
                        pe.matmul(dst, lora[:, 1, f * P:(f + 1) * P], low[:, 1, :], start=True, stop=False)
                        mm = pe.matmul(dst, lora[0:32, 2, f * P:(f + 1) * P], low[0:32, 2, :], start=False, stop=True)
                mm.then_inc(lora_mm, 1)

            def head_sums(src, count):
                pe.wait_ge(sq_ready, count)
                for q in range(2):
                    pe.matmul(gen_bank(), cc("ones64"), src[:, 2 * q:2 * q + 2, :].rearrange("p a b -> p (a b)"),
                              start=True, stop=True).then_inc(gen_mm, 1)

            head_sums(e1, 1)
            pe.wait_ge(fm_ready, FM["til"])
            for x in range(NX):
                for src in (a_til, bh_fm, kh_fm, v_fm):
                    bank = gen_bank()
                    for pr in range(4):
                        mm = pe.transpose(bank[:, pr * P:(pr + 1) * P], src[:, pr, x * P:(x + 1) * P], ident)
                    mm.then_inc(gen_mm, 1)

            def by_head(lhs, rhs, x):
                for q in range(2):
                    bank = gen_bank()
                    rows = slice(64 * q, 64 * q + 64)
                    for pr in range(4):
                        mm = pe.matmul(bank[:, pr * P:(pr + 1) * P], lhs[rows, pr, x * P:(x + 1) * P],
                                       rhs[rows, pr, x * P:(x + 1) * P], start=True, stop=True)
                    mm.then_inc(gen_mm, 1)

            def square(lhs, rhs):
                for q in range(2):
                    bank = gen_bank()
                    for u in range(4):
                        mm = pe.matmul(bank[:, u * P:(u + 1) * P], lhs[:, 4 * q + u, :], rhs[:, 4 * q + u, :],
                                       start=True, stop=True)
                    mm.then_inc(gen_mm, 1)

            def all_out():
                pe.wait_ge(gen_out, gi[0])

            m_lT, m_l, m_ak, m_rb, m_rk, m_off, m_a, m_b = mats
            for x in range(NX):
                by_head(b_til, a_til, x)
                by_head(a_til, b_til, x)
                by_head(k_til, a_til, x)
                by_head(b_til, r_til, x)
                by_head(k_til, r_til, x)
                all_out()
                bank = gen_bank()
                for hd in range(HEADS2):
                    mm = pe.matmul(bank[:, hd * HD2:(hd + 1) * HD2], m_ak[:, hd, :], v_tm[:, x, hd * HD2:(hd + 1) * HD2],
                                   start=True, stop=True)
                mm.then_inc(gen_mm, 1)
                square(m_lT, m_l)
                square(m_l, m_lT)
                all_out()
                square(m_a, m_ak)
                square(m_b, m_a)
                square(m_a, m_b)
                all_out()
                square(m_l, m_ak)
                square(m_lT, m_l)
                all_out()
                square(m_a, m_ak)
                all_out()
                square(m_ak, sol)
                all_out()
                square(m_off, m_b)
                all_out()
                square(m_ak, m_lT)
                all_out()
                bank = gen_bank()
                for hd in range(HEADS2):
                    rows = slice(64 * (hd % 2), 64 * (hd % 2) + 64)
                    mm = pe.matmul(bank[rows, (hd // 2) * P:(hd // 2 + 1) * P], sol[:, hd, 0:HD2], m_rb[:, hd, :],
                                   start=True, stop=True)
                mm.then_inc(gen_mm, 1)
                bank = gen_bank()
                for hd in range(HEADS2):
                    rows = slice(64 * (hd % 2), 64 * (hd % 2) + 64)
                    dst = bank[rows, (hd // 2) * P:(hd // 2 + 1) * P]
                    pe.matmul(dst, sol[:, hd, HD2:P], m_rb[:, hd, :], start=True, stop=False)
                    mm = pe.matmul(dst, v_tm[:, x, hd * HD2:(hd + 1) * HD2], m_rk[:, hd, :], start=False, stop=True)
                mm.then_inc(gen_mm, 1)
                for c in range(4):
                    bank = gen_bank()
                    tok = slice(CH * c, CH * c + CH)
                    for hd in range(HEADS2):
                        rows, hc = slice(64 * (hd % 2), 64 * (hd % 2) + 64), slice(hd * HD2, (hd + 1) * HD2)
                        o_ = (hd // 2) * HD2
                        pe.matmul(bank[rows, o_:o_ + HD2], sol[tok, hd, 0:HD2], bh_tm[tok, x, hc], start=True, stop=True)
                        o_ += 4 * HD2
                        pe.matmul(bank[rows, o_:o_ + HD2], bh_tm[tok, x, hc], sol[tok, hd, HD2:P], start=True, stop=False)
                        mm = pe.matmul(bank[rows, o_:o_ + HD2], kh_tm[tok, x, hc], v_tm[tok, x, hc], start=False, stop=True)
                    mm.then_inc(gen_mm, 1)
            pe.wait_ge(lora_out, 6)
            for c in range(1, NCH - 1):
                for b in range(2 * c - 2, 2 * c):
                    fm_split("gate2", b)
                pe.wait_ge(state_ready, c)
                bank = gen_bank()
                for hd in range(HEADS2):
                    rows = slice(64 * (hd % 2), 64 * (hd % 2) + 64)
                    mm = pe.matmul(bank[rows, (hd // 2) * HD2:(hd // 2 + 1) * HD2], step_m[rows, hd // 2, c, :],
                                   state[rows, c, hd // 2, :], start=True, stop=True)
                mm.then_inc(gen_mm, 1)
            for b in range(2 * NCH - 4, 16):
                fm_split("gate2", b)
            pe.wait_ge(state_ready, NCH - 1)
            for q in range(2):
                bank = gen_bank()
                for hd in range(4 * q, 4 * q + 4):
                    rows = slice(64 * (hd % 2), 64 * (hd % 2) + 64)
                    for c in range(1, NCH):
                        o_ = (hd // 2 - 2 * q) * T + c * CH
                        mm = pe.matmul(bank[rows, o_:o_ + CH], state[rows, c, hd // 2, :],
                                       q_eff[rows, hd // 2, c * CH:(c + 1) * CH], start=True, stop=True)
                mm.then_inc(gen_mm, 1)
            head_sums(y_fm, 2)
            head_sums(y_sq, 3)
            head_sums(bonus, 4)
            pe.wait_ge(fm_ready, FM["rwkv"])
            pe.wait_ge(fm_out, FMBASE["gate2"] + 16)
            for j in range(4):
                if j:
                    pe.wait_ge(branch_out, j)
                for n, src in enumerate((ya_fm, y_out)):
                    w = arrive(BASE["branch"] + 2 * j + n)
                    for f in range(2):
                        for k in range(4):
                            mm = pe.matmul(prod[:, n, f * T:(f + 1) * T], w[:, (2 * k + f) * P:(2 * k + f + 1) * P],
                                           src[:, k, :], start=(k == 0), stop=(k == 3))
                    mm.then_inc(w_used, 1)
            pe.wait_ge(fm_ready, FM["mixed"])
            tm_square("out2", mixT)
            pe.wait_ge(normed, NORMED["ln0"])
            turn(resid, KD)
            pe.wait_ge(fm_ready, FM["ln0"])
            bank = gen_bank()
            for x in range(NX):
                for k in range(KD):
                    mm = pe.matmul(bank[:, x * 36:(x + 1) * 36], xT2[:, k, x * P:(x + 1) * P], router[:, k, :],
                                   start=(k == 0), stop=(k == KD - 1))
            mm.then_inc(gen_mm, 1)
            pe.wait_ge(normed, NORMED["comb"])
            bank = gen_bank()
            for x in range(NX):
                mm = pe.transpose(bank[0:NEXP, x * P:(x + 1) * P], comb[:, x, :], ident)
            mm.then_inc(gen_mm, 1)
            pe.wait_ge(fm_ready, FM["comb"])
            acc_free()
            es = SPLIT["moe"]

            def expert_up(s, e, i=0, first=False):
                for n in range(2):
                    if not first:
                        pe.wait_ge((silu_ready, mid_ready)[n], e + 2 * i)
                    for f in range(2):
                        fm_passes(prod[:, n, f * T:(f + 1) * T], s + 2 * n + f, i, 12)
                pe.matmul(gen[:, 0, 0:T], cc("ones")[0:NEXP, :], comb_d[0:NEXP, e + 2 * i, :], start=True, stop=True)\
                    .then_inc(comb_mm, 1)

            def expert_down(s, i=0, first=False, last=False):
                for f in range(2):
                    def rows(w, mid, start, stop):
                        for x in range(NX):
                            for n in range(2):
                                mm = pe.matmul(acc[:, 2 * x + n, :], mid[:, f * T + x * P:f * T + (x + 1) * P],
                                               w[:, n * 512:(n + 1) * 512], start=start, stop=stop, skip_group_check=True)
                        return mm

                    w = rounded(s + f, i, 12)
                    rows(w, mid_hi, first and f == 0, False)
                    rows(w, mid_lo, False, False).then_inc(hi_used, 1)
                    rows(rest(s + f, i, 12), mid_hi, False, last and f == 1).then_inc(w_used, 1)

            expert_up(es, 0, first=True)
            expert_up(es + 4, 1)
            expert_down(es + 8, first=True)
            with pe.Fori(0, (NEXP - 2) // 2) as i:
                for j in range(2):
                    expert_up(es + 10 + 6 * j, 2 + j, i)
                    expert_down(es + 14 + 6 * j, i)
            pe.wait_ge(mid_ready, NEXP)
            expert_down(es + 6 * NEXP - 2, last=True)
            acc_free()
            pe.wait_ge(ple_in, 16)
            for b in range(2):
                w = arrive(BASE["ple_proj"] + b)
                for x in range(NX):
                    for k in range(2):
                        mm = pe.matmul(acc[:, 2 * x + b, :], pT_ple[:, k, x * P:(x + 1) * P], w[:, k * 512:(k + 1) * 512],
                                       start=(k == 0), stop=(k == 1))
                mm.then_inc(w_used, 1)
            pe.wait_ge(normed, NORMED["ln1"])
            turn(resid, KD)
            pe.wait_ge(fm_ready, FM["ln1"])
            tm_square("ple_gate", xT2)

        @block.scalar
        def _(act):
            def take(name, b, dst, func, **kw):
                act.wait_ge(w_used, BASE[name] + b + 1)
                act.activation(dst, prod[:, (FMBASE[name] + b) % 2, 0:T], func, **kw).then_inc(fm_out, 1)

            def rounded(name, b, i=0, n=RING):
                g, s = BASE[name] + b, SPLIT[name] + b
                act.wait_ge(landed[g % RING], 16 * (g // RING + 1) + 16 * (n // RING) * i)
                if s >= PAIR:
                    act.wait_ge(hi_used, s - PAIR + 1 + n * i)
                    act.wait_ge(lo_ready[s % PAIR], s // PAIR + n // PAIR * i)
                act.activation(whi[:, s % PAIR, :], ring[:, g % RING, :], ACT.Copy).then_inc(hi_ready, 1)

            def rounded_take(name, n, dst, func):
                for b in range(n):
                    if b + PAIR < n:
                        rounded(name, b + PAIR)
                    take(name, b, dst(b), func)

            def root(name, dst, src):
                act.wait_ge(ms_ready, ROOT[name])
                act.activation(dst, src, ACT.Sqrt).then_inc(root_ready, 1)

            def norm_root(name):
                root(name, st[:, 4:6], st[:, 2:4])

            def soft(base, s):
                for h in range(4):
                    act.wait_ge(att_m, base + h + 1)
                    act.activation(s[:, h, 0:P], s[:, h, 0:P], ACT.Exp, bias=st[:, 16 + h:17 + h],
                                   accum_out=st[:, 24 + h:25 + h])
                    act.activation(s[:, h, P:ATT_COLS], s[:, h, P:ATT_COLS], ACT.Exp, bias=st[:, 20 + h:21 + h],
                                   accum_out=st[:, 28 + h:29 + h]).then_inc(att_p, 1)

            act.dma_start(resid[:, :, :], dram["x"].rearrange("a (x p) d -> p (a x) d", p=P)).then_inc(x_in, 16)
            norm_root("mix0")
            for b in range(16):
                take("even_qk", b, qk1[:, b, :], ACT.Copy)
            act.wait_ge(w_used, BASE["even_vg"] + 8)
            for n, dst in enumerate((v_moba, v_ret)):
                for x in range(NX):
                    mv = act.activation(dst[:, x, :], acc[:, 2 * n + x, :], ACT.Copy)
            mv.then_inc(acc_out, 1)
            act.wait_ge(w_used, BASE["even_vg"] + 12)
            for x in range(NX):
                mv = act.activation(g_ret[:, x, :], acc[:, x, :], ACT.Silu)
            mv.then_inc(acc_out, 1)
            soft(0, sc1)
            root("ret", st[:, 56:64], st[:, 48:56])

            def peer(layer):
                q, u, v = f"peer_q{layer}", f"peer_u{layer}", f"peer_v{layer}"
                for b in range(PAIR):
                    rounded(q, b)
                norm_root(f"ffn{layer}")
                rounded_take(q, 16, lambda b: peer_qT[:, b, :], ACT.Copy)
                for b in range(PAIR):
                    rounded(u, b)

                def hidden(i):
                    for j in range(RING):
                        rounded(u, j + PAIR, i)
                        act.wait_ge(w_used, BASE[u] + j + 1 + RING * i)
                        act.activation(hid[:, RING * i + j, :], prod[:, (FMBASE[u] + j) % 2, 0:T], ACT.Gelu).then_inc(fm_out, 1)

                early = 12
                with act.Fori(0, early) as i:
                    hidden(i)
                act.wait_ge(topk_ready, layer + 1)
                act.activation(sel_i[:, 2, :, :], sel_i[:, 2, :, :], ACT.Exp).then_inc(gate_exp, 1)
                with act.Fori(early, NK // RING) as i:
                    hidden(i)

                def chunk(j, i=0):
                    if j >= PAIR:
                        rounded(v, j, i)
                    if j >= RING:
                        act.wait_ge(w_used, BASE[v] + j - RING + 1 + RING * i)
                    act.activation(hid_hi[:, j % RING, :], hid[:, RING * i + j, :], ACT.Copy).then_inc(hh_ready, 1)

                for half in range(2):
                    act.wait_ge(gated, 2 * layer * HALF + (half + 1) * HALF)
                    if half == 0:
                        for j in range(RING):
                            chunk(j)
                    with act.Fori(half * (HALF // RING - 1), (half + 1) * HALF // RING - 1) as i:
                        for j in range(RING):
                            chunk(RING + j, i)
                act.wait_ge(w_used, BASE[v] + NK)
                for n in range(4):
                    mv = act.activation(peer_yT[:, 2 * n:2 * n + 2, :].rearrange("p a b -> p (a b)"), acc[:, n, :], ACT.Copy)
                mv.then_inc(acc_out, 1)

            peer(0)
            for b in range(PAIR):
                rounded("odd_in", b)
            norm_root("mix1")
            rounded_take("odd_in", 24, lambda b: (cv_b, cv_c, cv_h)[b % 3][:, b // 3, :], ACT.Copy)
            peer(1)
            norm_root("final")
            norm_root("ln_in")
            for b in range(8):
                take("qk2", b, qk2[:, b, :], ACT.Copy)
            act.wait_ge(w_used, BASE["v2"] + 4)
            for x in range(NX):
                mv = act.activation(v2[:, x, :], acc[:, x, :], ACT.Copy)
            mv.then_inc(acc_out, 1)
            soft(4, sc2)
            for b in range(RW_TILES):
                take("rw2", b, cols[:, b, 1:T + 1], ACT.Copy)
            soft(8, sc2)
            act.wait_ge(shifted, 1)
            act.activation(low[0:64, 0, :], low[0:64, 0, :], ACT.Tanh).then_inc(low_act, 1)
            act.activation(low[:, 1:3, :], low[:, 1:3, :], ACT.Sigmoid).then_inc(low_act, 1)
            for n in range(6):
                act.wait_ge(lora_mm, n + 1)
                for j in range(2):
                    f = 2 * (n % 2) + j
                    src = prod[:, n % 2, j * T:(j + 1) * T]
                    if n < 4:
                        dst, base = ((e2, vcol("decay", f)), (aa_fm, vcol("aaa", f)))[n // 2]
                        mv = act.activation(dst[:, f, :], src, ACT.Sigmoid, bias=base)
                    else:
                        mv = act.activation(g_fm[:, f, :], src, ACT.Copy)
                mv.then_inc(lora_out, 1)
            root("kk", e1, e1)
            act.wait_ge(logw_ready, 1)
            act.activation(a_til, a_til, ACT.Exp)
            act.activation(r_til, cum, ACT.Exp)
            act.activation(b_til, cum, ACT.Exp, scale=-1.0)
            act.activation(bh_fm, bh_fm, ACT.Exp).then_inc(exp_ready, 1)
            for b in range(PAIR):
                rounded("gate2", b)
            rounded_take("gate2", 16, lambda b: gates2[:, b, :], ACT.Sigmoid)
            root("gn", y_rs, y_rs)
            for b in range(PAIR):
                rounded("moe", b)
            norm_root("ln0")
            act.wait_ge(max_ready, 1)
            for x in range(NX):
                act.activation(g8m[:, x, 0:4], logit[:, x, 0:4], ACT.Exp, bias=st[:, 104 + x:105 + x],
                               accum_out=st[:, 106 + x:107 + x])
            act.activation(st[:, 112:114], st[:, 110:112], ACT.Exp).then_inc(moe_exp, 1)
            def silu(b, e, i=0):
                act.wait_ge(w_used, BASE["moe"] + b + 2 + 12 * i)
                act.activation(h_sig[:, e % 2, :], prod[:, 0, :], ACT.Silu).then_inc(silu_ready, 1)

            for e in range(2):
                for b in range(4 * e, 4 * e + 4):
                    if b >= PAIR:
                        rounded("moe", b)
                silu(4 * e, e)
            with act.Fori(0, (NEXP - 2) // 2) as i:
                for j in range(2):
                    for b in range(8 + 6 * j, 14 + 6 * j):
                        rounded("moe", b, i, 12)
                    silu(10 + 6 * j, j, i)
            for b in range(6 * NEXP - 4, 6 * NEXP):
                rounded("moe", b)
            act.wait_ge(w_used, BASE["ple_proj"] + 2)
            for n in range(4):
                mv = act.activation(ple[:, n // 2, (n % 2) * 512:(n % 2 + 1) * 512], acc[:, n, :], ACT.Copy)
            mv.then_inc(acc_out, 1)
            norm_root("ln1")
            act.wait_ge(w_used, BASE["ple_gate"] + 8)
            for n in range(4):
                mv = act.activation(sig_ple[:, n // 2, (n % 2) * 512:(n % 2 + 1) * 512], acc[:, n, :], ACT.Sigmoid)
            mv.then_inc(ple_sig, 1)
            norm_root("ln2")

        @block.vector
        def _(dve):
            chain = [0]
            taken = [0]

            def link(ins):
                chain[0] += 1
                ins.then_inc(v_chain, 1)
                dve.wait_ge(v_chain, chain[0])

            def group():
                dve.wait_ge(gen_mm, taken[0] + 1)
                taken[0] += 1
                return gen[:, (taken[0] - 1) % 2, :]

            def wide(ap, axis, n):
                shape = list(ap.shape)
                shape.insert(axis, n)
                return ap.unsqueeze(axis).broadcast_to(shape)

            def rstd(name):
                dve.wait_ge(root_ready, ROOT[name])
                link(dve.reciprocal(st[:, 6:8], st[:, 4:6]))

            def mean_square(eps):
                for x in range(NX):
                    link(dve.tensor_tensor_reduce(ln_sq, resid[:, x, :], resid[:, x, :], 1.0, 0.0, ALU.mult, ALU.add,
                                                  st[:, x:x + 1]))
                dve.tensor_scalar(st[:, 2:4], st[:, 0:2], 1.0 / D, eps, ALU.mult, ALU.add).then_inc(ms_ready, 1)

            def rms_norm(name):
                mean_square(EPS)
                rstd(name)
                for x in range(NX):
                    last = dve.tensor_scalar(xn[:, x, :], resid[:, x, :], st[:, 6 + x:7 + x], None, ALU.mult)
                last.then_inc(normed, 1)

            def layer_norm(name, arrived, out_sem):
                link(dve.tensor_reduce(st[:, 8:10], resid[:, :, :], AX, ALU.add))
                link(dve.tensor_scalar(st[:, 10:12], st[:, 8:10], -1.0 / D, None, ALU.mult))
                for x in range(NX):
                    c = dve.tensor_scalar(resid[:, x, :], resid[:, x, :], st[:, 10 + x:11 + x], None, ALU.add)
                link(c)
                mean_square(LN_EPS)
                rstd(name)
                dve.wait_ge(gain_in[1], arrived)
                for x in range(NX):
                    c = dve.scalar_tensor_tensor(resid[:, x, :], resid[:, x, :], st[:, 6 + x:7 + x], gains[:, 1, :],
                                                 ALU.mult, ALU.mult)
                link(c)
                link(dve.tensor_tensor(resid[:, :, :], resid[:, :, :], wide(gains[:, 2, :], 1, NX), ALU.add))
                dve.sem_inc(gain_used, 1)
                dve.sem_inc(out_sem, 1)

            def take_fm(dst, tiles, gain=None, split=False):
                for x in range(NX):
                    for q in range(tiles // 4):
                        bank = group().rearrange("p (a b) -> p a b", b=P)
                        out_ = dst[:, 4 * q:4 * q + 4, x * P:(x + 1) * P]
                        if gain is None:
                            c = dve.tensor_copy(out_, bank)
                        else:
                            c = dve.tensor_tensor(out_, bank, wide(vcol(gain, 4 * q, 4), 2, P), ALU.mult)
                        link2(c)
                        if split:
                            hi, lo = (t[:, 4 * q:4 * q + 4, x * P:(x + 1) * P] for t in (xh, xl))
                            link(dve.tensor_copy(hi, out_))
                            link(dve.tensor_tensor(lo, out_, hi.bitcast(F32), ALU.subtract))
                dve.sem_inc(fm_ready, 1)

            def link2(ins):
                ins.then_inc(gen_out, 1)
                dve.wait_ge(gen_out, taken[0])

            def add_acc(scale):
                for x in range(NX):
                    c = dve.scalar_tensor_tensor(resid[:, x, :], resid[:, x, :], scale,
                                                 acc[:, 2 * x:2 * x + 2, :].rearrange("p a b -> p (a b)"), ALU.mult, ALU.add)
                c.then_inc(acc_out, 1)
                dve.wait_ge(acc_out, acc_uses[0])

            acc_uses = [0]

            dve.wait_ge(small_in, 32)
            dve.wait_ge(x_in, 16)
            rms_norm("mix0")
            take_fm(xT, KD, "mix0")
            dve.wait_ge(table_b_in, 16)
            for n in range(8):
                dve.wait_ge(fm_out, 2 * n + 2)
                pair = qk1[:, 2 * n:2 * n + 2, :]
                bank = group().rearrange("p (a b) -> p a b", b=T)
                dve.tensor_tensor(rope_tmp, bank, wide(cb("sin"), 1, 2), ALU.mult).then_inc(gen_out, 1)
                link(dve.tensor_tensor(pair, pair, wide(cb("cos"), 1, 2), ALU.mult))
                dve.tensor_tensor(pair, pair, rope_tmp, ALU.add).then_inc(roped, 1)
                dve.wait_ge(roped, n + 1)

            def soft(scores, s, scale, bias_of, mask_band):
                for h in range(4):
                    dve.wait_ge(att_s, scores + h + 1)
                    link(dve.scalar_tensor_tensor(s[:, h, :], acc[:, h, 0:ATT_COLS], scale, bias_of(h), ALU.mult, ALU.add))
                    if h == 3:
                        dve.sem_inc(acc_out, 1)
                    if mask_band:
                        dve.memset(s[0:64, h, 64:P], NEG)
                        link(dve.memset(s[0:64, h, 2 * P + 64:3 * P], NEG))
                    dve.tensor_reduce(st[:, 32 + h:33 + h], s[:, h, 0:P], AX, ALU.max)
                    link(dve.tensor_reduce(st[:, 36 + h:37 + h], s[:, h, P:ATT_COLS], AX, ALU.max))
                    dve.tensor_scalar(st[:, 16 + h:24:4], st[:, 32 + h:40:4], -1.0, None, ALU.mult).then_inc(att_m, 1)

            def probs_T(pT):
                for h in range(4):
                    bank = group()
                    link2(dve.tensor_copy(pT[:, h, :], bank[:, 0:ATT_COLS]))
                    dve.sem_inc(att_pt, 1)

            def take_heads(n, soft_count, dst, width):
                dve.wait_ge(att_p, soft_count)
                link(dve.reciprocal(st[:, 32:40], st[:, 24:32]))
                dve.wait_ge(att_o, n)
                for x in range(NX):
                    c = dve.tensor_tensor(dst(x).rearrange("p (a b) -> p a b", b=width),
                                          prod[:, x, 0:4 * width].rearrange("p (a b) -> p a b", b=width),
                                          wide(st[:, 32 + 4 * x:36 + 4 * x], 2, width), ALU.mult)
                c.then_inc(att_done, 1)

            soft(0, sc1, HD1 ** -0.5, lambda h: cb("causal"), False)
            probs_T(pT1)
            take_heads(1, 4, lambda x: cat1[:, x, 0:512], HD1)
            for h in range(4):
                dve.wait_ge(att_s, 5 + h)
                c = dve.tensor_tensor(rT1[:, h, :], acc[:, h, 0:ATT_COLS],
                                      cb("decay")[:, h * ATT_COLS:(h + 1) * ATT_COLS], ALU.mult)
                c.then_inc(att_pt, 1)
            dve.wait_ge(att_pt, 8)
            dve.sem_inc(acc_out, 1)
            dve.wait_ge(att_o, 2)
            for x in range(NX):
                c = dve.tensor_copy(cat1[:, x, 512:D], prod[:, x, :])
            c.then_inc(att_done, 1)
            dve.wait_ge(att_done, 2)
            ret = cat1[:, :, 512:D]
            link(dve.tensor_tensor(ret_sq, ret, ret, ALU.mult))
            for x in range(NX):
                c = dve.tensor_reduce(st[:, 40 + 4 * x:44 + 4 * x], ret_sq[:, x, :].rearrange("p (a b) -> p a b", b=HD1),
                                      AX, ALU.add)
            link(c)
            dve.tensor_scalar(st[:, 48:56], st[:, 40:48], 1.0 / HD1, EPS, ALU.mult, ALU.add).then_inc(ms_ready, 1)
            dve.wait_ge(root_ready, ROOT["ret"])
            link(dve.reciprocal(st[:, 64:72], st[:, 56:64]))
            for x in range(NX):
                v = cat1[:, x, 512:D].rearrange("p (a b) -> p a b", b=HD1)
                c = dve.tensor_tensor(v, v, wide(st[:, 64 + 4 * x:68 + 4 * x], 2, HD1), ALU.mult)
            link(c)
            dve.wait_ge(acc_out, 2)
            dve.tensor_tensor(ret, ret, g_ret, ALU.mult).then_inc(normed, 1)
            take_fm(xT, KD)
            dve.wait_ge(w_used, BASE["even_out"] + 8)
            acc_uses[0] = 5
            add_acc(1.0)

            def top16(vals, idx, src, n):
                for r in range(2):
                    lo = slice(8 * r, 8 * r + 8)
                    for m in range(n):
                        c = dve.max(vals(m)[:, lo], src(m))
                    link(c)
                    for m in range(n):
                        c = dve.max_index(idx(m)[:, lo], vals(m)[:, lo], src(m))
                    if r == 0:
                        for m in range(n):
                            c = dve.match_replace(src(m), vals(m)[:, lo], src(m), -3.0e38)
                    link(c)

            def route(x):
                top16(lambda m: top_s[:, m, :], lambda m: top_u[:, m, :].bitcast(U32), lambda m: score[:, x, m, :], 16)
                dve.tensor_copy(top_f, top_u.bitcast(U32))
                c4 = cand.rearrange("p h (a b) -> p h a b", b=TOPK)
                link(dve.tensor_tensor(c4, wide(top_s[:, 0::2, :], 3, TOPK), wide(top_s[:, 1::2, :], 2, TOPK), ALU.add))
                top16(lambda m: sel_s[:, x, m, :], lambda m: pos_u[:, m, :].bitcast(U32), lambda m: cand[:, m, :], PEER_H)
                for n, (op, by) in enumerate(((ALU.logical_shift_right, 4), (ALU.bitwise_and, TOPK - 1))):
                    link(dve.tensor_scalar(pos_a.bitcast(U32), pos_u.bitcast(U32), by, None, op))
                    link(dve.tensor_copy(pos_f, pos_a.bitcast(U32)))
                    flat = pos_f.rearrange("p h k -> p (h k)")
                    link(dve.tensor_tensor(pick, wide(iota[:, 0:TOPK], 1, P), wide(flat, 2, TOPK), ALU.is_equal))
                    p4 = pick.rearrange("p (h k) a -> p h k a", k=TOPK)
                    link(dve.tensor_tensor(p4, p4, wide(top_f[:, n::2, :], 2, TOPK), ALU.mult))
                    link(dve.tensor_reduce(sel_i[:, n, x, :], pick, AX, ALU.add))
                g = sel_i[:, 2, x, :].rearrange("p (h k) -> p h k", k=TOPK)
                return dve.tensor_tensor(g, sel_s[:, x, :, :], wide(sel_s[:, x, :, 0], 2, TOPK), ALU.subtract)

            def peer(layer):
                rms_norm(f"ffn{layer}")
                take_fm(xT, KD, f"ffn{layer}", split=True)
                for b in range(2):
                    for x in range(NX):
                        for q in range(2):
                            bank = group().rearrange("p (a b) -> p a b", b=NK)
                            link2(dve.tensor_copy(score[:, x, 8 * b + 4 * q:8 * b + 4 * q + 4, :], bank))
                for x in range(NX):
                    last = route(x)
                last.then_inc(topk_ready, 1)
                dve.wait_ge(gate_exp, layer + 1)
                gate = sel_i[:, 2, :, :].rearrange("p x (h k) -> p (x h) k", k=TOPK)
                link(dve.tensor_reduce(st[:, 16:32], gate, AX, ALU.add))
                link(dve.reciprocal(st[:, 32:48], st[:, 16:32]))
                dve.tensor_tensor(gate, gate, wide(st[:, 32:48], 2, TOPK), ALU.mult).then_inc(normed, 1)
                for x in range(NX):
                    bank = group()
                    link2(dve.tensor_copy(hk[:, 0:3, x * P:(x + 1) * P],
                                          bank[:, 0:3 * P].rearrange("p (a b) -> p a b", b=P)))
                gate_hi = mid_lo[:, 0:T]
                link(dve.tensor_copy(gate_hi, hk[:, 2, :]))
                link(dve.tensor_tensor(hk[:, 3, :], hk[:, 2, :], gate_hi.bitcast(F32), ALU.subtract))
                link(dve.tensor_copy(hk[:, 2, :], gate_hi.bitcast(F32)))

                def chunk_rest(n, i):
                    dve.wait_ge(hh_ready, layer * NK + n + 1 + RING * i)
                    dve.tensor_tensor(hid_lo[:, n % RING, :], hid[:, n + RING * i, :], hid_hi[:, n % RING, :].bitcast(F32),
                                      ALU.subtract).then_inc(hl_ready, 1)

                for half in range(2):
                    dve.wait_ge(fm_out, FMBASE[f"peer_u{layer}"] + (half + 1) * HALF)
                    before, chained = (2 * layer + half) * HALF, chain[0]
                    with dve.Fori(0, HALF // RING) as i:
                        for j in range(RING):
                            tok = bass.ds(GTOK * j + GTOK * RING * i, GTOK)
                            hi, lo = hot2[:, 0, :, :], hot2[:, 1, :, :]
                            dve.tensor_tensor(hi, wide(iota[:, half * HALF:(half + 1) * HALF], 1, GTOK),
                                              wide(hk[:, 1, tok], 2, HALF), ALU.is_equal).then_inc(v_chain, 1)
                            dve.tensor_tensor(hot1[:, :, :], wide(iota, 1, GTOK), wide(hk[:, 0, tok], 2, NK), ALU.is_equal)
                            dve.wait_ge(v_chain, chained + 2 * j + 1 + 2 * RING * i)
                            dve.tensor_tensor(lo, hi.bitcast(F32), wide(hk[:, 3, tok], 2, HALF), ALU.mult).then_inc(v_chain, 1)
                            dve.wait_ge(v_chain, chained + 2 * j + 2 + 2 * RING * i)
                            dve.tensor_tensor(hi, hi.bitcast(F32), wide(hk[:, 2, tok], 2, HALF), ALU.mult).then_inc(hot_ready, 1)
                            if half == 1:
                                chunk_rest(j, i)
                            dve.wait_ge(tok_mm, before + j + 1 + RING * i)
                            h = hid[:, half * HALF:(half + 1) * HALF, tok]
                            dve.tensor_tensor(h, h, gen[:, 0, 0:GTOK * HALF].rearrange("p (t c) -> p c t", c=HALF), ALU.mult)\
                                .then_inc(gated, 1)
                    chain[0] += 2 * HALF
                with dve.Fori(HALF // RING, NK // RING) as i:
                    for j in range(RING):
                        chunk_rest(j, i)
                for x in range(NX):
                    for q in range(2):
                        bank = group()
                        r = resid[:, x, 512 * q:512 * q + 512]
                        link2(dve.tensor_tensor(r, r, bank, ALU.add))

            peer(0)
            rms_norm("mix1")
            take_fm(xT, KD, "mix1", split=True)
            dve.memset(cv_u[:, :, 0:2], 0.0)
            for k in range(KD):
                dve.wait_ge(fm_out, FMBASE["odd_in"] + 3 * k + 3)
                link(dve.tensor_tensor(cv_u[:, k, 2:T + 2], cv_c[:, k, :], cv_h[:, k, :], ALU.mult))
                link(dve.tensor_scalar(cv_y[:, k, :], cv_u[:, k, 0:T], vcol("conv", k), None, ALU.mult))
                for w in (1, 2):
                    link(dve.scalar_tensor_tensor(cv_y[:, k, :], cv_u[:, k, w:w + T], vcol("conv", 8 * w + k),
                                                  cv_y[:, k, :], ALU.mult, ALU.add))
                c = dve.tensor_tensor(cv_z[:, k, :], cv_b[:, k, :], cv_y[:, k, :], ALU.mult)
            c.then_inc(fm_ready, 1)
            dve.wait_ge(w_used, BASE["odd_out"] + 8)
            acc_uses[0] = 7
            add_acc(1.0)
            peer(1)
            dve.sem_inc(arena_free, 1)
            mean_square(EPS)
            rstd("final")
            dve.wait_ge(gain_in[0], 16)
            for x in range(NX):
                c = dve.scalar_tensor_tensor(resid[:, x, :], resid[:, x, :], st[:, 6 + x:7 + x], gains[:, 0, :],
                                             ALU.mult, ALU.mult)
            c.then_inc(gain_used, 1)
            dve.wait_ge(gain_used, 1)
            layer_norm("ln_in", 32, normed)
            take_fm(xT2, KD, split=True)
            dve.wait_ge(block2_in, 80)
            soft(8, sc2, HD2 ** -0.5, lambda h: band_bias[:, h, :], True)
            link(dve.memset(cols[:, :, 0:1], 0.0))
            dve.wait_ge(fm_out, FMBASE["gate2"])
            dve.tensor_tensor(rkv, cols[:, 0:12, 0:T], cols[:, 0:12, 1:T + 1], ALU.subtract)
            link(dve.tensor_tensor(low, cols[:, 12:15, 0:T], cols[:, 12:15, 1:T + 1], ALU.subtract))
            for n in range(RW_TILES):
                v = rkv[:, n, :] if n < 12 else low[:, n - 12, :]
                c = dve.scalar_tensor_tensor(v, v, vcol("mu", n), cols[:, n, 1:T + 1], ALU.mult, ALU.add)
            link(c)
            dve.sem_inc(shifted, 1)
            probs_T(pT2)
            take_heads(3, 8, lambda x: ob2[:, x, 0:256], HD2)
            soft(12, sc2, HD2 ** -0.5, lambda h: band_bias[:, 4 + h, :], True)
            probs_T(pT2)
            take_heads(4, 12, lambda x: ob2[:, x, 256:512], HD2)
            dve.wait_ge(att_done, 4)
            dve.sem_inc(normed, 1)
            take_fm(ya_fm, 4)
            for pr in range(4):
                c = dve.tensor_scalar(kk_fm[:, pr, :], k_fm[:, pr, :], vcol("k_k", pr), None, ALU.mult)
            link(c)
            dve.tensor_tensor(e1, kk_fm, kk_fm, ALU.mult).then_inc(sq_ready, 1)
            for q in range(2):
                bank = group().rearrange("p (a b) -> p a b", b=T)
                link2(dve.tensor_scalar(e1[:, 2 * q:2 * q + 2, :], bank, 1e-24, None, ALU.max))
            dve.sem_inc(ms_ready, 1)
            dve.wait_ge(root_ready, ROOT["kk"])
            link(dve.reciprocal(e1, e1))
            link(dve.tensor_tensor(kk_fm, kk_fm, e1, ALU.mult))
            dve.wait_ge(lora_out, 6)
            for pr in range(4):
                c = dve.tensor_scalar(e1[:, pr, :], aa_fm[:, pr, :], -1.0, vcol("k_a", pr), ALU.add, ALU.mult)
            link(c)
            link(dve.scalar_tensor_tensor(k_fm, e1, 1.0, k_fm, ALU.add, ALU.mult))
            link(dve.memset(start, 1.0))
            link(dve.memset(start[:, ::CH], 0.0))
            link(dve.tensor_scalar(e1, e2, -float(np.exp(-0.5)), None, ALU.mult))
            for pr in range(4):
                c = dve.tensor_tensor_scan(cum[:, pr, :], start, e1[:, pr, :], 0.0, ALU.mult, ALU.add)
            link(c)
            dve.tensor_tensor(a_til, cum, e1, ALU.subtract)
            for pr in range(4):
                cpr = cum[:, pr, :].rearrange("p (c t) -> p c t", t=CH)
                c = dve.tensor_tensor(bh_fm[:, pr, :].rearrange("p (c t) -> p c t", t=CH),
                                      wide(cpr[:, :, CH - 1], 2, CH), cpr, ALU.subtract)
            c.then_inc(logw_ready, 1)
            dve.wait_ge(exp_ready, 1)
            for pr in range(4):
                c = dve.tensor_copy(st[:, 72 + NCH * pr:72 + NCH * (pr + 1)], r_til[:, pr, CH - 1::CH])
            link(c)
            dve.scalar_tensor_tensor(a_til, a_til, -1.0, kk_fm, ALU.mult, ALU.mult)
            link(dve.tensor_tensor(kk_fm, kk_fm, aa_fm, ALU.mult))
            dve.tensor_tensor(k_til, b_til, k_fm, ALU.mult)
            dve.tensor_tensor(kh_fm, bh_fm, k_fm, ALU.mult)
            dve.tensor_tensor(b_til, b_til, kk_fm, ALU.mult)
            dve.tensor_tensor(bh_fm, bh_fm, kk_fm, ALU.mult)
            link(dve.tensor_tensor(r_til, r_til, r_fm, ALU.mult))
            dve.sem_inc(fm_ready, 1)
            for x in range(NX):
                for dst in (a_tm, bh_tm, kh_tm, v_tm):
                    bank = group()
                    link2(dve.tensor_copy(dst[:, x, :], bank))
            m_lT, m_l, m_ak, m_rb, m_rk, m_off, m_a, m_b = mats

            def masked(dst, mask, also=None):
                for q in range(2):
                    bank = group().rearrange("p (a b) -> p a b", b=P)
                    if also is not None:
                        dve.tensor_tensor(also[0][:, q::2, :], bank, wide(cc(also[1]), 1, 4), ALU.mult)
                    link2(dve.tensor_tensor(dst[:, q::2, :], bank, wide(cc(mask), 1, 4), ALU.mult))

            def stored(dst, plus=None):
                for q in range(2):
                    bank = group().rearrange("p (a b) -> p a b", b=P)
                    d = dst[:, 4 * q:4 * q + 4, :]
                    if plus is None:
                        link2(dve.tensor_copy(d, bank))
                    else:
                        link2(dve.tensor_tensor(d, plus[:, 4 * q:4 * q + 4, :], bank, ALU.add))

            for x in range(NX):
                masked(m_lT, "up16", (m_off, "off32"))
                masked(m_l, "low16")
                masked(m_ak, "up32")
                masked(m_rb, "upi32")
                masked(m_rk, "upi32")
                bank = group()
                dve.tensor_copy(sol[:, :, 0:HD2], a_tm[:, x, :].rearrange("p (a b) -> p a b", b=HD2))
                dve.tensor_tensor(m_ak, m_lT, wide(ident, 1, 8), ALU.add)
                link2(dve.tensor_copy(sol[:, :, HD2:P], bank.rearrange("p (a b) -> p a b", b=HD2)))
                stored(m_a)
                stored(m_b)
                stored(m_ak, m_ak)
                stored(m_l)
                stored(m_lT)
                stored(m_ak, m_ak)
                stored(m_a)
                stored(m_ak, m_ak)
                stored(m_b)
                stored(m_lT)
                stored(sol, m_b)
                tx = slice(x * P, (x + 1) * P)
                bank = group().rearrange("p (a b) -> p a b", b=P)
                link2(dve.tensor_tensor(q_eff[:, :, tx], bank, r_til[:, :, tx], ALU.add))
                bank = group().rearrange("p (a b) -> p a b", b=P)
                link2(dve.tensor_copy(y_fm[:, :, tx], bank))
                cs = slice(4 * x, 4 * x + 4)
                for pr in range(4):
                    c = dve.tensor_tensor(step_m[:, pr, cs, :], wide(cc("eye64"), 1, 4),
                                          wide(st[:, 72 + NCH * pr + 4 * x:76 + NCH * pr + 4 * x], 2, HD2), ALU.mult)
                link(c)
                for c in range(4 * x, 4 * x + 4):
                    bank = group().rearrange("p (n a b) -> p n a b", n=2, b=HD2)
                    dve.tensor_tensor(step_m[:, :, c, :], step_m[:, :, c, :], bank[:, 0], ALU.add)
                    link2(dve.tensor_copy(step_n[:, :, c, :], bank[:, 1]))
            dve.tensor_copy(state[:, 1, :, :], step_n[:, :, 0, :]).then_inc(state_ready, 1)
            for c in range(1, NCH - 1):
                bank = group()[:, 0:4 * HD2].rearrange("p (a b) -> p a b", b=HD2)
                link2(dve.tensor_tensor(state[:, c + 1, :, :], step_n[:, :, c, :], bank, ALU.add))
                dve.sem_inc(state_ready, 1)
            for q in range(2):
                bank = group().rearrange("p (a b) -> p a b", b=T)
                d = y_fm[:, 2 * q:2 * q + 2, CH:T]
                link2(dve.tensor_tensor(d, d, bank[:, :, CH:T], ALU.add))
            dve.sem_inc(sq_ready, 1)
            for q in range(2):
                bank = group().rearrange("p (a b) -> p a b", b=T)
                link2(dve.scalar_tensor_tensor(y_tmp[:, 2 * q:2 * q + 2, :], bank, -1.0 / HD2, y_fm[:, 2 * q:2 * q + 2, :],
                                               ALU.mult, ALU.add))
            dve.tensor_tensor(y_sq, y_tmp, y_tmp, ALU.mult).then_inc(sq_ready, 1)
            for pr in range(4):
                c = dve.scalar_tensor_tensor(bonus[:, pr, :], r_fm[:, pr, :], vcol("r_k", pr), k_fm[:, pr, :],
                                             ALU.mult, ALU.mult)
            for q in range(2):
                bank = group().rearrange("p (a b) -> p a b", b=T)
                link2(dve.tensor_scalar(y_rs[:, 2 * q:2 * q + 2, :], bank, 1.0 / HD2, GN_EPS, ALU.mult, ALU.add))
            dve.sem_inc(sq_ready, 1)
            dve.sem_inc(ms_ready, 1)
            for q in range(2):
                bank = group().rearrange("p (a b) -> p a b", b=T)
                h = slice(2 * q, 2 * q + 2)
                link2(dve.tensor_tensor(y_mu[:, h, :], bank, v_fm[:, h, :], ALU.mult))
            dve.wait_ge(root_ready, ROOT["gn"])
            link(dve.reciprocal(y_rs, y_rs))
            link(dve.tensor_tensor(y_tmp, y_tmp, y_rs, ALU.mult))
            for pr in range(4):
                c = dve.tensor_scalar(y_tmp[:, pr, :], y_tmp[:, pr, :], vcol("gn_g", pr), vcol("gn_b", pr), ALU.mult, ALU.add)
            link(c)
            link(dve.tensor_tensor(y_tmp, y_tmp, y_mu, ALU.add))
            dve.tensor_tensor(y_out, y_tmp, g_fm, ALU.mult).then_inc(fm_ready, 1)
            for j in range(4):
                h = slice(2 * j, 2 * j + 2)
                for n, dst in enumerate((mixT[:, h, :], mix_tmp)):
                    dve.wait_ge(w_used, BASE["branch"] + 2 * j + n + 1)
                    c = dve.tensor_tensor(dst, gates2[:, 8 * n + 2 * j:8 * n + 2 * j + 2, :],
                                          prod[:, n, :].rearrange("p (a b) -> p a b", b=T), ALU.mult)
                c.then_inc(branch_out, 1)
                dve.wait_ge(branch_out, j + 1)
                link(dve.tensor_tensor(mixT[:, h, :], mixT[:, h, :], mix_tmp, ALU.add))
            dve.sem_inc(fm_ready, 1)
            dve.wait_ge(w_used, BASE["out2"] + 8)
            acc_uses[0] = 12
            add_acc(ALPHA)
            layer_norm("ln0", 64, normed)
            take_fm(xT2, KD, split=True)
            bank = group()[:, 0:NX * 36].rearrange("p (a b) -> p a b", b=36)
            link2(dve.tensor_tensor(logit, bank, wide(router_b, 1, NX), ALU.add))
            link(dve.memset(g8, -3.0e38))
            link(dve.tensor_copy(g8[:, :, 0:4], logit[:, :, 0:4]))
            for x in range(NX):
                c = dve.max(sel8m[:, x, :], g8[:, x, :])
            link(c)
            for x in range(NX):
                c = dve.max_index(g8i[:, x, :].bitcast(U32), sel8m[:, x, :], g8[:, x, :])
            link(c)
            dve.tensor_scalar(st[:, 104:106], sel8m[:, :, 0], -1.0, None, ALU.mult)
            link(dve.tensor_copy(sel8f, g8i.bitcast(U32)))
            for x in range(NX):
                c = dve.tensor_scalar(hot_g[:, x, :], cc("iota8"), sel8f[:, x, 0:1], None, ALU.is_equal)
            link(c)
            elog = logit[:, :, 4:36].rearrange("p x (g e) -> p x e g", e=8)
            for x in range(NX):
                c = dve.tensor_tensor(sel_t[:, x, :, :], elog[:, x, :, :], wide(hot_g[:, x, 0:4], 1, 8), ALU.mult)
            link(c)
            link(dve.tensor_reduce(sel8, sel_t, AX, ALU.add))
            for x in range(NX):
                c = dve.max(sel8m[:, x, :], sel8[:, x, :])
            link(c)
            for x in range(NX):
                c = dve.max_index(sel8i[:, x, :].bitcast(U32), sel8m[:, x, :], sel8[:, x, :])
            link(c)
            dve.tensor_copy(sel8f, sel8i.bitcast(U32))
            link(dve.tensor_tensor(st[:, 110:112], sel8m[:, :, 1], sel8m[:, :, 0], ALU.subtract))
            dve.sem_inc(max_ready, 1)
            dve.wait_ge(moe_exp, 1)
            link(dve.tensor_scalar(st[:, 118:120], st[:, 112:114], 1.0, None, ALU.add))
            link(dve.tensor_tensor(st[:, 118:120], st[:, 118:120], st[:, 106:108], ALU.mult))
            link(dve.reciprocal(st[:, 114:116], st[:, 118:120]))
            link(dve.tensor_tensor(st[:, 116:118], st[:, 114:116], st[:, 112:114], ALU.mult))
            for x in range(NX):
                dve.tensor_scalar(comb8[:, x, :], cc("iota8"), sel8f[:, x, 0:1], st[:, 114 + x:115 + x],
                                  ALU.is_equal, ALU.mult)
                c = dve.tensor_scalar(comb8b[:, x, :], cc("iota8"), sel8f[:, x, 1:2], st[:, 116 + x:117 + x],
                                      ALU.is_equal, ALU.mult)
            link(c)
            link(dve.tensor_tensor(comb8, comb8, comb8b, ALU.add))
            for x in range(NX):
                c = dve.tensor_tensor(comb[:, x, :].rearrange("p (g e) -> p g e", e=8), wide(comb8[:, x, :], 1, 4),
                                      wide(hot_g[:, x, 0:4], 2, 8), ALU.mult)
            c.then_inc(normed, 1)
            bank = group()
            link2(dve.tensor_copy(combT[0:NEXP, :], bank[0:NEXP, 0:T]))
            dve.tensor_tensor(comb_d[0:NEXP, :, :], wide(combT[0:NEXP, :], 1, NEXP), wide(ident[0:NEXP, 0:NEXP], 2, T),
                              ALU.mult).then_inc(fm_ready, 1)
            eb = BASE["moe"]

            def weigh(e, i, chained):
                first = eb if e == 0 else eb + 4 + 6 * (e - 1)
                mid = h_mid[:, e % 2, :]
                c = chained + 3 * e + 6 * i
                dve.wait_ge(silu_ready, e + 1 + 2 * i)
                dve.wait_ge(w_used, first + 4 + 12 * i)
                dve.tensor_tensor(mid, h_sig[:, e % 2, :], prod[:, 1, :], ALU.mult).then_inc(v_chain, 1)
                dve.wait_ge(v_chain, c + 1)
                dve.wait_ge(comb_mm, e + 1 + 2 * i)
                m2 = mid.rearrange("p (a b) -> p a b", b=T)
                dve.tensor_tensor(m2, m2, wide(gen[:, 0, 0:T], 1, 2), ALU.mult).then_inc(v_chain, 1)
                if e:
                    dve.wait_ge(w_used, first + 6 + 12 * i)
                dve.wait_ge(v_chain, c + 2)
                dve.tensor_copy(mid_hi, mid).then_inc(v_chain, 1)
                dve.wait_ge(v_chain, c + 3)
                dve.tensor_tensor(mid_lo, mid, mid_hi.bitcast(F32), ALU.subtract).then_inc(mid_ready, 1)

            chained = chain[0]
            weigh(0, 0, chained)
            weigh(1, 0, chained)
            with dve.Fori(0, (NEXP - 2) // 2) as i:
                for j in range(2):
                    weigh(2 + j, i, chained)
            chain[0] += 3 * NEXP
            dve.wait_ge(w_used, eb + 6 * NEXP)
            acc_uses[0] = 13
            add_acc(ALPHA)
            layer_norm("ln1", 96, normed)
            take_fm(xT2, KD)
            dve.wait_ge(acc_out, 14)
            dve.wait_ge(ple_sig, 1)
            link(dve.tensor_tensor(ple, ple, sig_ple, ALU.mult))
            link(dve.scalar_tensor_tensor(resid[:, :, :], resid[:, :, :], ALPHA, ple, ALU.mult, ALU.add))
            layer_norm("ln2", 128, normed)


def _fm(w):
    n = w.shape[1] // P
    return w.reshape(KD, P, n, P).transpose(2, 1, 0, 3).reshape(n, P, BLK)


def _tm(w):
    k, n = w.shape[0] // (2 * P), w.shape[1] // 512
    return w.reshape(k, 2, P, n, 512).transpose(3, 0, 2, 1, 4).reshape(n * k, P, BLK)


def _col(v, tiles):
    return v.reshape(tiles, P).T


def _layout(i):
    a = {}
    w = i["even_w_in"][0]
    a["even_qk"] = _fm(np.concatenate([w[:, 0:1024], w[:, 1536:2560]], axis=1))
    a["even_vg"] = _tm(np.concatenate([w[:, 1024:1536], w[:, 2560:3584]], axis=1))
    a["even_out"] = _tm(i["even_w_out"][0])
    a["odd_in"] = _fm(i["odd_w_in"][0].reshape(D, 3, KD, P).transpose(0, 2, 1, 3).reshape(D, 3 * D))
    a["odd_out"] = _tm(i["odd_w_out"][0])
    for n in range(LAYERS):
        a[f"peer_q{n}"] = _fm(i["peer_w_q"][n])
        a[f"peer_keys{n}"] = i["peer_sub_keys"][n].reshape(2, 8, NK, P).transpose(0, 3, 1, 2).reshape(2, P, BLK)
        a[f"peer_u{n}"] = i["peer_u"][n].reshape(NK, NK, KD, P).transpose(1, 3, 2, 0).reshape(NK, P, BLK)
    a["peer_v"] = i["peer_v"]
    w = i["w_in_2"][0]
    a["qk2"] = _fm(w[:, 0:1024])
    a["v2"] = _tm(w[:, 1024:1536])
    a["rw2"] = _fm(np.pad(w[:, 1536:3360], ((0, 0), (0, RW_TILES * P - 1824))))
    a["gate2"] = _fm(w[:, 3360:])
    for name, key in (("branch_a", "w_branch_attn_2"), ("branch_r", "w_branch_rwkv_2")):
        a[name] = i[key][0].reshape(4, P, 4, 2, P).transpose(2, 1, 0, 3, 4).reshape(4, P, BLK)
    a["out2"] = _tm(i["w_out_2"][0])
    for name, key in (("exp_gate", "exp_gate_2"), ("exp_up", "exp_up_2")):
        a[name] = i[key][0].reshape(NEXP, KD, P, 2, P).transpose(0, 3, 2, 1, 4).reshape(2 * NEXP, P, BLK)
    a["exp_down"] = i["exp_down_2"][0].reshape(2 * NEXP, P, BLK)
    a["ple_proj"] = _tm(i["ple_proj_2"][0])
    a["ple_gate"] = _tm(i["ple_gate_2"][0])
    a["x"] = i["x"]
    a["const_a"], a["const_b"], a["const_c"] = constant_tables()
    vec = [_col(i["norm_mix"][0], 8), _col(i["norm_mix"][1], 8), _col(i["norm_ffn"][0], 8), _col(i["norm_ffn"][1], 8)]
    vec += [_col(i["odd_conv"][0][w], 8) for w in range(3)]
    vec += [_col(np.pad(i["tok_mix_2"][0], (0, RW_TILES * P - 1824)), RW_TILES)]
    vec += [_col(i[k][0].reshape(-1), 4) for k in ("decay_base_2", "aaa_base_2", "k_k_2", "k_a_2", "r_k_2", "gn_g_2", "gn_b_2")]
    a["vec"] = np.concatenate(vec, axis=1)
    a["final_norm"] = i["final_norm"]
    a["ln_in_g"], a["ln_in_b"] = i["ln_in_g_2"], i["ln_in_b_2"]
    a["ln_g"], a["ln_b"] = i["ln_g_2"][0], i["ln_b_2"][0]
    both = np.concatenate([i["router_grp_2"][0], i["router_exp_2"][0]], axis=1)
    a["router"] = both.reshape(KD, P, 36).transpose(1, 0, 2)
    a["router_b"] = np.concatenate([i["router_grp_bias_2"][0], i["router_exp_bias_2"][0]])
    lora = np.zeros((P, 3, 512), np.float32)
    lora[0:64, 0], lora[64:128, 0] = i["decay_up_2"][0], i["aaa_up_2"][0]
    lora[:, 1], lora[0:32, 2] = i["gate_up_2"][0][0:128], i["gate_up_2"][0][128:160]
    a["lora"] = lora
    pos = np.arange(T)
    place = np.clip(pos[:, None] - pos[None, :], -128, 128) + 128
    place = np.concatenate([place[0:P, 0:P], place[P:T, :]], axis=1)
    a["band_bias"] = i["rel_bias_2"][:, place].transpose(1, 0, 2)
    a["p"] = i["p_2"][0, 0].reshape(T, 2, P).transpose(2, 1, 0)
    return {k: np.ascontiguousarray(v) for k, v in a.items()}


def kernel(**inputs):
    from concourse.bacc import Bacc
    from concourse.bass_utils import run_bass_kernel_spmd

    arrays = _layout({k: np.asarray(v) for k, v in inputs.items()})
    nc = Bacc("TRN2", target_bir_lowering=False, num_devices=1)
    dram = {k: nc.dram_tensor(f"in_{k}", v.shape, mybir.dt.from_np(v.dtype), kind="ExternalInput").ap()
            for k, v in arrays.items()}
    out = nc.dram_tensor("out_x", (1, T, D), F32, kind="ExternalOutput").ap()
    build(nc, dram, out)
    r = run_bass_kernel_spmd(nc, [{f"in_{k}": v for k, v in arrays.items()}], core_ids=[0])
    return r.results[0]["out_x"]
```

```python
from contextlib import ExitStack

import numpy as np

import concourse.bass as bass
from concourse import mybir

ALU = mybir.AluOpType
ACT = mybir.ActivationFunctionType
F32 = mybir.dt.float32
F32R = mybir.dt.float32r
BF16 = mybir.dt.bfloat16
U32 = mybir.dt.uint32
AX = mybir.AxisListType.X

P = 128
T = 256
NX = T // P
D = 1024
KD = D // P
RING = 4
PAIR = 2
BLK = 1024
EPS = 1e-6
LN_EPS = 1e-5
GN_EPS = 64e-5
ALPHA = 2.0 ** 0.25
NEG = -1e30

LAYERS = 2
HEADS1 = 4
HD1 = 128
PEER_H = 8
NK = 128
TOPK = 16
HALF = NK // 2
GTOK = 4
PARTS = 3

HEADS2 = 8
HD2 = 64
RW_TILES = 15
CH = 32
NCH = T // CH
GATE_EARLY = 10
NEXP = 32
DEXP = 256
ATT_COLS = 3 * P

STREAM = [("even_qk", 16), ("even_vg", 12), ("even_out", 8)]
for _l in range(LAYERS):
    if _l == 1:
        STREAM += [("odd_in", 24), ("odd_out", 8)]
    STREAM += [(f"peer_q{_l}", 16), (f"peer_keys{_l}", 2), (f"peer_u{_l}", NK), (f"peer_v{_l}", NK)]
STREAM += [("qk2", 8), ("v2", 4), ("rw2", RW_TILES), ("gate2", 16), ("branch", 8), ("out2", 8),
           ("moe", 6 * NEXP), ("ple_proj", 2), ("ple_gate", 8)]
BASE, _n = {}, 0
for _name, _k in STREAM:
    BASE[_name] = _n
    _n += _k
FMBASE, _n = {}, 0
for _name, _k in STREAM:
    if _name in ("even_qk", "odd_in", "qk2", "rw2", "gate2") or _name[:6] in ("peer_q", "peer_u"):
        FMBASE[_name] = _n
        _n += _k
WHOLE = ("peer_keys0", "peer_keys1", "branch", "ple_proj")
SPLIT, SPLIT_BLOCKS = {}, []
for _name, _k in STREAM:
    if _name not in WHOLE:
        SPLIT[_name] = len(SPLIT_BLOCKS)
        SPLIT_BLOCKS += range(BASE[_name], BASE[_name] + _k)
SPLIT_PLACE = {g: s for s, g in enumerate(SPLIT_BLOCKS)}


def _order(*names):
    return {name: n + 1 for n, name in enumerate(names)}


NORMED = {name: NX * n for name, n in _order("mix0", "cat", "ffn0", "route0", "mix1", "ffn1", "route1", "blk2", "band", "ln0", "comb", "ln1", "ln2").items()}
FM = _order("mix0", "cat", "ffn0", "mix1", "ffn1", "blk2", "band", "til", "rwkv", "ln0", "comb", "comb_rest", "ln1")
ROOT = _order("mix0", "ret", "ffn0", "mix1", "ffn1", "final", "ln_in", "kk", "gn", "ln0", "ln1", "ln2")

VEC, _n = {}, 0
for _name, _k in (("conv", 24), ("mu", RW_TILES), ("decay", 4),
                  ("aaa", 4), ("k_k", 4), ("k_a", 4), ("r_k", 4), ("gn_g", 4), ("gn_b", 4)):
    VEC[_name] = _n
    _n += _k
NVEC = _n

CA, CB, CC = {}, {}, {}
for _tab, _items in ((CA, (("ident", 128), ("iota", 128))),
                     (CB, (("rot", 128), ("cos", T), ("sin", T), ("causal", ATT_COLS), ("decay", HEADS1 * ATT_COLS))),
                     (CC, (("up16", 128), ("low16", 128), ("off32", 128), ("up32", 128), ("upi32", 128),
                           ("ones64", 128), ("eye64", 64), ("ones", 128), ("iota8", 8)))):
    _n = 0
    for _name, _k in _items:
        _tab[_name] = (_n, _k)
        _n += _k
    _tab["all"] = (0, _n)


def constant_tables():
    f = np.float32
    i = np.arange(P)
    a = np.zeros((P, CA["all"][1]), f)
    a[:, 0:128] = np.eye(P, dtype=f)
    a[:, 128:256] = np.arange(128, dtype=f)
    b = np.zeros((P, CB["all"][1]), f)

    def put(tab, arr, name, val):
        s, n = tab[name]
        arr[:, s:s + n] = val

    rot = np.zeros((P, P), f)
    rot[i[:64] + 64, i[:64]] = -1.0
    rot[i[:64], i[:64] + 64] = 1.0
    put(CB, b, "rot", rot)
    half = HD1 // 2
    inv = (f(10000.0) ** (-np.arange(half, dtype=f) / f(half))).astype(f)
    ang = (np.arange(T, dtype=f)[:, None] * inv[None, :]).astype(f)
    put(CB, b, "cos", np.cos(ang).astype(f).T[i % half])
    put(CB, b, "sin", np.sin(ang).astype(f).T[i % half])
    causal = np.zeros((P, 3, P), f)
    causal[:, 0] = causal[:, 2] = np.where(i[None, :] <= i[:, None], 0.0, NEG)
    put(CB, b, "causal", causal.reshape(P, -1))
    dec = np.zeros((P, HEADS1, 3, P))
    for h in range(HEADS1):
        lg = np.log(1.0 - 2.0 ** (-5.0 - h))
        diff = (i[None, :] - i[:, None]).astype(np.float64)
        dec[:, h, 0] = dec[:, h, 2] = np.where(diff >= 0, np.exp(lg * np.maximum(diff, 0)), 0.0)
        dec[:, h, 1] = np.exp(lg * (diff + P))
    put(CB, b, "decay", (dec * HD1 ** -0.5).astype(f).reshape(P, -1))
    c = np.zeros((P, CC["all"][1]), f)
    s, t = i[:, None], i[None, :]
    put(CC, c, "up16", (s // 16 == t // 16) & (s < t))
    put(CC, c, "low16", (s // 16 == t // 16) & (s > t))
    put(CC, c, "off32", (s // 32 == t // 32) & (s // 16 < t // 16))
    put(CC, c, "up32", (s // 32 == t // 32) & (s < t))
    put(CC, c, "upi32", (s // 32 == t // 32) & (s <= t))
    put(CC, c, "ones64", s // 64 == t // 64)
    put(CC, c, "eye64", i[:, None] % 64 == np.arange(64)[None, :])
    put(CC, c, "ones", 1.0)
    put(CC, c, "iota8", np.arange(8))
    return a, b, c


def build(nc, dram, out):
    with ExitStack() as ctx:
        def sb(name, cols, dt=F32):
            return ctx.enter_context(nc.sbuf_tensor(name, [P, cols], dt))

        def ps(name, banks):
            return ctx.enter_context(nc.psum_tensor(name, [P, banks, 512], F32))

        def sem(name):
            return ctx.enter_context(nc.semaphore(name))

        ring = ctx.enter_context(nc.sbuf_tensor("ring", [P, RING, BLK], F32))
        resid = ctx.enter_context(nc.sbuf_tensor("resid", [P, NX, D], F32))
        const_a = sb("const_a", CA["all"][1])
        vec = sb("vec", NVEC)
        gains = ctx.enter_context(nc.sbuf_tensor("gains", [P, 2, D], F32))
        whi = ctx.enter_context(nc.sbuf_tensor("whi", [P, PAIR, BLK], F32R))
        wlo = ctx.enter_context(nc.sbuf_tensor("wlo", [P, PAIR, BLK], F32R))
        xh = ctx.enter_context(nc.sbuf_tensor("xh", [P, KD, T], F32R))
        xl = ctx.enter_context(nc.sbuf_tensor("xl", [P, KD, T], F32R))
        mid_hi = ctx.enter_context(nc.sbuf_tensor("mid_hi", [P, 2 * T], F32R))[:, :]
        mid_lo = ctx.enter_context(nc.sbuf_tensor("mid_lo", [P, 2 * T], F32R))[:, :]
        hid_hi, hid_lo = xh[:, 0:RING, :], xl[:, 0:RING, :]
        aux = sb("aux", 9 * NK * GTOK // 2)

        def aux16(off, n):
            return aux[:, off // 2:(off + n) // 2].bitcast(BF16)

        o = 0
        places = aux16(o, NK * GTOK).rearrange("p (a t) -> p a t", t=GTOK); o += NK * GTOK
        hot1 = aux16(o, 2 * NK * GTOK).rearrange("p (n a t) -> p n a t", n=2, t=GTOK); o += 2 * NK * GTOK
        hot = aux16(o, HALF * GTOK).rearrange("p (a t) -> p a t", t=GTOK); o += HALF * GTOK
        hot2 = aux16(o, 2 * PARTS * HALF * GTOK).rearrange("p (n g a t) -> p n g a t", n=2, g=PARTS, t=GTOK)
        o += 2 * PARTS * HALF * GTOK
        hk = aux16(o, (2 + PARTS) * T).rearrange("p (a b) -> p a b", b=T); o += (2 + PARTS) * T
        assert o <= 9 * NK * GTOK
        const_c = aux[:, 0:CC["all"][1]]
        router = aux[:, CC["all"][1]:CC["all"][1] + KD * 36].rearrange("p (a b) -> p a b", b=36)
        router_b = aux[:, CC["all"][1] + KD * 36:CC["all"][1] + KD * 36 + 36]
        st = sb("st", 128)
        arena = sb("arena", NK * T)

        def at(off, *dims):
            n = int(np.prod(dims))
            assert off + n <= NK * T
            v = arena[:, off:off + n]
            if len(dims) == 2:
                v = v.rearrange("p (a b) -> p a b", b=dims[1])
            elif len(dims) == 3:
                v = v.rearrange("p (a b c) -> p a b c", b=dims[1], c=dims[2])
            return v

        def ca(name):
            return const_a[:, CA[name][0]:CA[name][0] + CA[name][1]]

        def cc(name):
            return const_c[:, CC[name][0]:CC[name][0] + CC[name][1]]

        def vcol(name, i, n=1):
            return vec[:, VEC[name] + i:VEC[name] + i + n]

        ident, iota = ca("ident"), ca("iota")
        xT2 = at(18432, KD, T)
        const_b = at(0, CB["all"][1])

        def cb(name):
            return const_b[:, CB[name][0]:CB[name][0] + CB[name][1]]

        o = CB["all"][1]
        qk1 = at(o, 16, T); o += 16 * T
        v_moba = at(o, NX, 512); o += NX * 512
        v_ret = at(o, NX, 512); o += NX * 512
        g_ret = at(o, NX, 512); o += NX * 512
        sc1 = at(o, HEADS1, ATT_COLS); o += HEADS1 * ATT_COLS
        pT1 = at(o, HEADS1, ATT_COLS); o += HEADS1 * ATT_COLS
        rT1 = at(o, HEADS1, ATT_COLS); o += HEADS1 * ATT_COLS
        cat1 = at(o, NX, D); o += NX * D
        rope_tmp = at(o, 2, T); o += 2 * T
        xn = at(24576, NX, D)
        ret_sq = at(26624, NX, 512)
        hid = at(0, NK, T)
        peer_qT = at(16384, 16, T)
        score = at(20480, NX, 16, NK)
        o = 26624
        top_s = at(o, 16, TOPK); o += 256
        top_u = at(o, 16, TOPK); o += 256
        top_f = at(o, 16, TOPK); o += 256
        sel_s = at(o, NX, PEER_H, TOPK); o += 256
        pos_u = at(o, PEER_H, TOPK); o += 128
        pos_a = at(o, PEER_H, TOPK); o += 128
        pos_f = at(o, PEER_H, TOPK); o += 128
        sel_i = at(o, 3, NX, P); o += 3 * 256
        cand = at(o, PEER_H, TOPK * TOPK); o += 2048
        pick = at(24576, PEER_H * TOPK, TOPK)
        assert o <= NK * T
        gate_f = at((NK - 1) * T, T)
        final_gain = at(5120, D)
        cv_b = at(0, KD, T)
        cv_c = at(2048, KD, T)
        cv_h = at(4096, KD, T)
        cv_u = at(6144, KD, T + 2)
        cv_y = at(8448, KD, T)
        cv_z = at(10496, KD, T)
        rkv = at(1024, 12, T)
        r_fm, k_fm, v_fm = (at(1024 * (1 + n), 4, T) for n in range(3))
        g_fm = at(4096, 4, T)
        a_til, b_til, k_til, r_til = (at(5120 + 1024 * n, 4, T) for n in range(4))
        a_tm, bh_tm, kh_tm, v_tm = (at(9216 + 1024 * n, NX, 512) for n in range(4))
        qk2 = at(5120, 8, T)
        v2 = at(7168, NX, 512)
        sc2 = at(8192, 4, ATT_COLS)
        pT2 = at(9728, 4, ATT_COLS)
        ob2 = at(11264, NX, 512)
        ya_fm = at(13312, 4, T)
        step_m = at(14336, 4, NCH, HD2)
        step_n = at(16384, 4, NCH, HD2)
        state = at(18432, NCH, 4, HD2)
        q_eff = at(20736, 4, T)
        y_fm = at(21760, 4, T)
        sol = at(22784, 8, P)
        mats = [at(23808 + 1024 * n, 8, P) for n in range(8)]
        cols = at(14336, RW_TILES, T + 1)
        kk_fm = at(18432, 4, T)
        aa_fm = at(19456, 4, T)
        cum = at(20480, 4, T)
        e1 = at(21504, 4, T)
        e2 = at(22528, 4, T)
        bh_fm = at(23552, 4, T)
        kh_fm = at(24576, 4, T)
        lora = at(25600, 3, 512)
        band_bias = at(27136, HEADS2, ATT_COLS)
        low = at(30208, 3, T)
        gates2 = [gains[:, m // 2, (m % 2) * 2 * T:(m % 2 + 1) * 2 * T].rearrange("p (a b) -> p a b", b=T) for m in range(4)]
        o = CC["all"][1] + KD * 36 + 36
        gates2 += [aux[:, o:o + 2 * T].rearrange("p (a b) -> p a b", b=T)]
        gates2 += [at(9216 + 2 * T * m, 2, T) for m in range(3)]
        start = at(32000, T)
        y_out = at(22784, 4, T)
        y_sq = at(23808, 4, T)
        y_mu = at(24832, 4, T)
        y_rs = at(25856, 4, T)
        bonus = at(26880, 4, T)
        y_tmp = at(27904, 4, T)
        mixT = at(5120, KD, T)
        mix_tmp = at(7168, 2, T)
        comb_d = at(512, NEXP, T)
        h_sig = at(8704, 2, 2 * T)
        h_mid = at(9728, 2, 2 * T)
        o = 10752
        logit = at(o, NX, 36); o += 72
        g8 = at(o, NX, 8); o += 16
        g8m = at(o, NX, 8); o += 16
        g8i = at(o, NX, 8); o += 16
        hot_g = at(o, NX, 8); o += 16
        sel8 = at(o, NX, 8); o += 16
        sel8m = at(o, NX, 8); o += 16
        sel8i = at(o, NX, 8); o += 16
        sel8f = at(o, NX, 8); o += 16
        sel_t = at(o, NX, 8, 4); o += 64
        comb8 = at(o, NX, 8); o += 16
        comb8b = at(o, NX, 8); o += 16
        comb = at(o, NX, NEXP); o += 64
        combT = at(o, T); o += T
        pT_ple = at(0, 2, T)
        assert o <= 12800
        ple = at(12800, NX, D)
        sig_ple = at(14848, NX, D)

        acc = ps("acc", 4)
        prod = ps("prod", 2)
        gen = ps("gen", 2)

        landed = [sem(f"landed{i}") for i in range(RING)]
        hi_ready = sem("hi_ready")
        hi_used = sem("hi_used")
        lo_ready = [sem(f"lo_ready{i}") for i in range(PAIR)]
        w_used = sem("w_used")
        fm_out = sem("fm_out")
        acc_out = sem("acc_out")
        gen_mm = sem("gen_mm")
        gen_out = sem("gen_out")
        x_in = [sem(f"x_in{x}") for x in range(NX)]
        small_in = sem("small_in")
        table_b_in = sem("table_b_in")
        final_in = sem("final_in")
        gain_in = [sem("gain_in0"), sem("gain_in1")]
        x_rounded = sem("x_rounded")
        block2_in = sem("block2_in")
        ple_in = sem("ple_in")
        arena_free = sem("arena_free")
        ms_ready = sem("ms_ready")
        root_ready = sem("root_ready")
        normed = sem("normed")
        fm_ready = sem("fm_ready")
        roped = sem("roped")
        att_s = sem("att_s")
        att_m = sem("att_m")
        att_p = sem("att_p")
        att_pt = sem("att_pt")
        att_o = sem("att_o")
        att_done = sem("att_done")
        topk_ready = sem("topk_ready")
        gate_exp = sem("gate_exp")
        hot_ready = sem("hot_ready")
        tok_mm = sem("tok_mm")
        hh_ready = sem("hh_ready")
        hl_ready = sem("hl_ready")
        gated = sem("gated")
        mix_out = sem("mix_out")
        conv_out = sem("conv_out")
        shifted = sem("shifted")
        low_act = sem("low_act")
        lora_mm = sem("lora_mm")
        lora_out = sem("lora_out")
        logw_ready = sem("logw_ready")
        exp_ready = sem("exp_ready")
        sq_ready = sem("sq_ready")
        state_ready = sem("state_ready")
        branch_out = sem("branch_out")
        silu_ready = sem("silu_ready")
        mid_ready = sem("mid_ready")
        comb_mm = sem("comb_mm")
        max_ready = sem("max_ready")
        moe_exp = sem("moe_exp")
        ple_sig = sem("ple_sig")
        v_chain = sem("v_chain")
        out_done = sem("out_done")

        turned = {}

        block = ctx.enter_context(nc.Block())

        @block.sync
        def _(sp):
            def load(g, src, i=0, n=RING):
                if g >= RING:
                    if g - RING in SPLIT_PLACE:
                        s = SPLIT_PLACE[g - RING]
                        sp.wait_ge(lo_ready[s % PAIR], s // PAIR + 1 + n // PAIR * i)
                    else:
                        sp.wait_ge(w_used, g - RING + 1 + n * i)
                sp.dma_start(ring[:, g % RING, :], src).then_inc(landed[g % RING], 16)

            def stream(name, src, n):
                base = BASE[name]
                for b in range(min(n, RING)):
                    load(base + b, src[b])
                whole = n // RING
                if whole > 2:
                    with sp.Fori(0, whole - 1) as i:
                        for j in range(RING):
                            load(base + RING + j, src[RING * i + RING + j], i)
                else:
                    for b in range(RING, RING * whole):
                        load(base + b, src[b])
                for b in range(max(RING, RING * whole), n):
                    load(base + b, src[b])

            for x in range(NX):
                sp.dma_start(resid[:, x, :], dram["x"].rearrange("a (x p) d -> p (a x) d", p=P)[:, x, :]).then_inc(x_in[x], 16)
            for name in ("even_qk", "even_vg", "even_out"):
                stream(name, dram[name], dict(STREAM)[name])
            for layer in range(LAYERS):
                if layer == 1:
                    stream("odd_in", dram["odd_in"], 24)
                    stream("odd_out", dram["odd_out"], 8)
                stream(f"peer_q{layer}", dram[f"peer_q{layer}"], 16)
                stream(f"peer_keys{layer}", dram[f"peer_keys{layer}"], 2)
                stream(f"peer_u{layer}", dram[f"peer_u{layer}"], NK)
                stream(f"peer_v{layer}", dram["peer_v"][layer].rearrange("(a c) d -> c a d", c=NK), NK)
            stream("qk2", dram["qk2"], 8)
            stream("v2", dram["v2"], 4)
            stream("rw2", dram["rw2"], RW_TILES)
            stream("gate2", dram["gate2"], 16)
            for n, name in enumerate(("branch_a", "branch_r")):
                for j in range(4):
                    load(BASE["branch"] + 4 * n + j, dram[name][j])
            stream("out2", dram["out2"], 8)
            g = BASE["moe"]
            for j in range(4):
                load(g + j, (dram["exp_gate"], dram["exp_up"])[j // 2][j % 2])

            def expert(g, e, i):
                for j in range(4):
                    load(g + j, (dram["exp_gate"], dram["exp_up"])[j // 2][2 * e + j % 2], i, 12)
                for j in range(2):
                    load(g + 4 + j, dram["exp_down"][2 * e - 2 + j], i, 12)

            with sp.Fori(0, (NEXP - 2) // 2) as i:
                for j in range(2):
                    expert(g + 4 + 6 * j, 2 * i + 1 + j, i)
            expert(g + 4 + 6 * (NEXP - 2), NEXP - 1, 0)
            for j in range(2):
                load(g + 6 * NEXP - 2 + j, dram["exp_down"][2 * NEXP - 2 + j])
            stream("ple_proj", dram["ple_proj"], 2)
            stream("ple_gate", dram["ple_gate"], 8)
            for x in range(NX):
                sp.wait_ge(normed, NORMED["ln2"] - NX + x + 1)
                sp.dma_start(out.rearrange("a (x p) d -> p (a x) d", p=P)[:, x, :], resid[:, x, :]).then_inc(out_done, 16)
            sp.wait_ge(out_done, 16 * NX)

        @block.gpsimd
        def _(pool):
            def rest(g, s, i=0):
                pool.wait_ge(hi_ready, s + 1 + RING * i)
                if s >= PAIR:
                    pool.wait_ge(w_used, SPLIT_BLOCKS[s - PAIR] + 1 + RING * i)
                pool.tensor_tensor(wlo[:, s % PAIR, :], ring[:, g % RING, :], whi[:, s % PAIR, :].bitcast(F32), ALU.subtract)\
                    .then_inc(lo_ready[s % PAIR], 1)

            def rests(name, n):
                g, s = BASE[name], SPLIT[name]
                for b in range(RING):
                    rest(g + b, s + b)
                if n >= 3 * RING:
                    with pool.Fori(0, n // RING - 1) as i:
                        for j in range(RING):
                            rest(g + RING + j, s + RING + j, i)
                else:
                    for b in range(RING, n // RING * RING):
                        rest(g + b, s + b)
                for b in range(n // RING * RING, n):
                    rest(g + b, s + b)

            def gain(row, src, used=None):
                if used:
                    pool.wait_ge(normed, NORMED[used])
                pool.dma_start(gains[:, row, :], src.partition_broadcast(P)).then_inc(gain_in[row], 16)

            gain(0, dram["norm_mix"][0])
            pool.dma_start(const_b, dram["const_b"]).then_inc(table_b_in, 16)
            gain(1, dram["norm_ffn"][0])
            rests("even_qk", 36)
            gain(0, dram["norm_mix"][1], "mix0")
            rests("peer_q0", 16)
            rests("peer_u0", 2 * NK)
            gain(1, dram["norm_ffn"][1], "ffn0")
            rests("odd_in", 32)
            gain(0, dram["ln_in_g"], "mix1")
            rests("peer_q1", 16)
            gain(1, dram["ln_in_b"], "ffn1")
            rests("peer_u1", 2 * NK)
            pool.wait_ge(w_used, BASE["peer_v1"] + NK - RING)
            pool.dma_start(final_gain, dram["final_norm"].partition_broadcast(P)).then_inc(final_in, 16)
            pool.wait_ge(arena_free, 1)
            pool.dma_start(lora[:, :, :], dram["lora"]).then_inc(block2_in, 16)
            pool.dma_start(band_bias[:, :, :], dram["band_bias"]).then_inc(block2_in, 16)
            pool.dma_start(const_c, dram["const_c"]).then_inc(block2_in, 16)
            pool.dma_start(router, dram["router"]).then_inc(block2_in, 16)
            pool.dma_start(router_b, dram["router_b"].partition_broadcast(P)).then_inc(block2_in, 16)
            pool.dma_start(pT_ple, dram["p"]).then_inc(ple_in, 16)

            def norm_gains(n, used):
                gain(0, dram["ln_g"][n], used)
                gain(1, dram["ln_b"][n], used)

            rests("qk2", 8 + 4 + RW_TILES + 16)
            rests("out2", 8)
            pool.wait_ge(branch_out, 4)
            norm_gains(0, "blk2")
            rests("moe", 6 * NEXP)
            norm_gains(1, "ln0")
            rests("ple_gate", 8)
            norm_gains(2, "ln1")

        @block.tensor
        def _(pe):
            gi = [0]
            au = [0]

            def arrive(g):
                pe.wait_ge(landed[g % RING], 16 * (g // RING + 1))
                return ring[:, g % RING, :]

            def gen_bank():
                if gi[0] >= 2:
                    pe.wait_ge(gen_out, gi[0] - 1)
                gi[0] += 1
                return gen[:, (gi[0] - 1) % 2, :]

            def acc_free():
                if au[0]:
                    pe.wait_ge(acc_out, au[0])
                au[0] += 1

            def rounded(s, i, n):
                pe.wait_ge(hi_ready, s + 1 + n * i)
                return whi[:, s % PAIR, :]

            def rest(s, i, n):
                pe.wait_ge(lo_ready[s % PAIR], s // PAIR + 1 + n // PAIR * i)
                return wlo[:, s % PAIR, :]

            def fm_passes(dst, s, i, n):
                w = rounded(s, i, n)
                for k in range(KD):
                    pe.matmul(dst, w[:, k * P:(k + 1) * P], xh[:, k, :], start=(k == 0), stop=False)
                    mm = pe.matmul(dst, w[:, k * P:(k + 1) * P], xl[:, k, :], start=False, stop=False)
                mm.then_inc(hi_used, 1)
                w = rest(s, i, n)
                for k in range(KD):
                    mm = pe.matmul(dst, w[:, k * P:(k + 1) * P], xh[:, k, :], start=False, stop=(k == KD - 1))
                mm.then_inc(w_used, 1)

            def fm_split(name, b, i=0):
                s, f = SPLIT[name] + b, FMBASE[name] + b
                if f >= 2:
                    pe.wait_ge(fm_out, f - 1 + RING * i)
                fm_passes(prod[:, f % 2, 0:T], s, i, RING)

            def tm_block(name, b, kpair, banks):
                s = SPLIT[name] + b

                def rows(w, part, start, stop):
                    for x in range(NX):
                        for k in range(2):
                            mm = pe.matmul(acc[:, banks[x], :], part[:, 2 * kpair + k, x * P:(x + 1) * P],
                                           w[:, k * 512:(k + 1) * 512], start=(start and k == 0), stop=(stop and k == 1))
                    return mm

                w = rounded(s, 0, RING)
                rows(w, xh, kpair == 0, False)
                rows(w, xl, False, False).then_inc(hi_used, 1)
                rows(rest(s, 0, RING), xh, False, kpair == KD // 2 - 1).then_inc(w_used, 1)

            def tm_square(name):
                acc_free()
                for b in range(8):
                    tm_block(name, b, b % 4, (b // 4, 2 + b // 4))

            def by_pairs(name, pairs):
                acc_free()
                for b in range(8):
                    if b < 4:
                        pe.wait_ge(pairs, b + 1)
                    tm_block(name, b, b % 4, (b // 4, 2 + b // 4))

            def turn(src, tiles, name):
                turned[name] = gi[0]
                for x in range(NX):
                    pe.wait_ge(normed, NORMED[name] - NX + x + 1)
                    for q in range(tiles // 4):
                        bank = gen_bank()
                        for k in range(4):
                            mm = pe.transpose(bank[:, k * P:(k + 1) * P], src[:, x, (4 * q + k) * P:(4 * q + k + 1) * P], ident)
                        mm.then_inc(gen_mm, 1)

            def attend_scores(q_of, k_of):
                acc_free()
                for h in range(4):
                    pe.matmul(acc[:, h, 0:P], q_of(h)[:, 0:P], k_of(h)[:, 0:P], start=True, stop=True)
                    pe.matmul(acc[:, h, P:ATT_COLS], q_of(h)[:, P:T], k_of(h), start=True, stop=True).then_inc(att_s, 1)

            def attend_values(soft, turned, p_sb, pT, v_of, width):
                for h in range(4):
                    pe.wait_ge(att_p, soft + h + 1)
                    bank = gen_bank()
                    for b in range(3):
                        mm = pe.transpose(bank[:, b * P:(b + 1) * P], p_sb[:, h, b * P:(b + 1) * P], ident)
                    mm.then_inc(gen_mm, 1)
                for h in range(4):
                    pe.wait_ge(att_pt, turned + h + 1)
                    values(pT, v_of, h, width, h == 3)

            def values(pT, v_of, h, width, last):
                cols_ = slice(h * width, (h + 1) * width)
                pe.matmul(prod[:, 0, cols_], pT[:, h, 0:P], v_of(0, h), start=True, stop=True)
                pe.matmul(prod[:, 1, cols_], pT[:, h, P:2 * P], v_of(0, h), start=True, stop=False)
                mm = pe.matmul(prod[:, 1, cols_], pT[:, h, 2 * P:3 * P], v_of(1, h), start=False, stop=True)
                if last:
                    mm.then_inc(att_o, 1)

            pe.wait_ge(small_in, 32)
            turn(xn, KD, "mix0")
            pe.wait_ge(fm_ready, FM["mix0"])
            for b in range(16):
                fm_split("even_qk", b)
            pe.wait_ge(table_b_in, 16)
            for b in range(12):
                if b in (0, 8):
                    acc_free()
                tm_block("even_vg", b, b % 4, ((0, 1), (2, 3), (0, 1))[b // 4])
                if b < 8:
                    pe.wait_ge(fm_out, 2 * b + 2)
                    pe.matmul(gen_bank(), cb("rot"), qk1[:, 2 * b:2 * b + 2, :].rearrange("p a b -> p (a b)"),
                              start=True, stop=True).then_inc(gen_mm, 1)
            pe.wait_ge(roped, 8)
            attend_scores(lambda h: qk1[:, h, :], lambda h: qk1[:, 4 + h, :])
            attend_values(0, 0, sc1, pT1, lambda x, h: v_moba[:, x, h * HD1:(h + 1) * HD1], HD1)
            acc_free()
            for h in range(4):
                q, k = qk1[:, 8 + h, :], qk1[:, 12 + h, :]
                pe.matmul(acc[:, h, 0:T], k[:, 0:P], q, start=True, stop=True)
                pe.matmul(acc[:, h, T:ATT_COLS], k[:, P:T], q[:, P:T], start=True, stop=True).then_inc(att_s, 1)
            pe.wait_ge(att_done, 1)
            for h in range(4):
                pe.wait_ge(att_pt, 4 + h + 1)
                values(rT1, lambda x, h: v_ret[:, x, h * HD1:(h + 1) * HD1], h, HD1, h == 3)
            turn(cat1, KD, "cat")
            pe.wait_ge(fm_ready, FM["cat"])
            tm_square("even_out")

            def peer(layer):
                turn(xn, KD, f"ffn{layer}")
                pe.wait_ge(fm_ready, FM[f"ffn{layer}"])
                pe.wait_ge(att_done, 2)
                for b in range(16):
                    fm_split(f"peer_q{layer}", b)
                for b in range(2):
                    pe.wait_ge(fm_out, FMBASE[f"peer_q{layer}"] + 8 * (b + 1))
                    w = arrive(BASE[f"peer_keys{layer}"] + b)
                    for x in range(NX):
                        for q in range(2):
                            bank = gen_bank()
                            for j in range(4):
                                n = 4 * q + j
                                mm = pe.matmul(bank[:, j * P:(j + 1) * P], peer_qT[:, 8 * b + n, x * P:(x + 1) * P],
                                               w[:, n * P:(n + 1) * P], start=True, stop=True)
                            mm.then_inc(gen_mm, 1)
                    pe.wait_ge(gen_mm, gi[0])
                    pe.nop().then_inc(w_used, 1)
                vs, hb = SPLIT[f"peer_v{layer}"], layer * NK
                tb = 2 * layer * HALF

                def hidden(i, j):
                    fm_split(f"peer_u{layer}", j, i)

                def token_gates(i, j, half):
                    n = tb + half * HALF + j
                    pe.wait_ge(hot_ready, n + 1 + RING * i)
                    if n >= 2:
                        pe.wait_ge(gated, n - 1 + RING * i)
                    for t in range(GTOK):
                        for g in range(PARTS):
                            mm = pe.matmul(gen[:, j % 2, t * HALF:(t + 1) * HALF], hot1[:, j % 2, :, t], hot2[:, j % 2, g, :, t],
                                           start=(g == 0), stop=(g == PARTS - 1))
                    mm.then_inc(tok_mm, 1)

                def down(i, j, first=False, last=False):
                    def values(w, h, start, stop):
                        for x in range(NX):
                            for n in range(2):
                                mm = pe.matmul(acc[:, 2 * x + n, :], h[:, j % RING, x * P:(x + 1) * P], w[:, n * 512:(n + 1) * 512],
                                               start=start, stop=stop, skip_group_check=True)
                        return mm

                    pe.wait_ge(hl_ready, hb + j + 1 + RING * i)
                    w = rounded(vs + j, i, RING)
                    values(w, hid_hi, first, False)
                    values(w, hid_lo, False, False).then_inc(hi_used, 1)
                    values(rest(vs + j, i, RING), hid_hi, False, last).then_inc(w_used, 1)

                with pe.Fori(0, HALF // RING - 2) as i:
                    for j in range(RING):
                        hidden(i, j)
                pe.wait_ge(normed, NORMED[f"route{layer}"])
                for x in range(NX):
                    bank = gen_bank()
                    for n in range(3):
                        mm = pe.transpose(bank[:, n * P:(n + 1) * P], sel_i[:, n, x, :], ident)
                    mm.then_inc(gen_mm, 1)
                for n in range(HALF - 2 * RING, HALF):
                    hidden(0, n)
                token_gates(0, 0, 0)
                with pe.Fori(0, HALF // RING - 1) as i:
                    for j in range(RING):
                        token_gates(i, j + 1, 0)
                        hidden(i + HALF // RING, j)
                for j in range(HALF - RING, HALF):
                    if j + 1 < HALF:
                        token_gates(0, j + 1, 0)
                    hidden(0, HALF + j)
                acc_free()
                for j in range(RING):
                    token_gates(0, j, 1)
                    down(0, j, first=(j == 0))
                with pe.Fori(1, HALF // RING) as i:
                    for j in range(RING):
                        token_gates(i, j, 1)
                        down(i, j)
                with pe.Fori(HALF // RING, NK // RING - 1) as i:
                    for j in range(RING):
                        down(i, j)
                for j in range(RING):
                    down(NK // RING - 1, j, last=(j == RING - 1))
            peer(0)
            turn(xn, KD, "mix1")
            pe.wait_ge(fm_ready, FM["mix1"])
            for b in range(24):
                fm_split("odd_in", b)
            by_pairs("odd_out", conv_out)
            peer(1)
            turn(resid, KD, "blk2")
            pe.wait_ge(fm_ready, FM["blk2"])
            for b in range(8):
                fm_split("qk2", b)
            acc_free()
            for b in range(4):
                tm_block("v2", b, b, (0, 1))
            pe.wait_ge(fm_out, FMBASE["rw2"])

            def band(r):
                def rows(h, tile):
                    hh = 4 * r + h
                    return qk2[HD2 * (hh % 2):HD2 * (hh % 2 + 1), tile + hh // 2, :]
                return lambda h: rows(h, 0), lambda h: rows(h, 4), \
                    lambda x, h: v2[:, x, (4 * r + h) * HD2:(4 * r + h + 1) * HD2]

            q_of, k_of, v_of = band(0)
            attend_scores(q_of, k_of)
            for b in range(RW_TILES):
                fm_split("rw2", b)
            pe.wait_ge(fm_out, FMBASE["gate2"])
            attend_values(4, 8, sc2, pT2, v_of, HD2)
            q_of, k_of, v_of = band(1)
            pe.wait_ge(att_done, 3)
            attend_scores(q_of, k_of)
            attend_values(8, 12, sc2, pT2, v_of, HD2)
            turn(ob2, 4, "band")
            pe.wait_ge(block2_in, 80)
            pe.wait_ge(low_act, 2)
            for n in range(6):
                if n >= 2:
                    pe.wait_ge(lora_out, n - 1)
                for j in range(2):
                    f = 2 * (n % 2) + j
                    dst = prod[:, n % 2, j * T:(j + 1) * T]
                    if n < 4:
                        rows = slice(64 * (n // 2), 64 * (n // 2) + 64)
                        mm = pe.matmul(dst, lora[rows, 0, f * P:(f + 1) * P], low[rows, 0, :], start=True, stop=True)
                    else:
                        pe.matmul(dst, lora[:, 1, f * P:(f + 1) * P], low[:, 1, :], start=True, stop=False)
                        mm = pe.matmul(dst, lora[0:32, 2, f * P:(f + 1) * P], low[0:32, 2, :], start=False, stop=True)
                mm.then_inc(lora_mm, 1)

            def head_sums(src, count):
                pe.wait_ge(sq_ready, count)
                for q in range(2):
                    pe.matmul(gen_bank(), cc("ones64"), src[:, 2 * q:2 * q + 2, :].rearrange("p a b -> p (a b)"),
                              start=True, stop=True).then_inc(gen_mm, 1)

            head_sums(e1, 1)
            pe.wait_ge(lora_out, 6)
            for b in range(GATE_EARLY):
                fm_split("gate2", b)
            pe.wait_ge(fm_ready, FM["til"])
            for x in range(NX):
                for src in (a_til, bh_fm, kh_fm, v_fm):
                    bank = gen_bank()
                    for pr in range(4):
                        mm = pe.transpose(bank[:, pr * P:(pr + 1) * P], src[:, pr, x * P:(x + 1) * P], ident)
                    mm.then_inc(gen_mm, 1)

            def by_head(lhs, rhs, x):
                for q in range(2):
                    bank = gen_bank()
                    rows = slice(64 * q, 64 * q + 64)
                    for pr in range(4):
                        mm = pe.matmul(bank[:, pr * P:(pr + 1) * P], lhs[rows, pr, x * P:(x + 1) * P],
                                       rhs[rows, pr, x * P:(x + 1) * P], start=True, stop=True)
                    mm.then_inc(gen_mm, 1)

            def square(lhs, rhs):
                for q in range(2):
                    bank = gen_bank()
                    for u in range(4):
                        mm = pe.matmul(bank[:, u * P:(u + 1) * P], lhs[:, 4 * q + u, :], rhs[:, 4 * q + u, :],
                                       start=True, stop=True)
                    mm.then_inc(gen_mm, 1)

            def all_out():
                pe.wait_ge(gen_out, gi[0])

            m_lT, m_l, m_ak, m_rb, m_rk, m_off, m_a, m_b = mats
            for x in range(NX):
                by_head(b_til, a_til, x)
                by_head(a_til, b_til, x)
                by_head(k_til, a_til, x)
                by_head(b_til, r_til, x)
                by_head(k_til, r_til, x)
                all_out()
                bank = gen_bank()
                for hd in range(HEADS2):
                    mm = pe.matmul(bank[:, hd * HD2:(hd + 1) * HD2], m_ak[:, hd, :], v_tm[:, x, hd * HD2:(hd + 1) * HD2],
                                   start=True, stop=True)
                mm.then_inc(gen_mm, 1)
                square(m_lT, m_l)
                square(m_l, m_lT)
                square(m_a, m_ak)
                square(m_b, m_a)
                square(m_a, m_b)
                square(m_l, m_ak)
                square(m_lT, m_l)
                square(m_a, m_ak)
                square(m_ak, sol)
                square(m_off, m_b)
                square(m_ak, m_lT)
                all_out()
                bank = gen_bank()
                for hd in range(HEADS2):
                    rows = slice(64 * (hd % 2), 64 * (hd % 2) + 64)
                    mm = pe.matmul(bank[rows, (hd // 2) * P:(hd // 2 + 1) * P], sol[:, hd, 0:HD2], m_rb[:, hd, :],
                                   start=True, stop=True)
                mm.then_inc(gen_mm, 1)
                bank = gen_bank()
                for hd in range(HEADS2):
                    rows = slice(64 * (hd % 2), 64 * (hd % 2) + 64)
                    dst = bank[rows, (hd // 2) * P:(hd // 2 + 1) * P]
                    pe.matmul(dst, sol[:, hd, HD2:P], m_rb[:, hd, :], start=True, stop=False)
                    mm = pe.matmul(dst, v_tm[:, x, hd * HD2:(hd + 1) * HD2], m_rk[:, hd, :], start=False, stop=True)
                mm.then_inc(gen_mm, 1)
                for c in range(4):
                    bank = gen_bank()
                    tok = slice(CH * c, CH * c + CH)
                    for hd in range(HEADS2):
                        rows, hc = slice(64 * (hd % 2), 64 * (hd % 2) + 64), slice(hd * HD2, (hd + 1) * HD2)
                        o_ = (hd // 2) * HD2
                        pe.matmul(bank[rows, o_:o_ + HD2], sol[tok, hd, 0:HD2], bh_tm[tok, x, hc], start=True, stop=True)
                        o_ += 4 * HD2
                        pe.matmul(bank[rows, o_:o_ + HD2], bh_tm[tok, x, hc], sol[tok, hd, HD2:P], start=True, stop=False)
                        mm = pe.matmul(bank[rows, o_:o_ + HD2], kh_tm[tok, x, hc], v_tm[tok, x, hc], start=False, stop=True)
                    mm.then_inc(gen_mm, 1)
            for c in range(1, NCH - 1):
                fm_split("gate2", GATE_EARLY + c - 1)
                pe.wait_ge(state_ready, c)
                bank = gen_bank()
                for hd in range(HEADS2):
                    rows = slice(64 * (hd % 2), 64 * (hd % 2) + 64)
                    mm = pe.matmul(bank[rows, (hd // 2) * HD2:(hd // 2 + 1) * HD2], step_m[rows, hd // 2, c, :],
                                   state[rows, c, hd // 2, :], start=True, stop=True)
                mm.then_inc(gen_mm, 1)
            pe.wait_ge(state_ready, NCH - 1)
            for q in range(2):
                bank = gen_bank()
                for hd in range(4 * q, 4 * q + 4):
                    rows = slice(64 * (hd % 2), 64 * (hd % 2) + 64)
                    for c in range(1, NCH):
                        o_ = (hd // 2 - 2 * q) * T + c * CH
                        mm = pe.matmul(bank[rows, o_:o_ + CH], state[rows, c, hd // 2, :],
                                       q_eff[rows, hd // 2, c * CH:(c + 1) * CH], start=True, stop=True)
                mm.then_inc(gen_mm, 1)
            head_sums(y_fm, 2)
            head_sums(y_sq, 3)
            head_sums(bonus, 4)
            def branch(b, dst, src):
                w = arrive(BASE["branch"] + b)
                for f in range(2):
                    for k in range(4):
                        mm = pe.matmul(dst[:, f * T:(f + 1) * T], w[:, (2 * k + f) * P:(2 * k + f + 1) * P],
                                       src[:, k, :], start=(k == 0), stop=(k == 3))
                mm.then_inc(w_used, 1)

            acc_free()
            for j in range(4):
                branch(j, acc[:, j, :], ya_fm)
            pe.wait_ge(fm_ready, FM["rwkv"])
            pe.wait_ge(fm_out, FMBASE["gate2"] + 16)
            for j in range(4):
                if j >= 2:
                    pe.wait_ge(branch_out, j - 1)
                branch(4 + j, prod[:, j % 2, :], y_out)
            by_pairs("out2", mix_out)
            turn(resid, KD, "ln0")
            pe.wait_ge(fm_ready, FM["ln0"])
            bank = gen_bank()
            for x in range(NX):
                for k in range(KD):
                    mm = pe.matmul(bank[:, x * 36:(x + 1) * 36], xT2[:, k, x * P:(x + 1) * P], router[:, k, :],
                                   start=(k == 0), stop=(k == KD - 1))
            mm.then_inc(gen_mm, 1)
            es = SPLIT["moe"]

            def up_products(s, e, i=0, first=False, parts=(0, 1)):
                for n in parts:
                    if not first:
                        pe.wait_ge((silu_ready, mid_ready)[n], e + 2 * i)
                    for f in range(2):
                        fm_passes(prod[:, n, f * T:(f + 1) * T], s + 2 * n + f, i, 12)

            def expert_weights(e, i=0):
                pe.matmul(gen[:, 0, 0:T], cc("ones")[0:NEXP, :], comb_d[0:NEXP, e + 2 * i, :], start=True, stop=True)\
                    .then_inc(comb_mm, 1)

            up_products(es, 0, first=True)
            up_products(es + 4, 1, parts=(0,))
            pe.wait_ge(normed, NORMED["comb"])
            bank = gen_bank()
            for x in range(NX):
                mm = pe.transpose(bank[0:NEXP, x * P:(x + 1) * P], comb[:, x, :], ident)
            mm.then_inc(gen_mm, 1)
            pe.wait_ge(fm_ready, FM["comb"])
            acc_free()
            def expert_down(s, i=0, first=False, last=False):
                for f in range(2):
                    def rows(w, mid, start, stop):
                        for x in range(NX):
                            for n in range(2):
                                mm = pe.matmul(acc[:, 2 * x + n, :], mid[:, f * T + x * P:f * T + (x + 1) * P],
                                               w[:, n * 512:(n + 1) * 512], start=start, stop=stop, skip_group_check=True)
                        return mm

                    w = rounded(s + f, i, 12)
                    rows(w, mid_hi, first and f == 0, False)
                    rows(w, mid_lo, False, False).then_inc(hi_used, 1)
                    rows(rest(s + f, i, 12), mid_hi, False, last and f == 1).then_inc(w_used, 1)

            expert_weights(0)
            up_products(es + 4, 1, parts=(1,))
            expert_weights(1)
            expert_down(es + 8, first=True)
            pe.wait_ge(fm_ready, FM["comb_rest"])
            with pe.Fori(0, (NEXP - 2) // 2) as i:
                for j in range(2):
                    up_products(es + 10 + 6 * j, 2 + j, i)
                    expert_weights(2 + j, i)
                    expert_down(es + 14 + 6 * j, i)
            pe.wait_ge(mid_ready, NEXP)
            expert_down(es + 6 * NEXP - 2, last=True)
            acc_free()
            pe.wait_ge(ple_in, 16)
            for b in range(2):
                w = arrive(BASE["ple_proj"] + b)
                for x in range(NX):
                    for k in range(2):
                        mm = pe.matmul(acc[:, 2 * x + b, :], pT_ple[:, k, x * P:(x + 1) * P], w[:, k * 512:(k + 1) * 512],
                                       start=(k == 0), stop=(k == 1))
                mm.then_inc(w_used, 1)
            turn(resid, KD, "ln1")
            pe.wait_ge(fm_ready, FM["ln1"])
            tm_square("ple_gate")

        @block.scalar
        def _(act):
            def take(name, b, dst, func, **kw):
                act.wait_ge(w_used, BASE[name] + b + 1)
                act.activation(dst, prod[:, (FMBASE[name] + b) % 2, 0:T], func, **kw).then_inc(fm_out, 1)

            def rounded(name, b, i=0, n=RING):
                g, s = BASE[name] + b, SPLIT[name] + b
                act.wait_ge(landed[g % RING], 16 * (g // RING + 1) + 16 * (n // RING) * i)
                if s >= PAIR:
                    act.wait_ge(hi_used, s - PAIR + 1 + n * i)
                    act.wait_ge(lo_ready[s % PAIR], s // PAIR + n // PAIR * i)
                act.activation(whi[:, s % PAIR, :], ring[:, g % RING, :], ACT.Copy).then_inc(hi_ready, 1)

            def round_x(name):
                for n in range(NX * KD // 4):
                    x, q = n // 2, n % 2
                    act.wait_ge(gen_mm, turned[name] + n + 1)
                    act.activation(xh[:, 4 * q:4 * q + 4, x * P:(x + 1) * P],
                                   gen[:, (turned[name] + n) % 2, :].rearrange("p (a b) -> p a b", b=P), ACT.Copy)\
                        .then_inc(x_rounded, 1)

            def rounded_take(name, n, dst, func, then=None, first=0, last=None):
                for b in range(first, last or n):
                    if b + PAIR < n:
                        rounded(name, b + PAIR)
                    elif then:
                        rounded(then, b + PAIR - n)
                    take(name, b, dst(b), func)

            def round_blocks(name, first, last):
                for b in range(first, last):
                    rounded(name, b)

            def root(name, dst, src):
                act.wait_ge(ms_ready, ROOT[name])
                act.activation(dst, src, ACT.Sqrt).then_inc(root_ready, 1)

            def norm_root(name):
                root(name, st[:, 4:6], st[:, 2:4])

            def soft(base, s):
                for h in range(4):
                    act.wait_ge(att_m, base + h + 1)
                    act.activation(s[:, h, 0:P], s[:, h, 0:P], ACT.Exp, bias=st[:, 16 + h:17 + h],
                                   accum_out=st[:, 24 + h:25 + h])
                    act.activation(s[:, h, P:ATT_COLS], s[:, h, P:ATT_COLS], ACT.Exp, bias=st[:, 20 + h:21 + h],
                                   accum_out=st[:, 28 + h:29 + h]).then_inc(att_p, 1)

            act.dma_start(const_a[:, :], dram["const_a"]).then_inc(small_in, 16)
            act.dma_start(vec[:, :], dram["vec"]).then_inc(small_in, 16)
            norm_root("mix0")
            round_blocks("even_qk", 0, PAIR)
            round_x("mix0")
            rounded_take("even_qk", 16, lambda b: qk1[:, b, :], ACT.Copy, "even_vg")
            round_blocks("even_vg", PAIR, 10)
            act.wait_ge(w_used, BASE["even_vg"] + 8)
            for n, dst in enumerate((v_moba, v_ret)):
                for x in range(NX):
                    mv = act.activation(dst[:, x, :], acc[:, 2 * n + x, :], ACT.Copy)
            mv.then_inc(acc_out, 1)
            round_blocks("even_vg", 10, 12)
            round_blocks("even_out", 0, PAIR)
            act.wait_ge(w_used, BASE["even_vg"] + 12)
            for x in range(NX):
                mv = act.activation(g_ret[:, x, :], acc[:, x, :], ACT.Silu)
            mv.then_inc(acc_out, 1)
            soft(0, sc1)
            root("ret", st[:, 56:64], st[:, 48:56])
            round_x("cat")
            round_blocks("even_out", PAIR, 8)

            def peer(layer):
                q, u, v = f"peer_q{layer}", f"peer_u{layer}", f"peer_v{layer}"
                round_blocks(q, 0, PAIR)
                norm_root(f"ffn{layer}")
                round_x(f"ffn{layer}")
                rounded_take(q, 16, lambda b: peer_qT[:, b, :], ACT.Copy, u)
                rounded(u, PAIR)

                def hidden_chunk(j, i=0, last=False):
                    act.wait_ge(w_used, BASE[u] + j + 1 + RING * i)
                    act.activation(hid[:, RING * i + j, :], prod[:, (FMBASE[u] + j) % 2, 0:T], ACT.Gelu).then_inc(fm_out, 1)
                    if not last:
                        rounded(u, j + PAIR + 1, i)

                def hidden(i):
                    for j in range(RING):
                        hidden_chunk(j, i)

                early = 12
                with act.Fori(0, early) as i:
                    hidden(i)
                act.wait_ge(topk_ready, layer + 1)
                act.activation(sel_i[:, 2, :, :], sel_i[:, 2, :, :], ACT.Exp).then_inc(gate_exp, 1)
                with act.Fori(early, NK // RING - 1) as i:
                    hidden(i)
                for j in range(NK - RING, NK):
                    hidden_chunk(j, last=(j == NK - 1))

                def chunk(j, i=0):
                    if j >= PAIR:
                        rounded(v, j, i)
                    if j >= RING:
                        act.wait_ge(w_used, BASE[v] + j - RING + 1 + RING * i)
                    act.activation(hid_hi[:, j % RING, :], hid[:, RING * i + j, :], ACT.Copy).then_inc(hh_ready, 1)

                for half in range(2):
                    act.wait_ge(gated, 2 * layer * HALF + (half + 1) * HALF)
                    if half == 0:
                        for j in range(RING):
                            chunk(j)
                    with act.Fori(half * (HALF // RING - 1), (half + 1) * HALF // RING - 1) as i:
                        for j in range(RING):
                            chunk(RING + j, i)
            peer(0)
            round_blocks("odd_in", 0, PAIR)
            norm_root("mix1")
            round_x("mix1")
            rounded_take("odd_in", 24, lambda b: (cv_b, cv_c, cv_h)[b % 3][:, b // 3, :], ACT.Copy, "odd_out")
            round_blocks("odd_out", PAIR, 8)
            peer(1)
            round_blocks("qk2", 0, PAIR)
            norm_root("final")
            norm_root("ln_in")
            round_x("blk2")
            rounded_take("qk2", 8, lambda b: qk2[:, b, :], ACT.Copy, "v2")
            round_blocks("v2", PAIR, 4)
            round_blocks("rw2", 0, PAIR)
            act.wait_ge(w_used, BASE["v2"] + 4)
            for x in range(NX):
                mv = act.activation(v2[:, x, :], acc[:, x, :], ACT.Copy)
            mv.then_inc(acc_out, 1)
            soft(4, sc2)
            rounded_take("rw2", RW_TILES, lambda b: cols[:, b, 1:T + 1], ACT.Copy)
            round_blocks("gate2", 0, PAIR)
            soft(8, sc2)
            act.wait_ge(shifted, 1)
            act.activation(low[0:64, 0, :], low[0:64, 0, :], ACT.Tanh).then_inc(low_act, 1)
            act.activation(low[:, 1:3, :], low[:, 1:3, :], ACT.Sigmoid).then_inc(low_act, 1)
            for n in range(6):
                act.wait_ge(lora_mm, n + 1)
                for j in range(2):
                    f = 2 * (n % 2) + j
                    src = prod[:, n % 2, j * T:(j + 1) * T]
                    if n < 4:
                        dst, base = ((e2, vcol("decay", f)), (aa_fm, vcol("aaa", f)))[n // 2]
                        mv = act.activation(dst[:, f, :], src, ACT.Sigmoid, bias=base)
                    else:
                        mv = act.activation(g_fm[:, f, :], src, ACT.Copy)
                mv.then_inc(lora_out, 1)
            root("kk", e1, e1)
            gate = lambda b: gates2[b // 2][:, b % 2, :]
            rounded_take("gate2", 16, gate, ACT.Sigmoid, last=6)
            act.wait_ge(logw_ready, 1)
            act.activation(a_til, a_til, ACT.Exp)
            act.activation(r_til, cum, ACT.Exp)
            act.activation(b_til, cum, ACT.Exp, scale=-1.0)
            act.activation(bh_fm, bh_fm, ACT.Exp).then_inc(exp_ready, 1)
            rounded_take("gate2", 16, gate, ACT.Sigmoid, first=6)
            root("gn", y_rs, y_rs)
            round_blocks("out2", 0, 8)
            round_blocks("moe", 0, PAIR)
            norm_root("ln0")
            round_x("ln0")

            def silu(b, e, i=0):
                act.wait_ge(w_used, BASE["moe"] + b + 2 + 12 * i)
                act.activation(h_sig[:, e % 2, :], prod[:, 0, :], ACT.Silu).then_inc(silu_ready, 1)

            round_blocks("moe", PAIR, 4)
            silu(0, 0)
            round_blocks("moe", 4, 4 + PAIR)
            act.wait_ge(max_ready, 1)
            for x in range(NX):
                act.activation(g8m[:, x, 0:4], logit[:, x, 0:4], ACT.Exp, bias=st[:, 104 + x:105 + x],
                               accum_out=st[:, 106 + x:107 + x])
            act.activation(st[:, 112:114], st[:, 110:112], ACT.Exp).then_inc(moe_exp, 1)
            round_blocks("moe", 4 + PAIR, 8)
            silu(4, 1)
            with act.Fori(0, (NEXP - 2) // 2) as i:
                for j in range(2):
                    for b in range(8 + 6 * j, 14 + 6 * j):
                        rounded("moe", b, i, 12)
                    silu(10 + 6 * j, j, i)
            round_blocks("moe", 6 * NEXP - 4, 6 * NEXP)
            act.wait_ge(w_used, BASE["ple_proj"] + 2)
            for n in range(4):
                mv = act.activation(ple[:, n // 2, (n % 2) * 512:(n % 2 + 1) * 512], acc[:, n, :], ACT.Copy)
            mv.then_inc(acc_out, 1)
            round_blocks("ple_gate", 0, PAIR)
            norm_root("ln1")
            round_x("ln1")
            for n in range(2):
                round_blocks("ple_gate", (PAIR, 6)[n], (6, 8)[n])
                act.wait_ge(w_used, BASE["ple_gate"] + 4 * (n + 1))
                for x in range(NX):
                    mv = act.activation(sig_ple[:, x, 512 * n:512 * (n + 1)], acc[:, 2 * x + n, :], ACT.Sigmoid)
                mv.then_inc(ple_sig, 1)
            norm_root("ln2")

        @block.vector
        def _(dve):
            chain = [0]
            taken = [0]

            def link(ins):
                chain[0] += 1
                ins.then_inc(v_chain, 1)
                dve.wait_ge(v_chain, chain[0])

            def group():
                dve.wait_ge(gen_mm, taken[0] + 1)
                taken[0] += 1
                return gen[:, (taken[0] - 1) % 2, :]

            def wide(ap, axis, n):
                shape = list(ap.shape)
                shape.insert(axis, n)
                return ap.unsqueeze(axis).broadcast_to(shape)

            def rstd(name):
                dve.wait_ge(root_ready, ROOT[name])
                link(dve.reciprocal(st[:, 6:8], st[:, 4:6]))

            def half_stats(n):
                for x in range(NX):
                    c = tile_stats(x, (n,))
                return c

            def tile_stats(x, halves):
                for n in halves:
                    o = 16 + 12 * x + 6 * n
                    c = dve.bn_stats(st[:, o:o + 6], resid[:, x, 512 * n:512 * (n + 1)])
                return c

            def moments(last):
                link(last)
                for x in range(NX):
                    c = dve.bn_aggr(st[:, 40 + 2 * x:42 + 2 * x], st[:, 16 + 12 * x:28 + 12 * x])
                link(c)

            def mean_square(last):
                moments(last)
                link(dve.tensor_tensor(st[:, 0:2], st[:, 40:44:2], st[:, 40:44:2], ALU.mult))
                dve.scalar_tensor_tensor(st[:, 2:4], st[:, 0:2], EPS, st[:, 41:45:2], ALU.add, ALU.add).then_inc(ms_ready, 1)

            def rms_norm(name, last):
                mean_square(last)
                rstd(name)
                row = ("mix0", "ffn0", "mix1", "ffn1").index(name)
                dve.wait_ge(gain_in[row % 2], 16 * (row // 2 + 1))
                for x in range(NX):
                    dve.scalar_tensor_tensor(xn[:, x, :], resid[:, x, :], st[:, 6 + x:7 + x], gains[:, row % 2, :],
                                             ALU.mult, ALU.mult).then_inc(normed, 1)

            def layer_norm(name, last):
                moments(last)
                dve.tensor_scalar(st[:, 2:4], st[:, 41:45:2], LN_EPS, None, ALU.add).then_inc(ms_ready, 1)
                n = ("ln_in", "ln0", "ln1", "ln2").index(name)
                for row in range(2):
                    dve.wait_ge(gain_in[row], 16 * (3 + n))
                for x in range(NX):
                    dve.scalar_tensor_tensor(resid[:, x, :], resid[:, x, :], st[:, 40 + 2 * x:41 + 2 * x], gains[:, 0, :],
                                             ALU.subtract, ALU.mult)
                rstd(name)
                for x in range(NX):
                    dve.scalar_tensor_tensor(resid[:, x, :], resid[:, x, :], st[:, 6 + x:7 + x], gains[:, 1, :],
                                             ALU.mult, ALU.add).then_inc(normed, 1)
                dve.wait_ge(normed, NORMED["blk2" if name == "ln_in" else name])

            def take_fm(dst, tiles):
                for x in range(NX):
                    for q in range(tiles // 4):
                        bank = group().rearrange("p (a b) -> p a b", b=P)
                        link2(dve.tensor_copy(dst[:, 4 * q:4 * q + 4, x * P:(x + 1) * P], bank))
                dve.sem_inc(fm_ready, 1)

            def take_split(whole=None):
                for x in range(NX):
                    for q in range(KD // 4):
                        bank = group().rearrange("p (a b) -> p a b", b=P)
                        hi, lo = (t[:, 4 * q:4 * q + 4, x * P:(x + 1) * P] for t in (xh, xl))
                        roundings[0] += 1
                        dve.wait_ge(x_rounded, roundings[0])
                        if whole is not None:
                            dve.tensor_copy(whole[:, 4 * q:4 * q + 4, x * P:(x + 1) * P], bank)
                        link2(dve.tensor_tensor(lo, bank, hi.bitcast(F32), ALU.subtract))
                dve.sem_inc(fm_ready, 1)

            def split_x(src, hi, lo):
                link(dve.tensor_copy(hi, src))
                link(dve.tensor_tensor(lo, src, hi.bitcast(F32), ALU.subtract))

            def link2(ins):
                ins.then_inc(gen_out, 1)
                dve.wait_ge(gen_out, taken[0])

            def add_acc(scale, ready):
                for n in range(2):
                    dve.wait_ge(w_used, ready[n])
                    for x in range(NX):
                        r = resid[:, x, 512 * n:512 * (n + 1)]
                        c = dve.scalar_tensor_tensor(r, r, scale, acc[:, 2 * x + n, :], ALU.mult, ALU.add)
                    if n == 0:
                        link(c)
                    else:
                        c.then_inc(acc_out, 1)
                        dve.wait_ge(acc_out, acc_uses[0])
                    last = half_stats(n)
                return last

            def square_halves(name):
                return BASE[name] + 4, BASE[name] + 8

            acc_uses = [0]
            roundings = [0]

            for x in range(NX):
                dve.wait_ge(x_in[x], 16)
                last = tile_stats(x, range(2))
            rms_norm("mix0", last)
            dve.wait_ge(small_in, 32)
            dve.tensor_copy(places, wide(iota, 2, GTOK))
            take_split()
            dve.wait_ge(table_b_in, 16)
            for n in range(8):
                dve.wait_ge(fm_out, 2 * n + 2)
                pair = qk1[:, 2 * n:2 * n + 2, :]
                bank = group().rearrange("p (a b) -> p a b", b=T)
                dve.tensor_tensor(rope_tmp, bank, wide(cb("sin"), 1, 2), ALU.mult).then_inc(gen_out, 1)
                link(dve.tensor_tensor(pair, pair, wide(cb("cos"), 1, 2), ALU.mult))
                dve.tensor_tensor(pair, pair, rope_tmp, ALU.add).then_inc(roped, 1)
                dve.wait_ge(roped, n + 1)

            def soft(scores, s, scale, bias_of, mask_band):
                for h in range(4):
                    dve.wait_ge(att_s, scores + h + 1)
                    link(dve.scalar_tensor_tensor(s[:, h, :], acc[:, h, 0:ATT_COLS], scale, bias_of(h), ALU.mult, ALU.add))
                    if h == 3:
                        dve.sem_inc(acc_out, 1)
                    if mask_band:
                        dve.memset(s[0:64, h, 64:P], NEG)
                        link(dve.memset(s[0:64, h, 2 * P + 64:3 * P], NEG))
                    dve.tensor_reduce(st[:, 32 + h:33 + h], s[:, h, 0:P], AX, ALU.max)
                    link(dve.tensor_reduce(st[:, 36 + h:37 + h], s[:, h, P:ATT_COLS], AX, ALU.max))
                    dve.tensor_scalar(st[:, 16 + h:24:4], st[:, 32 + h:40:4], -1.0, None, ALU.mult).then_inc(att_m, 1)

            def probs_T(pT):
                for h in range(4):
                    bank = group()
                    link2(dve.tensor_copy(pT[:, h, :], bank[:, 0:ATT_COLS]))
                    dve.sem_inc(att_pt, 1)

            def take_heads(n, soft_count, dst, width):
                dve.wait_ge(att_p, soft_count)
                link(dve.reciprocal(st[:, 32:40], st[:, 24:32]))
                dve.wait_ge(att_o, n)
                for x in range(NX):
                    c = dve.tensor_tensor(dst(x).rearrange("p (a b) -> p a b", b=width),
                                          prod[:, x, 0:4 * width].rearrange("p (a b) -> p a b", b=width),
                                          wide(st[:, 32 + 4 * x:36 + 4 * x], 2, width), ALU.mult)
                c.then_inc(att_done, 1)

            soft(0, sc1, HD1 ** -0.5, lambda h: cb("causal"), False)
            probs_T(pT1)
            take_heads(1, 4, lambda x: cat1[:, x, 0:512], HD1)
            for h in range(4):
                dve.wait_ge(att_s, 5 + h)
                c = dve.tensor_tensor(rT1[:, h, :], acc[:, h, 0:ATT_COLS],
                                      cb("decay")[:, h * ATT_COLS:(h + 1) * ATT_COLS], ALU.mult)
                c.then_inc(att_pt, 1)
            dve.wait_ge(att_pt, 8)
            dve.sem_inc(acc_out, 1)
            dve.wait_ge(att_o, 2)
            for x in range(NX):
                c = dve.tensor_copy(cat1[:, x, 512:D], prod[:, x, :])
            c.then_inc(att_done, 1)
            dve.wait_ge(att_done, 2)
            ret = cat1[:, :, 512:D]
            link(dve.tensor_tensor(ret_sq, ret, ret, ALU.mult))
            for x in range(NX):
                c = dve.tensor_reduce(st[:, 40 + 4 * x:44 + 4 * x], ret_sq[:, x, :].rearrange("p (a b) -> p a b", b=HD1),
                                      AX, ALU.add)
            link(c)
            dve.tensor_scalar(st[:, 48:56], st[:, 40:48], 1.0 / HD1, EPS, ALU.mult, ALU.add).then_inc(ms_ready, 1)
            dve.wait_ge(root_ready, ROOT["ret"])
            link(dve.reciprocal(st[:, 64:72], st[:, 56:64]))
            for x in range(NX):
                v = cat1[:, x, 512:D].rearrange("p (a b) -> p a b", b=HD1)
                c = dve.tensor_tensor(v, v, wide(st[:, 64 + 4 * x:68 + 4 * x], 2, HD1), ALU.mult)
            link(c)
            dve.wait_ge(acc_out, 2)
            dve.tensor_tensor(ret, ret, g_ret, ALU.mult).then_inc(normed, NX)
            take_split()
            acc_uses[0] = 5
            last = add_acc(1.0, square_halves("even_out"))

            def top16(vals, idx, src, n):
                for r in range(2):
                    lo = slice(8 * r, 8 * r + 8)
                    for m in range(n):
                        c = dve.max(vals(m)[:, lo], src(m))
                    link(c)
                    for m in range(n):
                        c = dve.max_index(idx(m)[:, lo], vals(m)[:, lo], src(m))
                    if r == 0:
                        for m in range(n):
                            c = dve.match_replace(src(m), vals(m)[:, lo], src(m), -3.0e38)
                    link(c)

            def route(x):
                top16(lambda m: top_s[:, m, :], lambda m: top_u[:, m, :].bitcast(U32), lambda m: score[:, x, m, :], 16)
                dve.tensor_copy(top_f, top_u.bitcast(U32))
                c4 = cand.rearrange("p h (a b) -> p h a b", b=TOPK)
                link(dve.tensor_tensor(c4, wide(top_s[:, 0::2, :], 3, TOPK), wide(top_s[:, 1::2, :], 2, TOPK), ALU.add))
                top16(lambda m: sel_s[:, x, m, :], lambda m: pos_u[:, m, :].bitcast(U32), lambda m: cand[:, m, :], PEER_H)
                for n, (op, by) in enumerate(((ALU.logical_shift_right, 4), (ALU.bitwise_and, TOPK - 1))):
                    link(dve.tensor_scalar(pos_a.bitcast(U32), pos_u.bitcast(U32), by, None, op))
                    link(dve.tensor_copy(pos_f, pos_a.bitcast(U32)))
                    flat = pos_f.rearrange("p h k -> p (h k)")
                    link(dve.tensor_tensor(pick, wide(iota[:, 0:TOPK], 1, P), wide(flat, 2, TOPK), ALU.is_equal))
                    p4 = pick.rearrange("p (h k) a -> p h k a", k=TOPK)
                    link(dve.tensor_tensor(p4, p4, wide(top_f[:, n::2, :], 2, TOPK), ALU.mult))
                    link(dve.tensor_reduce(sel_i[:, n, x, :], pick, AX, ALU.add))
                g = sel_i[:, 2, x, :].rearrange("p (h k) -> p h k", k=TOPK)
                return dve.tensor_tensor(g, sel_s[:, x, :, :], wide(sel_s[:, x, :, 0], 2, TOPK), ALU.subtract)

            def peer(layer, last):
                rms_norm(f"ffn{layer}", last)
                take_split()
                for b in range(2):
                    for x in range(NX):
                        for q in range(2):
                            bank = group().rearrange("p (a b) -> p a b", b=NK)
                            link2(dve.tensor_copy(score[:, x, 8 * b + 4 * q:8 * b + 4 * q + 4, :], bank))
                for x in range(NX):
                    last = route(x)
                last.then_inc(topk_ready, 1)
                dve.wait_ge(gate_exp, layer + 1)
                gate = sel_i[:, 2, :, :].rearrange("p x (h k) -> p (x h) k", k=TOPK)
                link(dve.tensor_reduce(st[:, 16:32], gate, AX, ALU.add))
                link(dve.reciprocal(st[:, 32:48], st[:, 16:32]))
                dve.tensor_tensor(gate, gate, wide(st[:, 32:48], 2, TOPK), ALU.mult).then_inc(normed, NX)
                for x in range(NX):
                    bank = group()
                    tok = slice(x * P, (x + 1) * P)
                    dve.tensor_copy(hk[:, 0:2, tok], bank[:, 0:2 * P].rearrange("p (a b) -> p a b", b=P))
                    link2(dve.tensor_copy(gate_f[:, tok], bank[:, 2 * P:3 * P]))
                for g in range(PARTS):
                    link(dve.tensor_copy(hk[:, 2 + g, :], gate_f))
                    if g < PARTS - 1:
                        link(dve.tensor_tensor(gate_f, gate_f, hk[:, 2 + g, :], ALU.subtract))

                def chunk_rest(n, i):
                    dve.wait_ge(hh_ready, layer * NK + n + 1 + RING * i)
                    dve.tensor_tensor(hid_lo[:, n % RING, :], hid[:, n + RING * i, :], hid_hi[:, n % RING, :].bitcast(F32),
                                      ALU.subtract).then_inc(hl_ready, 1)

                for half in range(2):
                    before, chained = (2 * layer + half) * HALF, chain[0]

                    def one_hots(n, i=0):
                        tok = bass.ds(GTOK * n + GTOK * RING * i, GTOK)
                        if before + n:
                            dve.wait_ge(hot_ready, before + n + RING * i)
                        dve.tensor_tensor(hot, places[:, half * HALF:(half + 1) * HALF, :], wide(hk[:, 1, tok], 1, HALF),
                                          ALU.is_equal).then_inc(v_chain, 1)
                        dve.tensor_tensor(hot1[:, n % 2, :, :], places, wide(hk[:, 0, tok], 1, NK), ALU.is_equal)
                        dve.wait_ge(v_chain, chained + n + 1 + RING * i)
                        dve.tensor_tensor(hot2[:, n % 2, :, :, :], wide(hot, 1, PARTS), wide(hk[:, 2:2 + PARTS, tok], 2, HALF),
                                          ALU.mult).then_inc(hot_ready, 1)

                    def gate_group(n, i=0):
                        dve.wait_ge(tok_mm, before + n + 1 + RING * i)
                        h = hid[:, half * HALF:(half + 1) * HALF, bass.ds(GTOK * n + GTOK * RING * i, GTOK)]
                        dve.tensor_tensor(h, h, gen[:, n % 2, 0:GTOK * HALF].rearrange("p (t c) -> p c t", c=HALF), ALU.mult)\
                            .then_inc(gated, 1)

                    one_hots(0)
                    dve.wait_ge(fm_out, FMBASE[f"peer_u{layer}"] + (half + 1) * HALF)
                    with dve.Fori(0, HALF // RING - 1) as i:
                        for j in range(RING):
                            one_hots(j + 1, i)
                            if half == 1:
                                chunk_rest(j, i)
                            gate_group(j, i)
                    for j in range(HALF - RING, HALF):
                        if j + 1 < HALF:
                            one_hots(j + 1)
                        if half == 1:
                            chunk_rest(j, 0)
                        gate_group(j)
                    chain[0] += HALF
                with dve.Fori(HALF // RING, NK // RING) as i:
                    for j in range(RING):
                        chunk_rest(j, i)
                acc_uses[0] = 6 + 2 * layer
                return add_acc(1.0, 2 * [BASE[f"peer_v{layer}"] + NK])

            last = peer(0, last)
            rms_norm("mix1", last)
            take_split()
            dve.memset(cv_u[:, :, 0:2], 0.0)
            for k in range(KD):
                dve.wait_ge(fm_out, FMBASE["odd_in"] + 3 * k + 3)
                link(dve.tensor_tensor(cv_u[:, k, 2:T + 2], cv_c[:, k, :], cv_h[:, k, :], ALU.mult))
                link(dve.tensor_scalar(cv_y[:, k, :], cv_u[:, k, 0:T], vcol("conv", k), None, ALU.mult))
                for w in (1, 2):
                    link(dve.scalar_tensor_tensor(cv_y[:, k, :], cv_u[:, k, w:w + T], vcol("conv", 8 * w + k),
                                                  cv_y[:, k, :], ALU.mult, ALU.add))
                link(dve.tensor_tensor(cv_z[:, k, :], cv_b[:, k, :], cv_y[:, k, :], ALU.mult))
            dve.wait_ge(w_used, BASE["odd_out"])
            for k in range(0, KD, 2):
                split_x(cv_z[:, k:k + 2, :], xh[:, k:k + 2, :], xl[:, k:k + 2, :])
                dve.sem_inc(conv_out, 1)
            acc_uses[0] = 7
            last = peer(1, add_acc(1.0, square_halves("odd_out")))
            dve.sem_inc(arena_free, 1)
            mean_square(last)
            rstd("final")
            dve.wait_ge(final_in, 16)
            for x in range(NX):
                c = dve.scalar_tensor_tensor(resid[:, x, :], resid[:, x, :], st[:, 6 + x:7 + x], final_gain,
                                             ALU.mult, ALU.mult)
            link(c)
            half_stats(0)
            layer_norm("ln_in", half_stats(1))
            take_split()
            dve.wait_ge(block2_in, 80)
            soft(8, sc2, HD2 ** -0.5, lambda h: band_bias[:, h, :], True)
            link(dve.memset(cols[:, :, 0:1], 0.0))
            for n in range(0, RW_TILES, 3):
                dve.wait_ge(fm_out, FMBASE["rw2"] + n + 3)
                v = rkv[:, n:n + 3, :] if n < 12 else low
                link(dve.tensor_tensor(v, cols[:, n:n + 3, 0:T], cols[:, n:n + 3, 1:T + 1], ALU.subtract))
                for j in range(3):
                    c = dve.scalar_tensor_tensor(v[:, j, :], v[:, j, :], vcol("mu", n + j), cols[:, n + j, 1:T + 1],
                                                 ALU.mult, ALU.add)
            link(c)
            dve.sem_inc(shifted, 1)
            probs_T(pT2)
            take_heads(3, 8, lambda x: ob2[:, x, 0:256], HD2)
            soft(12, sc2, HD2 ** -0.5, lambda h: band_bias[:, 4 + h, :], True)
            probs_T(pT2)
            take_heads(4, 12, lambda x: ob2[:, x, 256:512], HD2)
            dve.wait_ge(att_done, 4)
            dve.sem_inc(normed, NX)
            take_fm(ya_fm, 4)
            for pr in range(4):
                c = dve.tensor_scalar(kk_fm[:, pr, :], k_fm[:, pr, :], vcol("k_k", pr), None, ALU.mult)
            link(c)
            dve.tensor_tensor(e1, kk_fm, kk_fm, ALU.mult).then_inc(sq_ready, 1)
            for q in range(2):
                bank = group().rearrange("p (a b) -> p a b", b=T)
                link2(dve.tensor_scalar(e1[:, 2 * q:2 * q + 2, :], bank, 1e-24, None, ALU.max))
            dve.sem_inc(ms_ready, 1)
            dve.wait_ge(root_ready, ROOT["kk"])
            link(dve.reciprocal(e1, e1))
            link(dve.tensor_tensor(kk_fm, kk_fm, e1, ALU.mult))
            dve.wait_ge(lora_out, 6)
            for pr in range(4):
                c = dve.tensor_scalar(e1[:, pr, :], aa_fm[:, pr, :], -1.0, vcol("k_a", pr), ALU.add, ALU.mult)
            link(c)
            link(dve.scalar_tensor_tensor(k_fm, e1, 1.0, k_fm, ALU.add, ALU.mult))
            link(dve.memset(start, 1.0))
            link(dve.memset(start[:, ::CH], 0.0))
            link(dve.tensor_scalar(e1, e2, -float(np.exp(-0.5)), None, ALU.mult))
            for pr in range(4):
                c = dve.tensor_tensor_scan(cum[:, pr, :], start, e1[:, pr, :], 0.0, ALU.mult, ALU.add)
            link(c)
            dve.tensor_tensor(a_til, cum, e1, ALU.subtract)
            for pr in range(4):
                cpr = cum[:, pr, :].rearrange("p (c t) -> p c t", t=CH)
                c = dve.tensor_tensor(bh_fm[:, pr, :].rearrange("p (c t) -> p c t", t=CH),
                                      wide(cpr[:, :, CH - 1], 2, CH), cpr, ALU.subtract)
            c.then_inc(logw_ready, 1)
            dve.wait_ge(exp_ready, 1)
            for pr in range(4):
                c = dve.tensor_copy(st[:, 72 + NCH * pr:72 + NCH * (pr + 1)], r_til[:, pr, CH - 1::CH])
            link(c)
            dve.scalar_tensor_tensor(a_til, a_til, -1.0, kk_fm, ALU.mult, ALU.mult)
            link(dve.tensor_tensor(kk_fm, kk_fm, aa_fm, ALU.mult))
            dve.tensor_tensor(k_til, b_til, k_fm, ALU.mult)
            dve.tensor_tensor(kh_fm, bh_fm, k_fm, ALU.mult)
            dve.tensor_tensor(b_til, b_til, kk_fm, ALU.mult)
            dve.tensor_tensor(bh_fm, bh_fm, kk_fm, ALU.mult)
            link(dve.tensor_tensor(r_til, r_til, r_fm, ALU.mult))
            dve.sem_inc(fm_ready, 1)
            for x in range(NX):
                for dst in (a_tm, bh_tm, kh_tm, v_tm):
                    bank = group()
                    link2(dve.tensor_copy(dst[:, x, :], bank))
            m_lT, m_l, m_ak, m_rb, m_rk, m_off, m_a, m_b = mats

            def masked(dst, mask, also=None):
                for q in range(2):
                    bank = group().rearrange("p (a b) -> p a b", b=P)
                    if also is not None:
                        dve.tensor_tensor(also[0][:, q::2, :], bank, wide(cc(also[1]), 1, 4), ALU.mult)
                    link2(dve.tensor_tensor(dst[:, q::2, :], bank, wide(cc(mask), 1, 4), ALU.mult))

            def stored(dst, plus=None):
                for q in range(2):
                    bank = group().rearrange("p (a b) -> p a b", b=P)
                    d = dst[:, 4 * q:4 * q + 4, :]
                    if plus is None:
                        link2(dve.tensor_copy(d, bank))
                    else:
                        link2(dve.tensor_tensor(d, plus[:, 4 * q:4 * q + 4, :], bank, ALU.add))

            for x in range(NX):
                masked(m_lT, "up16", (m_off, "off32"))
                masked(m_l, "low16")
                masked(m_ak, "up32")
                masked(m_rb, "upi32")
                masked(m_rk, "upi32")
                bank = group()
                dve.tensor_copy(sol[:, :, 0:HD2], a_tm[:, x, :].rearrange("p (a b) -> p a b", b=HD2))
                dve.tensor_tensor(m_ak, m_lT, wide(ident, 1, 8), ALU.add)
                link2(dve.tensor_copy(sol[:, :, HD2:P], bank.rearrange("p (a b) -> p a b", b=HD2)))
                stored(m_a)
                stored(m_b)
                stored(m_ak, m_ak)
                stored(m_l)
                stored(m_lT)
                stored(m_ak, m_ak)
                stored(m_a)
                stored(m_ak, m_ak)
                stored(m_b)
                stored(m_lT)
                stored(sol, m_b)
                tx = slice(x * P, (x + 1) * P)
                bank = group().rearrange("p (a b) -> p a b", b=P)
                link2(dve.tensor_tensor(q_eff[:, :, tx], bank, r_til[:, :, tx], ALU.add))
                bank = group().rearrange("p (a b) -> p a b", b=P)
                link2(dve.tensor_copy(y_fm[:, :, tx], bank))
                cs = slice(4 * x, 4 * x + 4)
                for pr in range(4):
                    c = dve.tensor_tensor(step_m[:, pr, cs, :], wide(cc("eye64"), 1, 4),
                                          wide(st[:, 72 + NCH * pr + 4 * x:76 + NCH * pr + 4 * x], 2, HD2), ALU.mult)
                link(c)
                for c in range(4 * x, 4 * x + 4):
                    bank = group().rearrange("p (n a b) -> p n a b", n=2, b=HD2)
                    dve.tensor_tensor(step_m[:, :, c, :], step_m[:, :, c, :], bank[:, 0], ALU.add)
                    link2(dve.tensor_copy(step_n[:, :, c, :], bank[:, 1]))
            dve.tensor_copy(state[:, 1, :, :], step_n[:, :, 0, :]).then_inc(state_ready, 1)
            for c in range(1, NCH - 1):
                bank = group()[:, 0:4 * HD2].rearrange("p (a b) -> p a b", b=HD2)
                link2(dve.tensor_tensor(state[:, c + 1, :, :], step_n[:, :, c, :], bank, ALU.add))
                dve.sem_inc(state_ready, 1)
            for q in range(2):
                bank = group().rearrange("p (a b) -> p a b", b=T)
                d = y_fm[:, 2 * q:2 * q + 2, CH:T]
                link2(dve.tensor_tensor(d, d, bank[:, :, CH:T], ALU.add))
            dve.sem_inc(sq_ready, 1)
            for q in range(2):
                bank = group().rearrange("p (a b) -> p a b", b=T)
                link2(dve.scalar_tensor_tensor(y_tmp[:, 2 * q:2 * q + 2, :], bank, -1.0 / HD2, y_fm[:, 2 * q:2 * q + 2, :],
                                               ALU.mult, ALU.add))
            dve.tensor_tensor(y_sq, y_tmp, y_tmp, ALU.mult).then_inc(sq_ready, 1)
            for pr in range(4):
                c = dve.scalar_tensor_tensor(bonus[:, pr, :], r_fm[:, pr, :], vcol("r_k", pr), k_fm[:, pr, :],
                                             ALU.mult, ALU.mult)
            for q in range(2):
                bank = group().rearrange("p (a b) -> p a b", b=T)
                link2(dve.tensor_scalar(y_rs[:, 2 * q:2 * q + 2, :], bank, 1.0 / HD2, GN_EPS, ALU.mult, ALU.add))
            dve.sem_inc(sq_ready, 1)
            dve.sem_inc(ms_ready, 1)
            for q in range(2):
                bank = group().rearrange("p (a b) -> p a b", b=T)
                h = slice(2 * q, 2 * q + 2)
                link2(dve.tensor_tensor(y_mu[:, h, :], bank, v_fm[:, h, :], ALU.mult))
            dve.wait_ge(root_ready, ROOT["gn"])
            link(dve.reciprocal(y_rs, y_rs))
            link(dve.tensor_tensor(y_tmp, y_tmp, y_rs, ALU.mult))
            for pr in range(4):
                c = dve.tensor_scalar(y_tmp[:, pr, :], y_tmp[:, pr, :], vcol("gn_g", pr), vcol("gn_b", pr), ALU.mult, ALU.add)
            link(c)
            link(dve.tensor_tensor(y_tmp, y_tmp, y_mu, ALU.add))
            dve.tensor_tensor(y_out, y_tmp, g_fm, ALU.mult).then_inc(fm_ready, 1)
            for j in range(4):
                dve.wait_ge(w_used, BASE["branch"] + j + 1)
                c = dve.tensor_tensor(mixT[:, 2 * j:2 * j + 2, :], gates2[j],
                                      acc[:, j, :].rearrange("p (a b) -> p a b", b=T), ALU.mult)
            c.then_inc(acc_out, 1)
            dve.wait_ge(acc_out, 12)
            for j in range(4):
                h = slice(2 * j, 2 * j + 2)
                dve.wait_ge(w_used, BASE["branch"] + 4 + j + 1)
                dve.tensor_tensor(mix_tmp, gates2[4 + j], prod[:, j % 2, :].rearrange("p (a b) -> p a b", b=T), ALU.mult)\
                    .then_inc(branch_out, 1)
                dve.wait_ge(branch_out, j + 1)
                link(dve.tensor_tensor(mixT[:, h, :], mixT[:, h, :], mix_tmp, ALU.add))
                split_x(mixT[:, h, :], xh[:, h, :], xl[:, h, :])
                dve.sem_inc(mix_out, 1)
            acc_uses[0] = 13
            layer_norm("ln0", add_acc(ALPHA, square_halves("out2")))
            take_split(xT2)
            bank = group()[:, 0:NX * 36].rearrange("p (a b) -> p a b", b=36)
            link2(dve.tensor_tensor(logit, bank, wide(router_b, 1, NX), ALU.add))
            link(dve.memset(g8, -3.0e38))
            link(dve.tensor_copy(g8[:, :, 0:4], logit[:, :, 0:4]))
            for x in range(NX):
                c = dve.max(sel8m[:, x, :], g8[:, x, :])
            link(c)
            for x in range(NX):
                c = dve.max_index(g8i[:, x, :].bitcast(U32), sel8m[:, x, :], g8[:, x, :])
            link(c)
            dve.tensor_scalar(st[:, 104:106], sel8m[:, :, 0], -1.0, None, ALU.mult)
            link(dve.tensor_copy(sel8f, g8i.bitcast(U32)))
            for x in range(NX):
                c = dve.tensor_scalar(hot_g[:, x, :], cc("iota8"), sel8f[:, x, 0:1], None, ALU.is_equal)
            link(c)
            elog = logit[:, :, 4:36].rearrange("p x (g e) -> p x e g", e=8)
            for x in range(NX):
                c = dve.tensor_tensor(sel_t[:, x, :, :], elog[:, x, :, :], wide(hot_g[:, x, 0:4], 1, 8), ALU.mult)
            link(c)
            link(dve.tensor_reduce(sel8, sel_t, AX, ALU.add))
            for x in range(NX):
                c = dve.max(sel8m[:, x, :], sel8[:, x, :])
            link(c)
            for x in range(NX):
                c = dve.max_index(sel8i[:, x, :].bitcast(U32), sel8m[:, x, :], sel8[:, x, :])
            link(c)
            dve.tensor_copy(sel8f, sel8i.bitcast(U32))
            link(dve.tensor_tensor(st[:, 110:112], sel8m[:, :, 1], sel8m[:, :, 0], ALU.subtract))
            dve.sem_inc(max_ready, 1)
            dve.wait_ge(moe_exp, 1)
            link(dve.tensor_scalar(st[:, 118:120], st[:, 112:114], 1.0, None, ALU.add))
            link(dve.tensor_tensor(st[:, 118:120], st[:, 118:120], st[:, 106:108], ALU.mult))
            link(dve.reciprocal(st[:, 114:116], st[:, 118:120]))
            link(dve.tensor_tensor(st[:, 116:118], st[:, 114:116], st[:, 112:114], ALU.mult))
            for x in range(NX):
                dve.tensor_scalar(comb8[:, x, :], cc("iota8"), sel8f[:, x, 0:1], st[:, 114 + x:115 + x],
                                  ALU.is_equal, ALU.mult)
                c = dve.tensor_scalar(comb8b[:, x, :], cc("iota8"), sel8f[:, x, 1:2], st[:, 116 + x:117 + x],
                                      ALU.is_equal, ALU.mult)
            link(c)
            link(dve.tensor_tensor(comb8, comb8, comb8b, ALU.add))
            for x in range(NX):
                c = dve.tensor_tensor(comb[:, x, :].rearrange("p (g e) -> p g e", e=8), wide(comb8[:, x, :], 1, 4),
                                      wide(hot_g[:, x, 0:4], 2, 8), ALU.mult)
            c.then_inc(normed, NX)
            bank = group()
            link2(dve.tensor_copy(combT[0:NEXP, :], bank[0:NEXP, 0:T]))

            def own_rows(first, last):
                dve.tensor_tensor(comb_d[0:NEXP, first:last, :], wide(combT[0:NEXP, :], 1, last - first),
                                  wide(ident[0:NEXP, first:last], 2, T), ALU.mult).then_inc(fm_ready, 1)

            own_rows(0, 2)
            eb = BASE["moe"]

            def weigh(e, i, chained):
                first = eb if e == 0 else eb + 4 + 6 * (e - 1)
                mid = h_mid[:, e % 2, :]
                c = chained + 3 * e + 6 * i
                dve.wait_ge(silu_ready, e + 1 + 2 * i)
                dve.wait_ge(w_used, first + 4 + 12 * i)
                dve.tensor_tensor(mid, h_sig[:, e % 2, :], prod[:, 1, :], ALU.mult).then_inc(v_chain, 1)
                dve.wait_ge(v_chain, c + 1)
                dve.wait_ge(comb_mm, e + 1 + 2 * i)
                m2 = mid.rearrange("p (a b) -> p a b", b=T)
                dve.tensor_tensor(m2, m2, wide(gen[:, 0, 0:T], 1, 2), ALU.mult).then_inc(v_chain, 1)
                if e:
                    dve.wait_ge(w_used, first + 6 + 12 * i)
                dve.wait_ge(v_chain, c + 2)
                dve.tensor_copy(mid_hi, mid).then_inc(v_chain, 1)
                dve.wait_ge(v_chain, c + 3)
                dve.tensor_tensor(mid_lo, mid, mid_hi.bitcast(F32), ALU.subtract).then_inc(mid_ready, 1)

            chained = chain[0]
            weigh(0, 0, chained)
            own_rows(2, NEXP)
            weigh(1, 0, chained)
            with dve.Fori(0, (NEXP - 2) // 2) as i:
                for j in range(2):
                    weigh(2 + j, i, chained)
            chain[0] += 3 * NEXP
            acc_uses[0] = 14
            layer_norm("ln1", add_acc(ALPHA, 2 * [eb + 6 * NEXP]))
            take_split()
            dve.wait_ge(acc_out, 15)
            for n in range(2):
                dve.wait_ge(ple_sig, n + 1)
                r, p, g = (t[:, :, 512 * n:512 * (n + 1)] for t in (resid, ple, sig_ple))
                link(dve.tensor_tensor(p, p, g, ALU.mult))
                link(dve.scalar_tensor_tensor(r, r, ALPHA, p, ALU.mult, ALU.add))
                last = half_stats(n)
            layer_norm("ln2", last)


def _fm(w):
    n = w.shape[1] // P
    return w.reshape(KD, P, n, P).transpose(2, 1, 0, 3).reshape(n, P, BLK)


def _tm(w):
    k, n = w.shape[0] // (2 * P), w.shape[1] // 512
    return w.reshape(k, 2, P, n, 512).transpose(3, 0, 2, 1, 4).reshape(n * k, P, BLK)


def _col(v, tiles):
    return v.reshape(tiles, P).T


def _layout(i):
    a = {}
    w = i["even_w_in"][0]
    a["even_qk"] = _fm(np.concatenate([w[:, 0:1024], w[:, 1536:2560]], axis=1))
    a["even_vg"] = _tm(np.concatenate([w[:, 1024:1536], w[:, 2560:3584]], axis=1))
    a["even_out"] = _tm(i["even_w_out"][0])
    a["odd_in"] = _fm(i["odd_w_in"][0].reshape(D, 3, KD, P).transpose(0, 2, 1, 3).reshape(D, 3 * D))
    a["odd_out"] = _tm(i["odd_w_out"][0])
    for n in range(LAYERS):
        a[f"peer_q{n}"] = _fm(i["peer_w_q"][n])
        a[f"peer_keys{n}"] = i["peer_sub_keys"][n].reshape(2, 8, NK, P).transpose(0, 3, 1, 2).reshape(2, P, BLK)
        a[f"peer_u{n}"] = i["peer_u"][n].reshape(NK, NK, KD, P).transpose(1, 3, 2, 0).reshape(NK, P, BLK)
    a["peer_v"] = i["peer_v"]
    w = i["w_in_2"][0]
    a["qk2"] = _fm(w[:, 0:1024])
    a["v2"] = _tm(w[:, 1024:1536])
    a["rw2"] = _fm(np.pad(w[:, 1536:3360], ((0, 0), (0, RW_TILES * P - 1824))))
    a["gate2"] = _fm(w[:, 3360:])
    for name, key in (("branch_a", "w_branch_attn_2"), ("branch_r", "w_branch_rwkv_2")):
        a[name] = i[key][0].reshape(4, P, 4, 2, P).transpose(2, 1, 0, 3, 4).reshape(4, P, BLK)
    a["out2"] = _tm(i["w_out_2"][0])
    for name, key in (("exp_gate", "exp_gate_2"), ("exp_up", "exp_up_2")):
        a[name] = i[key][0].reshape(NEXP, KD, P, 2, P).transpose(0, 3, 2, 1, 4).reshape(2 * NEXP, P, BLK)
    a["exp_down"] = i["exp_down_2"][0].reshape(2 * NEXP, P, BLK)
    a["ple_proj"] = _tm(i["ple_proj_2"][0])
    a["ple_gate"] = _tm(i["ple_gate_2"][0])
    a["x"] = i["x"]
    a["const_a"], a["const_b"], a["const_c"] = constant_tables()
    vec = [_col(i["odd_conv"][0][w], 8) for w in range(3)]
    vec += [_col(np.pad(i["tok_mix_2"][0], (0, RW_TILES * P - 1824)), RW_TILES)]
    vec += [_col(i[k][0].reshape(-1), 4) for k in ("decay_base_2", "aaa_base_2", "k_k_2", "k_a_2", "r_k_2", "gn_g_2", "gn_b_2")]
    a["vec"] = np.concatenate(vec, axis=1)
    a["norm_mix"], a["norm_ffn"], a["final_norm"] = i["norm_mix"], i["norm_ffn"], i["final_norm"]
    a["ln_in_g"], a["ln_in_b"] = i["ln_in_g_2"], i["ln_in_b_2"]
    a["ln_g"], a["ln_b"] = i["ln_g_2"][0], i["ln_b_2"][0]
    both = np.concatenate([i["router_grp_2"][0], i["router_exp_2"][0]], axis=1)
    a["router"] = both.reshape(KD, P, 36).transpose(1, 0, 2)
    a["router_b"] = np.concatenate([i["router_grp_bias_2"][0], i["router_exp_bias_2"][0]])
    lora = np.zeros((P, 3, 512), np.float32)
    lora[0:64, 0], lora[64:128, 0] = i["decay_up_2"][0], i["aaa_up_2"][0]
    lora[:, 1], lora[0:32, 2] = i["gate_up_2"][0][0:128], i["gate_up_2"][0][128:160]
    a["lora"] = lora
    pos = np.arange(T)
    place = np.clip(pos[:, None] - pos[None, :], -128, 128) + 128
    place = np.concatenate([place[0:P, 0:P], place[P:T, :]], axis=1)
    a["band_bias"] = i["rel_bias_2"][:, place].transpose(1, 0, 2)
    a["p"] = i["p_2"][0, 0].reshape(T, 2, P).transpose(2, 1, 0)
    return {k: np.ascontiguousarray(v) for k, v in a.items()}


def kernel(**inputs):
    from concourse.bacc import Bacc
    from concourse.bass_utils import run_bass_kernel_spmd

    arrays = _layout({k: np.asarray(v) for k, v in inputs.items()})
    nc = Bacc("TRN2", target_bir_lowering=False, num_devices=1)
    dram = {k: nc.dram_tensor(f"in_{k}", v.shape, mybir.dt.from_np(v.dtype), kind="ExternalInput").ap()
            for k, v in arrays.items()}
    out = nc.dram_tensor("out_x", (1, T, D), F32, kind="ExternalOutput").ap()
    build(nc, dram, out)
    r = run_bass_kernel_spmd(nc, [{f"in_{k}": v for k, v in arrays.items()}], core_ids=[0])
    return r.results[0]["out_x"]
```
